# Optimizing a Trainium2 kernel written in Bass

```python
import math, functools
import jax, jax.numpy as jnp
from jax import lax
import numpy as np
import math

D_MODEL = 2048
BATCH = 1
SEQ = 256
DEPTH = 2

HEAD_DIM = 128
N_MIX_HEADS = D_MODEL // HEAD_DIM
SB_HEADS = N_MIX_HEADS // 2
GDN_HEADS = N_MIX_HEADS - SB_HEADS
MOBA_HEADS = N_MIX_HEADS // 2
DIL_HEADS = N_MIX_HEADS - MOBA_HEADS
SB_W = SB_HEADS * HEAD_DIM
GDN_W = GDN_HEADS * HEAD_DIM
MOBA_W = MOBA_HEADS * HEAD_DIM
DIL_W = DIL_HEADS * HEAD_DIM
MIX_W_EVEN = SB_W + GDN_W
MIX_W_ODD = MOBA_W + DIL_W
SB_BLOCK = 128
GDN_CHUNK = 64
GDN_CONV = 4
MOBA_BLOCK = 256
MOBA_TOPK = 3
MOBA_QCHUNK = 32
DIL_WINDOWS = (128, 512, 2048)
DIL_RATES = (1, 4, 16)
D_FF = ((8 * D_MODEL + 3 * 256 - 1) // (3 * 256)) * 256
NORM_EPS = 1e-6
N_EVEN = (DEPTH + 1) // 2
N_ODD = DEPTH // 2
EVEN_SIZES = (SB_W, SB_W, SB_W, 3 * GDN_W, GDN_W, GDN_HEADS, GDN_HEADS)
EVEN_IN = sum(EVEN_SIZES)
ODD_SIZES = (MOBA_W, MOBA_W, MOBA_W, DIL_W, DIL_W, DIL_W)
ODD_IN = sum(ODD_SIZES)


def _split_points(sizes):
    return list(np.cumsum(sizes)[:-1])

def rms_norm(x, w):
    xf = x.astype(jnp.float32)
    y = xf * lax.rsqrt(jnp.mean(xf * xf, axis=-1, keepdims=True) + NORM_EPS)
    return (y * w.astype(jnp.float32)).astype(x.dtype)

def l2norm(t):
    return t * lax.rsqrt(jnp.sum(t * t, axis=-1, keepdims=True) + NORM_EPS)

def to_heads(t, n):
    b, s, _ = t.shape
    return t.reshape(b, s, n, -1).transpose(0, 2, 1, 3)

def from_heads(t):
    b, h, s, d = t.shape
    return t.transpose(0, 2, 1, 3).reshape(b, s, h * d)

def causal_depthwise_conv(x, w):
    k, c = w.shape
    return lax.conv_general_dilated(
        x, w[:, None, :].astype(x.dtype), window_strides=(1,), padding=[(k - 1, 0)],
        dimension_numbers=("NWC", "WIO", "NWC"), feature_group_count=c)

def stick_breaking_attention(q, k, v):
    b, h, s, d = q.shape
    nq = s // SB_BLOCK
    scale = d ** -0.5
    qb = q.reshape(b, h, nq, SB_BLOCK, d).transpose(2, 0, 1, 3, 4)
    kpos = jnp.arange(s)

    def block(args):
        qc, i = args
        z = jnp.einsum("bhqd,bhkd->bhqk", qc, k).astype(jnp.float32) * scale
        qpos = i * SB_BLOCK + jnp.arange(SB_BLOCK)
        past = kpos[None, :] < qpos[:, None]
        log_1m = jnp.where(past, jax.nn.log_sigmoid(-z), 0.0)
        between = lax.cumsum(log_1m, axis=3, reverse=True) - log_1m
        wts = jnp.where(past, jnp.exp(jax.nn.log_sigmoid(z) + between), 0.0)
        return jnp.einsum("bhqk,bhkd->bhqd", wts.astype(v.dtype), v)

    out = lax.map(block, (qb, jnp.arange(nq)))
    return out.transpose(1, 2, 0, 3, 4).reshape(b, h, s, d)

def gated_delta_rule(q, k, v, g, beta):
    b, h, s, dk = q.shape
    dv = v.shape[-1]
    c = GDN_CHUNK
    n = s // c
    f32 = jnp.float32
    q = l2norm(q.astype(f32)) * dk ** -0.5
    k = l2norm(k.astype(f32))
    v = v.astype(f32)
    chunk = lambda t: t.reshape((b, h, n, c) + t.shape[3:])
    q, k, v, g, beta = map(chunk, (q, k, v, g.astype(f32), beta.astype(f32)))
    g = jnp.cumsum(g, axis=-1)
    incl = jnp.tril(jnp.ones((c, c), bool))
    strict = jnp.tril(jnp.ones((c, c), bool), -1)
    diff = g[..., :, None] - g[..., None, :]
    decay = jnp.where(incl, jnp.exp(jnp.where(incl, diff, 0.0)), 0.0)
    kb = k * beta[..., None]
    lower = jnp.where(strict, jnp.einsum("bhncd,bhnkd->bhnck", kb, k) * decay, 0.0)
    tmat = lower + jnp.eye(c, dtype=f32)
    solve = functools.partial(lax.linalg.triangular_solve, left_side=True, lower=True,
                              unit_diagonal=True)
    u = solve(tmat, v * beta[..., None])
    w = solve(tmat, kb * jnp.exp(g)[..., None])
    intra = jnp.where(incl, jnp.einsum("bhncd,bhnkd->bhnck", q, k) * decay, 0.0)
    qg = q * jnp.exp(g)[..., None]
    g_last = g[..., -1]
    kd = k * jnp.exp(g_last[..., None] - g)[..., None]

    def step(state, inp):
        qg_c, kd_c, u_c, w_c, intra_c, gl_c = inp
        v_new = u_c - jnp.einsum("bhcd,bhde->bhce", w_c, state)
        o = (jnp.einsum("bhcd,bhde->bhce", qg_c, state)
             + jnp.einsum("bhck,bhke->bhce", intra_c, v_new))
        state = state * jnp.exp(gl_c)[..., None, None] + jnp.einsum("bhcd,bhce->bhde", kd_c, v_new)
        return state, o

    xs = tuple(jnp.moveaxis(t, 2, 0) for t in (qg, kd, u, w, intra, g_last))
    _, o = lax.scan(step, jnp.zeros((b, h, dk, dv), f32), xs)
    return jnp.moveaxis(o, 0, 2).reshape(b, h, s, dv)

def moba_attention(q, k, v):
    b, h, s, d = q.shape
    bs = MOBA_BLOCK
    sp = -(-s // bs) * bs
    pad = ((0, 0), (0, 0), (0, sp - s), (0, 0))
    q, k, v = (jnp.pad(t, pad) for t in (q, k, v))
    nb = sp // bs
    ksel = min(MOBA_TOPK, nb - 1)
    scale = d ** -0.5
    kb = k.reshape(b, h, nb, bs, d)
    vb = v.reshape(b, h, nb, bs, d)
    own = jnp.arange(sp) // bs
    if ksel > 0:
        kmean = jnp.mean(kb.astype(jnp.float32), axis=3)
        gate = jnp.einsum("bhsd,bhnd->bhsn", q.astype(jnp.float32), kmean)
        fully_past = jnp.arange(nb)[None, :] < own[:, None]
        gate = jnp.where(fully_past, gate, -jnp.inf)
        _, sel = lax.top_k(gate, ksel)
    else:
        sel = jnp.zeros((b, h, sp, 0), jnp.int32)
    valid = sel < own[None, None, :, None]
    nq = sp // MOBA_QCHUNK
    qs = jnp.moveaxis(q.reshape(b, h, nq, MOBA_QCHUNK, d), 2, 0)
    sels = jnp.moveaxis(sel.reshape(b, h, nq, MOBA_QCHUNK, ksel), 2, 0)
    vals = jnp.moveaxis(valid.reshape(b, h, nq, MOBA_QCHUNK, ksel), 2, 0)
    bi = jnp.arange(b)[:, None, None]
    hi = jnp.arange(h)[None, :, None]

    def chunk(args):
        qc, selc, valc, ci = args
        ob = (ci * MOBA_QCHUNK) // bs
        k_own = lax.dynamic_index_in_dim(kb, ob, axis=2, keepdims=False)
        v_own = lax.dynamic_index_in_dim(vb, ob, axis=2, keepdims=False)
        qpos = ci * MOBA_QCHUNK + jnp.arange(MOBA_QCHUNK)
        kpos = ob * bs + jnp.arange(bs)
        s_own = jnp.einsum("bhqd,bhkd->bhqk", qc, k_own).astype(jnp.float32) * scale
        s_own = jnp.where(kpos[None, :] <= qpos[:, None], s_own, -jnp.inf)
        scores, v_sel = [], []
        for j in range(ksel):
            kj = kb[bi, hi, selc[..., j]]
            v_sel.append(vb[bi, hi, selc[..., j]])
            sj = jnp.einsum("bhqd,bhqkd->bhqk", qc, kj).astype(jnp.float32) * scale
            scores.append(jnp.where(valc[..., j, None], sj, -jnp.inf))
        p = jax.nn.softmax(jnp.concatenate(scores + [s_own], axis=-1), axis=-1).astype(v.dtype)
        o = jnp.einsum("bhqk,bhkd->bhqd", p[..., ksel * bs:], v_own)
        for j in range(ksel):
            o = o + jnp.einsum("bhqk,bhqkd->bhqd", p[..., j * bs:(j + 1) * bs], v_sel[j])
        return o

    out = lax.map(chunk, (qs, sels, vals, jnp.arange(nq)))
    return jnp.moveaxis(out, 0, 2).reshape(b, h, sp, d)[:, :, :s]

def dilated_branch(q, k, v, window, rate):
    b, h, s, d = q.shape
    span = window // rate
    seg = rate * span
    sp = -(-s // seg) * seg
    nblk = sp // seg
    scale = d ** -0.5

    def to_residue(t):
        t = jnp.pad(t, ((0, 0), (0, 0), (0, sp - s), (0, 0)))
        t = t.reshape(b, h, sp // rate, rate, d).transpose(0, 1, 3, 2, 4)
        return t.reshape(b, h, rate, nblk, span, d)

    qr, kr, vr = to_residue(q), to_residue(k), to_residue(v)
    prev = lambda t: jnp.pad(t, ((0, 0),) * 3 + ((1, 0), (0, 0), (0, 0)))[:, :, :, :-1]
    kk = jnp.concatenate([prev(kr), kr], axis=4)
    vv = jnp.concatenate([prev(vr), vr], axis=4)
    sc = jnp.einsum("bhrnqd,bhrnkd->bhrnqk", qr, kk).astype(jnp.float32) * scale
    qi = jnp.arange(span)[:, None]
    ki = jnp.arange(2 * span)[None, :]
    dist = span + qi - ki
    blk = jnp.arange(nblk)[:, None, None]
    ok = (dist >= 0) & (dist <= span) & ((blk > 0) | (ki >= span))[...]
    sc = jnp.where(ok, sc, -jnp.inf)
    m = jnp.max(sc, axis=-1, keepdims=True)
    p = jnp.exp(sc - m)
    den = jnp.sum(p, axis=-1)
    o = jnp.einsum("bhrnqk,bhrnkd->bhrnqd", p, vv.astype(jnp.float32)) / den[..., None]
    lse = m[..., 0] + jnp.log(den)
    o = o.reshape(b, h, rate, sp // rate, d).transpose(0, 1, 3, 2, 4).reshape(b, h, sp, d)[:, :, :s]
    lse = lse.reshape(b, h, rate, sp // rate).transpose(0, 1, 3, 2).reshape(b, h, sp)[:, :, :s]
    return o, lse

def dilated_attention(q, k, v):
    outs, lses = [], []
    for window, rate in zip(DIL_WINDOWS, DIL_RATES):
        o, lse = dilated_branch(q, k, v, window, rate)
        outs.append(o)
        lses.append(lse)
    wts = jax.nn.softmax(jnp.stack(lses, 0), axis=0)
    return jnp.einsum("gbhs,gbhsd->bhsd", wts, jnp.stack(outs, 0))

def even_mixer(u, w_in, conv_w, a_log, dt_bias, onorm_w, w_out):
    proj = u @ w_in
    sb_q, sb_k, sb_v, gdn_qkv, gdn_z, gdn_a, gdn_b = jnp.split(proj, _split_points(EVEN_SIZES), axis=-1)
    o_sb = stick_breaking_attention(to_heads(sb_q, SB_HEADS), to_heads(sb_k, SB_HEADS),
                                    to_heads(sb_v, SB_HEADS))
    qkv = jax.nn.silu(causal_depthwise_conv(gdn_qkv, conv_w))
    g_q, g_k, g_v = jnp.split(qkv, 3, axis=-1)
    f32 = jnp.float32
    beta = jax.nn.sigmoid(gdn_b.astype(f32)).transpose(0, 2, 1)
    g = (-jnp.exp(a_log.astype(f32)) * jax.nn.softplus(gdn_a.astype(f32) + dt_bias.astype(f32))
         ).transpose(0, 2, 1)
    o_gdn = gated_delta_rule(to_heads(g_q, GDN_HEADS), to_heads(g_k, GDN_HEADS),
                             to_heads(g_v, GDN_HEADS), g, beta)
    o_gdn = rms_norm(o_gdn, onorm_w) * jax.nn.silu(to_heads(gdn_z, GDN_HEADS).astype(f32))
    mixed = jnp.concatenate([from_heads(o_sb), from_heads(o_gdn).astype(u.dtype)], axis=-1)
    return mixed @ w_out

def odd_mixer(u, w_in, w_out):
    proj = u @ w_in
    mq, mk, mv, dq, dk, dv = jnp.split(proj, _split_points(ODD_SIZES), axis=-1)
    o_moba = moba_attention(to_heads(mq, MOBA_HEADS), to_heads(mk, MOBA_HEADS), to_heads(mv, MOBA_HEADS))
    o_dil = dilated_attention(to_heads(dq, DIL_HEADS), to_heads(dk, DIL_HEADS), to_heads(dv, DIL_HEADS))
    mixed = jnp.concatenate([from_heads(o_moba), from_heads(o_dil).astype(u.dtype)], axis=-1)
    return mixed @ w_out

def swiglu(u, w_gate, w_up, w_down):
    return (jax.nn.silu(u @ w_gate) * (u @ w_up)) @ w_down

def first_inputs(seed: int = 0) -> dict:
    key = jax.random.key(seed)
    ks = jax.random.split(key, 20)
    f32 = jnp.float32
    nrm = lambda k, shape, sc: jax.random.normal(k, shape, f32) * sc
    gain = lambda k, shape: 1.0 + 0.02 * jax.random.normal(k, shape, f32)
    x = nrm(ks[0], (BATCH, SEQ, D_MODEL), 1.0)
    dt = jnp.exp(jax.random.uniform(ks[8], (N_EVEN, GDN_HEADS), f32, math.log(1e-3), math.log(1e-1)))
    return {
        "x": x,
        "mix_norm_pre": gain(ks[1], (DEPTH, D_MODEL)),
        "mix_norm_post": gain(ks[2], (DEPTH, D_MODEL)),
        "ffn_norm_pre": gain(ks[3], (DEPTH, D_MODEL)),
        "ffn_norm_post": gain(ks[4], (DEPTH, D_MODEL)),
        "ev_w_in": nrm(ks[5], (N_EVEN, D_MODEL, EVEN_IN), D_MODEL ** -0.5),
        "ev_conv_w": nrm(ks[6], (N_EVEN, GDN_CONV, 3 * GDN_W), GDN_CONV ** -0.5),
        "ev_a_log": jnp.log(jax.random.uniform(ks[7], (N_EVEN, GDN_HEADS), f32, 1.0, 16.0)),
        "ev_dt_bias": dt + jnp.log(-jnp.expm1(-dt)),
        "ev_onorm": gain(ks[9], (N_EVEN, HEAD_DIM)),
        "ev_w_out": nrm(ks[10], (N_EVEN, MIX_W_EVEN, D_MODEL), MIX_W_EVEN ** -0.5),
        "od_w_in": nrm(ks[11], (N_ODD, D_MODEL, ODD_IN), D_MODEL ** -0.5),
        "od_w_out": nrm(ks[12], (N_ODD, MIX_W_ODD, D_MODEL), MIX_W_ODD ** -0.5),
        "ffn_w_gate": nrm(ks[13], (DEPTH, D_MODEL, D_FF), D_MODEL ** -0.5),
        "ffn_w_up": nrm(ks[14], (DEPTH, D_MODEL, D_FF), D_MODEL ** -0.5),
        "ffn_w_down": nrm(ks[15], (DEPTH, D_FF, D_MODEL), D_FF ** -0.5),
    }

def first_block(x, mix_norm_pre, mix_norm_post, ffn_norm_pre, ffn_norm_post, ev_w_in, ev_conv_w,
              ev_a_log, ev_dt_bias, ev_onorm, ev_w_out, od_w_in, od_w_out, ffn_w_gate, ffn_w_up,
              ffn_w_down):
    h = x
    for layer in range(DEPTH):
        i = layer // 2
        u = rms_norm(h, mix_norm_pre[layer])
        if layer % 2 == 0:
            u = even_mixer(u, ev_w_in[i], ev_conv_w[i], ev_a_log[i], ev_dt_bias[i], ev_onorm[i], ev_w_out[i])
        else:
            u = odd_mixer(u, od_w_in[i], od_w_out[i])
        h = h + rms_norm(u, mix_norm_post[layer])
        u = swiglu(rms_norm(h, ffn_norm_pre[layer]), ffn_w_gate[layer], ffn_w_up[layer], ffn_w_down[layer])
        h = h + rms_norm(u, ffn_norm_post[layer])
    return h


DEPTH_2 = 1

D_MIX = D_MODEL
POOL_WIDTH = D_MIX // 2
SSM_WIDTH = D_MIX - POOL_WIDTH
POOL_WINDOWS = (2, 4, 8, 16)
N_POOL_GROUPS = len(POOL_WINDOWS)
POOL_GROUP = POOL_WIDTH // N_POOL_GROUPS
SSM_GROUP = 16
N_SSM_GROUPS = SSM_WIDTH // SSM_GROUP
SSM_STATE = 64
PLE_DIM = 256
EPS = 1e-6
DT_MIN = 1e-3
DT_MAX = 1e-1
A_RE_MAX = -1e-4


def rmsnorm(x, gain):
    x32 = x.astype(jnp.float32)
    y = x32 * lax.rsqrt(jnp.mean(x32 * x32, axis=-1, keepdims=True) + EPS)
    return (y * gain.astype(jnp.float32)).astype(x.dtype)

def pool_mixer(u, w_pool, pool_scale):
    B, L, _ = u.shape
    ug = u.astype(jnp.float32).reshape(B, L, N_POOL_GROUPS, POOL_GROUP)
    t = jnp.arange(L)
    outs = []
    for g, w in enumerate(POOL_WINDOWS):
        v = ug[:, :, g]
        cs = jnp.cumsum(v, axis=1)
        lagged = jnp.pad(cs, ((0, 0), (w, 0), (0, 0)))[:, :L]
        count = jnp.minimum(t + 1, w).astype(jnp.float32)[None, :, None]
        outs.append((cs - lagged) / count - v)
    pooled = jnp.stack(outs, axis=2)
    mixed = jnp.einsum('blgc,gcd->blgd', pooled, w_pool.astype(jnp.float32))
    out = mixed.reshape(B, L, POOL_WIDTH) * pool_scale.astype(jnp.float32)
    return out.astype(u.dtype)

def _scan_combine(e1, e2):
    ar1, ai1, br1, bi1 = e1
    ar2, ai2, br2, bi2 = e2
    ar = ar2 * ar1 - ai2 * ai1
    ai = ar2 * ai1 + ai2 * ar1
    br = ar2 * br1 - ai2 * bi1 + br2
    bi = ar2 * bi1 + ai2 * br1 + bi2
    return (ar, ai, br, bi)

def ssm_mixer(u, a_re, a_im, log_dt, b_re, b_im, c_re, c_im, d_skip, w_glu):
    B, L, _ = u.shape
    f32 = jnp.float32
    u32 = u.astype(f32).reshape(B, L, N_SSM_GROUPS, SSM_GROUP)
    lam_re = jnp.minimum(a_re.astype(f32), A_RE_MAX)
    lam_im = a_im.astype(f32)
    dt = jnp.exp(log_dt.astype(f32))[:, None]
    mag = jnp.exp(lam_re * dt)
    ang = lam_im * dt
    ab_re = mag * jnp.cos(ang)
    ab_im = mag * jnp.sin(ang)
    den = lam_re * lam_re + lam_im * lam_im
    n_re = ab_re - 1.0
    n_im = ab_im
    q_re = (n_re * lam_re + n_im * lam_im) / den
    q_im = (n_im * lam_re - n_re * lam_im) / den
    br = b_re.astype(f32)
    bi = b_im.astype(f32)
    bb_re = q_re[..., None] * br - q_im[..., None] * bi
    bb_im = q_re[..., None] * bi + q_im[..., None] * br
    bu_re = jnp.einsum('blgc,gnc->blgn', u32, bb_re)
    bu_im = jnp.einsum('blgc,gnc->blgn', u32, bb_im)
    shp = (1, L, N_SSM_GROUPS, SSM_STATE)
    a_re_t = jnp.broadcast_to(ab_re[None, None], shp)
    a_im_t = jnp.broadcast_to(ab_im[None, None], shp)
    _, _, s_re, s_im = lax.associative_scan(
        _scan_combine, (a_re_t, a_im_t, bu_re, bu_im), axis=1)
    y = (jnp.einsum('blgn,gcn->blgc', s_re, c_re.astype(f32))
         - jnp.einsum('blgn,gcn->blgc', s_im, c_im.astype(f32))
         + d_skip.astype(f32).reshape(N_SSM_GROUPS, SSM_GROUP) * u32)
    y = y.reshape(B, L, SSM_WIDTH)
    g = jax.nn.gelu(y)
    hg = g @ w_glu.astype(f32)
    out = hg[..., :SSM_WIDTH] * jax.nn.sigmoid(hg[..., SSM_WIDTH:])
    return out.astype(u.dtype)

def second_inputs(seed: int = 0) -> dict:
    key = jax.random.key(seed)
    ks = jax.random.split(key, 20)
    f32 = jnp.float32
    n = lambda k, shape, s: jax.random.normal(k, shape, f32) * s
    x = jax.random.normal(ks[0], (BATCH, SEQ, D_MODEL), f32)
    p = jax.random.normal(ks[1], (DEPTH_2, BATCH, SEQ, PLE_DIM), f32)
    norm_gain = 1.0 + n(ks[2], (DEPTH_2, D_MODEL), 0.02)
    w_in = n(ks[3], (DEPTH_2, D_MODEL, 2 * D_MIX), D_MODEL ** -0.5)
    w_pool = n(ks[4], (DEPTH_2, N_POOL_GROUPS, POOL_GROUP, POOL_GROUP), POOL_GROUP ** -0.5)
    pool_scale = 1.0 + n(ks[5], (DEPTH_2, POOL_WIDTH), 0.02)
    a_re = -0.5 + n(ks[6], (DEPTH_2, N_SSM_GROUPS, SSM_STATE), 0.01)
    a_im = (math.pi * jnp.arange(SSM_STATE, dtype=f32))[None, None, :] + n(
        ks[7], (DEPTH_2, N_SSM_GROUPS, SSM_STATE), 0.01)
    log_dt = jax.random.uniform(ks[8], (DEPTH_2, N_SSM_GROUPS), f32,
                                math.log(DT_MIN), math.log(DT_MAX))
    b_scale = (2.0 * SSM_GROUP) ** -0.5
    b_re = n(ks[9], (DEPTH_2, N_SSM_GROUPS, SSM_STATE, SSM_GROUP), b_scale)
    b_im = n(ks[10], (DEPTH_2, N_SSM_GROUPS, SSM_STATE, SSM_GROUP), b_scale)
    c_scale = SSM_STATE ** -0.5
    c_re = n(ks[11], (DEPTH_2, N_SSM_GROUPS, SSM_GROUP, SSM_STATE), c_scale)
    c_im = n(ks[12], (DEPTH_2, N_SSM_GROUPS, SSM_GROUP, SSM_STATE), c_scale)
    d_skip = n(ks[13], (DEPTH_2, SSM_WIDTH), 1.0)
    w_glu = n(ks[14], (DEPTH_2, SSM_WIDTH, 2 * SSM_WIDTH), SSM_WIDTH ** -0.5)
    w_out = n(ks[15], (DEPTH_2, D_MIX, D_MODEL), D_MIX ** -0.5)
    w_ple = n(ks[16], (DEPTH_2, PLE_DIM, D_MODEL), PLE_DIM ** -0.5)
    w_ple_gate = n(ks[17], (DEPTH_2, D_MODEL, D_MODEL), D_MODEL ** -0.5)
    final_gain = 1.0 + n(ks[18], (D_MODEL,), 0.02)
    return {"x": x, "p": p, "norm_gain": norm_gain, "w_in": w_in, "w_pool": w_pool,
            "pool_scale": pool_scale, "a_re": a_re, "a_im": a_im, "log_dt": log_dt,
            "b_re": b_re, "b_im": b_im, "c_re": c_re, "c_im": c_im, "d_skip": d_skip,
            "w_glu": w_glu, "w_out": w_out, "w_ple": w_ple, "w_ple_gate": w_ple_gate,
            "final_gain": final_gain}

def second_block(x, p, norm_gain, w_in, w_pool, pool_scale, a_re, a_im, log_dt, b_re, b_im,
              c_re, c_im, d_skip, w_glu, w_out, w_ple, w_ple_gate, final_gain):
    h = x
    for i in range(DEPTH_2):
        hn = rmsnorm(h, norm_gain[i])
        proj = hn @ w_in[i]
        pool_in = proj[..., :POOL_WIDTH]
        pool_gate = proj[..., POOL_WIDTH:2 * POOL_WIDTH]
        ssm_in = proj[..., 2 * POOL_WIDTH:2 * POOL_WIDTH + SSM_WIDTH]
        ssm_gate = proj[..., 2 * POOL_WIDTH + SSM_WIDTH:]
        ya = pool_mixer(pool_in, w_pool[i], pool_scale[i]) * jax.nn.silu(pool_gate)
        yb = ssm_mixer(ssm_in, a_re[i], a_im[i], log_dt[i], b_re[i], b_im[i],
                       c_re[i], c_im[i], d_skip[i], w_glu[i]) * jax.nn.silu(ssm_gate)
        h = h + jnp.concatenate([ya, yb], axis=-1) @ w_out[i]
        h = h + (p[i] @ w_ple[i]) * jax.nn.sigmoid(h @ w_ple_gate[i])
    return rmsnorm(h, final_gain)


def setup_inputs(seed=0):
    out = dict(first_inputs(seed))
    for name, value in second_inputs(seed + 1).items():
        if name != "x":
            out[name + "_2"] = value
    return out


def reference(
    x, mix_norm_pre, mix_norm_post, ffn_norm_pre, ffn_norm_post, ev_w_in, ev_conv_w, ev_a_log,
    ev_dt_bias, ev_onorm, ev_w_out, od_w_in, od_w_out, ffn_w_gate, ffn_w_up, ffn_w_down, p_2,
    norm_gain_2, w_in_2, w_pool_2, pool_scale_2, a_re_2, a_im_2, log_dt_2, b_re_2, b_im_2,
    c_re_2, c_im_2, d_skip_2, w_glu_2, w_out_2, w_ple_2, w_ple_gate_2, final_gain_2,
):
    x = first_block(
        x, mix_norm_pre, mix_norm_post, ffn_norm_pre, ffn_norm_post, ev_w_in, ev_conv_w,
        ev_a_log, ev_dt_bias, ev_onorm, ev_w_out, od_w_in, od_w_out, ffn_w_gate, ffn_w_up,
        ffn_w_down,
    )
    return second_block(
        x, p_2, norm_gain_2, w_in_2, w_pool_2, pool_scale_2, a_re_2, a_im_2, log_dt_2, b_re_2,
        b_im_2, c_re_2, c_im_2, d_skip_2, w_glu_2, w_out_2, w_ple_2, w_ple_gate_2, final_gain_2,
    )


_drawn_inputs = setup_inputs


def setup_inputs(seed=0):
    import zlib

    import numpy as np

    out = dict(_drawn_inputs(seed))
    spreads = {}
    factors = {'ffn_norm_post': 3.432,
     'ev_onorm': 3.533,
     'norm_gain_2': 8.0,
     'pool_scale_2': 23.041,
     'a_re_2': 64.0,
     'a_im_2': 64.0,
     'log_dt_2': 64.0,
     'b_re_2': 64.0,
     'b_im_2': 64.0,
     'c_re_2': 64.0,
     'c_im_2': 64.0,
     'final_gain_2': 7.752,
     'p_2': 8.0,
     'w_ple_2': 8.0,
     'w_ple_gate_2': 8.0}
    for name, (base, spread) in spreads.items():
        noise = np.random.default_rng([zlib.crc32(name.encode()), seed]).standard_normal(out[name].shape)
        drawn = base * np.exp(spread * noise) if base else spread * noise
        out[name] = __import__('jax').numpy.asarray(drawn.astype(out[name].dtype))
    for name, factor in factors.items():
        out[name] = (out[name] * factor).astype(out[name].dtype)
    return out
```

```python
from contextlib import ExitStack
import math

import numpy as np

import concourse.bass as bass
from concourse import mybir

ALU = mybir.AluOpType
ACT = mybir.ActivationFunctionType
AX_X = mybir.AxisListType.X
F32 = mybir.dt.float32
F32R = mybir.dt.float32r

P = 128
TOK = 256
TT = TOK // P
DM = 2048
KM = DM // P
DFF = 5632
FF_IT = DFF // 512
FF_A, FF_B = 6, 5
HEADS = 8
HD = 128
EPS = 1e-6
SCALE = HD ** -0.5
CH = 512
NEG = -1e30
AR = 15104
RING = 4
PAIRS = 32
TWO_PI = 2 * math.pi
CW1 = 6.28125
CW2 = TWO_PI - CW1
PI_IN = 3.1415925
HALF_IN = 0.49999997
MAGIC = 1.5 * 2 ** 23

LINEARS = [
    ("ev_gdn", 6, 16), ("ev_sb", 6, 16), ("ev_z", 2, 16), ("ev_out", 4, 16),
    ("up0a", 2 * FF_A, 16), ("dn0a", 4, 4 * FF_A), ("up0b", 2 * FF_B, 16), ("dn0b", 4, 4 * FF_B),
    ("od_in", 12, 16), ("od_out", 4, 16),
    ("up1a", 2 * FF_A, 16), ("dn1a", 4, 4 * FF_A), ("up1b", 2 * FF_B, 16), ("dn1b", 4, 4 * FF_B),
    ("s_in", 8, 16), ("glu", 4, 8), ("s_out", 4, 16), ("ple", 4, 2), ("pg", 4, 16),
]
PROJ0 = {"ev_gdn": 0, "ev_sb": 6, "ev_z": 12, "od_in": 14, "s_in": 26}
TURN = {("ev_gdn", c): c for c in range(6)}
TURN |= {("ev_sb", c): 6 + c for c in range(4)}
TURN |= {("od_in", c): 10 + n for n, c in enumerate((0, 1, 2, 3, 6, 7, 8, 9))}
TURN |= {("s_in", c): 18 + c for c in range(4)}
TOF = {n: k for k, n in enumerate(("ev_gdn", "ev_out", "up0a", "od_in", "od_out", "up1a", "s_in", "s_out", "pg"))}
FFB = {"up0a": 0, "up0b": FF_A, "up1a": FF_IT, "up1b": FF_IT + FF_A}
POST = {"ev_out": 0, "dn0b": 1, "od_out": 2, "dn1b": 3}
PJ_EVEN, PJ_ODD, PJ_SSM = 6144, 12288, 8192
CONV, UNIT = 7168, 6144
SBW, ATW = 7168, 13312
POOLED, POOLT, WPOOL = 9216, 11264, 12288
UT, PT, SGP, SGS, BT, CT, SPAR, SCOL = 0, 2048, 4096, 6144, 9216, 11264, 14336, 14848
SROW = SPAR
SSM_AT = [22 + 5 * ct for ct in range(8)]
POOL_AT = [(1, 2), (2, 0), (2, 2), (3, 0)]
CHUNKS = {n: c for n, c, _ in LINEARS}
KTS = {n: k for n, _, k in LINEARS}
GRAN0, CHUNK0 = {}, {}
_g = _c = 0
for _n, _nc, _k in LINEARS:
    GRAN0[_n], CHUNK0[_n] = _g, _c
    _g += _nc * _k // 2
    _c += _nc


def gran(name, c, j=0):
    return GRAN0[name] + c * (KTS[name] // 2) + j


def shape_constants():
    i = np.arange(P)
    row, col = i[:, None], i[None, :]
    common = [np.eye(P), (row <= col), (row >= col), np.ones((P, P))]
    neg_strict = np.where(col < row, 0.0, NEG)
    neg_incl_t = np.where(col >= row, 0.0, NEG)
    level = [((row >> (l + 1)) == (col >> (l + 1))) & ((row >> l) & 1 == 1) & ((col >> l) & 1 == 0)
             for l in range(7)]
    key = (i[:, None, None] + P * np.arange(2)[None, :, None])
    qry = np.arange(TOK)[None, None, :]
    past = (key < qry).reshape(P, 2 * TOK)
    even = [neg_strict, neg_incl_t, level[0]] + [m.T for m in level] + [past, np.where(past, 0.0, NEG)]
    q = np.concatenate([np.repeat(i[:, None], P, 1), np.repeat(i[:, None] + P, TOK, 1)], 1)
    k = np.concatenate([np.repeat(i[None], P, 0), np.repeat(np.arange(TOK)[None], P, 0)], 1)
    causal = np.where(k <= q, 0.0, NEG)
    seen = ((q - k <= 128).astype(int) + ((q - k) % 4 == 0) + ((q - k) % 16 == 0)) * (k <= q)
    dil = np.where(seen > 0, np.log(np.maximum(seen, 1)), NEG)
    odd = [causal, dil]
    t = np.arange(TOK)
    inv = [np.repeat((1.0 / np.minimum(t + 1, w))[None], P, 0) for w in (2, 4, 8, 16)]
    parity = np.stack([(i // 16) % 2 == 0, (i // 16) % 2 == 1], 1)
    second = inv + [np.repeat(i[None], P, 0), parity]
    cat = lambda xs: np.ascontiguousarray(np.concatenate([x.astype(np.float32) for x in xs], 1))
    return {"c_common": cat(common), "c_even": cat(even), "c_odd": cat(odd), "c_second": cat(second)}


def build(nc, A, out):
    ctx = ExitStack()
    with ctx:
        def sb(name, shape, dt=F32, scope=ctx):
            return scope.enter_context(nc.sbuf_tensor(name, [P] + shape, dt))

        raw = sb("raw", [RING, 4, CH])
        whi = sb("whi", [RING, 2, CH], F32R)
        wlo = sb("wlo", [RING, 2, CH], F32R)
        h = sb("h", [TT, DM])
        u = sb("u", [TT, DM])
        cc = sb("cc", [4 * P])
        pc = sb("pc", [2304])
        grow = sb("grow", [DM])
        cols = sb("cols", [2 * P])
        st = sb("st", [192])
        ident, tri_u, tri_l, ones = (cc[:, k * P:(k + 1) * P] for k in range(4))
        xh = sb("xh", [KM, TOK], F32R)
        xl = sb("xl", [KM, TOK], F32R)
        with nc.sbuf_tensor("hTh", [P, 4 * FF_A, TOK], F32R) as hTh, \
                nc.sbuf_tensor("hTl", [P, 4 * FF_A, TOK], F32R) as hTl:
            pass
        ar = sb("ar", [AR])

        def at(o, *shape):
            n = math.prod(shape)
            assert o + n <= AR, (o, n)
            v = ar[:, o:o + n]
            if len(shape) == 2:
                v = v.rearrange("p (a b) -> p a b", a=shape[0])
            if len(shape) == 3:
                v = v.rearrange("p (a b c) -> p a b c", a=shape[0], b=shape[1])
            return v

        sg, hm = at(12288, TT, CH), at(12288 + 1024, TT, CH)
        acc = [ctx.enter_context(nc.psum_tensor(f"acc{i}", [P, CH], F32)) for i in range(4)]
        side = [ctx.enter_context(nc.psum_tensor(f"side{i}", [P, CH], F32)) for i in range(4)]

        ss = st[:, 0:8]
        ssum, rms_u, rstd_u = st[:, 8:10], st[:, 10:12], st[:, 12:14]
        ssh, rms_h, rstd = st[:, 14:16], st[:, 16:18], st[:, 18:20]

        def conv_col(tap, blk):
            return cols[:, tap * 24 + blk:tap * 24 + blk + 1]

        def gain_col(n, k):
            return cols[:, P + n * KM + k:P + n * KM + k + 1]

        def dskip_col(k):
            return cols[:, P + 80 + k:P + 81 + k]

        def pool_col(k):
            return cols[:, P + 88 + k:P + 89 + k]

        sems = {}

        def S(name):
            if name not in sems:
                sems[name] = ctx.enter_context(nc.semaphore(name))
            return sems[name]

        block = ctx.enter_context(nc.Block())

        def kview(w):
            return w.rearrange("(k p) n -> p k n", p=P)

        ev_in, od_in, s_in = kview(A["ev_w_in"][0]), kview(A["od_w_in"][0]), kview(A["w_in_2"][0])
        WEIGHTS = {
            "ev_gdn": (ev_in, [3072 + CH * c for c in range(6)]), "ev_z": (ev_in, [6144, 6656]),
            "ev_sb": (ev_in, [CH * c for c in range(6)]), "ev_out": (kview(A["ev_w_out"][0]), None),
            "od_in": (od_in, None), "od_out": (kview(A["od_w_out"][0]), None),
            "s_in": (s_in, [2048, 2560, 0, 512, 1024, 1536, 3072, 3584]),
            "glu": (kview(A["w_glu_2"][0]), [0, 1024, 512, 1536]),
            "s_out": (kview(A["w_out_2"][0]), None), "pg": (kview(A["w_ple_gate_2"][0]), None),
        }
        for l in range(2):
            down = kview(A["ffn_w_down"][l])
            WEIGHTS[f"dn{l}a"] = (down[:, 0:4 * FF_A, :], None)
            WEIGHTS[f"dn{l}b"] = (down[:, 4 * FF_A:, :], None)

        @block.sync
        def _(sp):
            def slot(n, src, ring=None):
                ring = n % RING if ring is None else ring
                if not isinstance(n, int) or n >= RING:
                    sp.wait_ge(S("lo_done"), 2 * n - 2 * RING + 2)
                sp.dma_start(raw[:, ring], src).then_inc(S(f"landed{ring}"), 16)

            for name, nch, nk in LINEARS:
                n0 = GRAN0[name] // 2
                if name[:2] == "up":
                    l, first = int(name[2]), 0 if name[3] == "a" else FF_A
                    g, w = kview(A["ffn_w_gate"][l]), kview(A["ffn_w_up"][l])
                    with sp.Fori(0, nch // 2) as i:
                        for m in range(8):
                            src = (g if m < 4 else w)[:, 4 * (m % 4):4 * (m % 4) + 4,
                                                      bass.ds(first * CH + i * CH, CH)]
                            slot(n0 + m + 8 * i, src, m % RING)
                elif name == "ple":
                    w = A["w_ple_2"][0].rearrange("(k p) (c n) -> p c k n", p=P, n=CH)
                    for m in range(2):
                        for c in range(2):
                            if c == 0:
                                sp.wait_ge(S("lo_done"), 2 * (n0 + m) - 2 * RING + 2)
                            sp.dma_start(raw[:, (n0 + m) % RING, 2 * c:2 * c + 2], w[:, 2 * m + c])\
                              .then_inc(S("ple_landed"), 16)
                else:
                    w, at_col = WEIGHTS[name]
                    per = nk // 4
                    for c in range(nch):
                        o = at_col[c] if at_col else c * CH
                        for m in range(per):
                            slot(n0 + c * per + m, w[:, 4 * m:4 * m + 4, o:o + CH])

        def raw_granule(place):
            return raw[:, place // 2, 2 * (place % 2):2 * (place % 2) + 2]

        def landed(eng, g):
            n = g // 2
            if GRAN0["ple"] <= g < GRAN0["pg"]:
                eng.wait_ge(S("ple_landed"), 64)
            else:
                before = sum(1 for k in range(GRAN0["ple"] // 2, GRAN0["pg"] // 2) if k < n and k % RING == n % RING)
                eng.wait_ge(S(f"landed{n % RING}"), 16 * (n // RING + 1 - before))

        def tab(ct):
            return grow[:, 1024 * (ct % 2):1024 * (ct % 2) + 1024].rearrange("p (m r t) -> p m r t", m=2, r=4)

        def products(n):
            return u[:, 1, 1024 * (n % 2):1024 * (n % 2) + 1024].rearrange("p (m x) -> p m x", m=2)

        states = u[:, 0].rearrange("p (r x) -> p r x", r=4)
        spare = pc[:, 1154:2178]

        def par(k):
            o = SPAR + PAIRS * k if k < 16 else SCOL + 96 + PAIRS * (k - 16)
            return at(o, PAIRS)

        (LAM, LR, ANG, AS, AC, MAG, SN, CS, AS2, AC2, S128, C128, K_, NRE, NIM, DEN, QRE, QIM, DTP, TA, TB) = range(21)
        TURNS = K_
        ANGLES = 20

        def scol(k):
            return at(SCOL + PAIRS * k, PAIRS)

        @block.gpsimd
        def _(pool):
            pool.dma_start(cc[:], A["c_common"]).then_inc(S("common_in"), 16)
            rows = at(0, 2, P)
            pool.dma_start(rows[0:96, 0], A["ev_conv_w"][0].rearrange("t (b p) -> (t b) p", p=P))\
                .then_inc(S("rows_in"), 16)
            gains = [A["mix_norm_pre"][0], A["ffn_norm_pre"][0], A["mix_norm_pre"][1], A["ffn_norm_pre"][1],
                     A["norm_gain_2"][0]]
            for n, g in enumerate(gains):
                pool.dma_start(rows[KM * n:KM * n + KM, 1], g.rearrange("(k p) -> k p", p=P))\
                    .then_inc(S("rows_in"), 16)
            pool.dma_start(rows[80:88, 1], A["d_skip_2"][0].rearrange("(k p) -> k p", p=P))\
                .then_inc(S("rows_in"), 16)
            pool.dma_start(rows[88:96, 1], A["pool_scale_2"][0].rearrange("(k p) -> k p", p=P))\
                .then_inc(S("rows_in"), 16)
            pool.dma_start(pc[:], A["c_even"]).then_inc(S("masks_in"), 16)
            pool.dma_start(grow[:, 0:8], A["ev_dt_bias"].to_broadcast([P, 8])).then_inc(S("gdn_rows_in"), 16)
            pool.dma_start(grow[:, 8:16], A["ev_a_log"].to_broadcast([P, 8])).then_inc(S("gdn_rows_in"), 16)
            pool.dma_start(grow[:, 128:256], A["ev_onorm"].to_broadcast([P, P])).then_inc(S("gdn_rows_in"), 16)
            pool.dma_start(grow[:, 256:512].rearrange("p (k n) -> p k n", n=16), ev_in[:, :, 7168:7184])\
                .then_inc(S("gdn_rows_in"), 16)

            def gain_row(n, row, wait, count):
                pool.wait_ge(S(wait), count)
                pool.dma_start(grow[:], row.unsqueeze(0).to_broadcast([P, DM])).then_inc(S("grow_in"), 16)

            gain_row(0, A["mix_norm_post"][0], "gdn_out", 20)
            pool.wait_ge(S("sb_scored"), 3 * HEADS)
            pool.dma_start(pc[:, 0:768], A["c_odd"]).then_inc(S("masks_in"), 16)
            gain_row(1, A["ffn_norm_post"][0], "ug_done", 8)
            gain_row(2, A["mix_norm_post"][1], "ug_done", 16)
            gain_row(3, A["ffn_norm_post"][1], "ug_done", 24)
            pool.wait_ge(S("at_scored"), 3 * 16)
            pool.dma_start(pc[:, 0:1154], A["c_second"]).then_inc(S("masks_in"), 16)
            pool.wait_ge(S("ssq_done"), 2 * 5)
            ssm_rows = at(SROW, 4, P)
            for n, w in enumerate((A["a_re_2"][0], A["a_im_2"][0])):
                pool.dma_start(ssm_rows[0:PAIRS, n], w.rearrange("(a b) n -> a (b n)", b=2)).then_inc(S("srow_in"), 16)
            pool.dma_start(ssm_rows[0:PAIRS, 3, 0:2], A["log_dt_2"][0].rearrange("(a b) -> a b", b=2))\
                .then_inc(S("srow_in"), 16)
            braw, craw = at(PT, 2, PAIRS, 16), at(PT + 1024, 2, 8, 64)
            for n, w in enumerate((A["c_re_2"][0], A["c_im_2"][0])):
                pool.dma_start(craw[:, n], w.rearrange("(a g) c n -> (g c) a n", g=8)).then_inc(S("c_in"), 16)
            for n, w in enumerate((A["b_re_2"][0], A["b_im_2"][0])):
                pool.dma_start(braw[:, n], w.rearrange("(a b) n c -> (b n) a c", b=2)).then_inc(S("b_in"), 16)
            iota = pc[:, 4 * TOK:4 * TOK + P].unsqueeze(1).to_broadcast([P, 4, P])
            pool.wait_ge(S("par"), ANGLES + 1)
            pool.wait_ge(S("masks_in"), 48)
            pool.wait_ge(S("ug_done"), 32)
            for ct in range(8):
                nearest, angle = tab(ct)[:, 0], tab(ct)[:, 1]
                if ct >= 2:
                    pool.wait_ge(S("unrotated"), 8 * (ct - 1))
                f = par(TURNS)[:, 4 * ct:4 * ct + 4].unsqueeze(2).to_broadcast([P, 4, P])
                pool.tensor_tensor(angle, iota, f, ALU.mult).then_inc(S("tab_arg"), 1)
                pool.wait_ge(S("tab_arg"), 5 * ct + 1)
                pool.tensor_scalar(nearest, angle, MAGIC, None, ALU.add, ALU.bypass).then_inc(S("tab_arg"), 1)
                pool.wait_ge(S("tab_arg"), 5 * ct + 2)
                pool.tensor_scalar(nearest, nearest, -MAGIC, None, ALU.add, ALU.bypass).then_inc(S("tab_arg"), 1)
                pool.wait_ge(S("tab_arg"), 5 * ct + 3)
                pool.tensor_tensor(angle, angle, nearest, ALU.subtract).then_inc(S("tab_arg"), 1)
                pool.wait_ge(S("tab_arg"), 5 * ct + 4)
                pool.tensor_scalar(angle, angle, HALF_IN, -HALF_IN, ALU.min, ALU.max).then_inc(S("tab_arg"), 1)
            pool.wait_ge(S("y_part"), 32)
            pool.dma_start(at(WPOOL, 8, 256), A["w_pool_2"][0].rearrange("g (k p) d -> p (g k) d", p=P))\
                .then_inc(S("wpool_in"), 16)
            gain_row(4, A["final_gain_2"], "unrotated", 64)
            pool.wait_ge(S("pool_mixed"), 4)
            pool.dma_start(at(13312, TT, 256), A["p_2"][0, 0].rearrange("(t p) n -> p t n", p=P))\
                .then_inc(S("p_in"), 16)

        dtb, alog, onorm = grow[:, 0:8], grow[:, 8:16], grow[:, 128:256]
        wab = grow[:, 256:512].rearrange("p (k n) -> p k n", n=16)
        ab = grow[:, 512:544].rearrange("p (t n) -> p t n", t=TT)

        def g16(k):
            return grow[:, 544 + 16 * k:560 + 16 * k]

        def g16t(k):
            return g16(k).rearrange("p (t n) -> p t n", t=TT)

        AV, T1_, T2_, T3_, SPL, GL, BE, GC, EG, NBEG, KA, EKA, OSS, ORR = range(14)
        rn = grow[:, 800:832]
        rn2 = grow[:, 832:864]

        qkv = at(0, TT, 3072)

        def unit(t, k):
            o = UNIT + (8 * t + k) * CH
            return ar[:, o:o + CH].rearrange("p (h n) -> p h n", h=4)

        KT, QT, M_, A_, LT_, MT_, T_, LM_ = range(8)

        def mask(k, n=1):
            return pc[:, k * P:(k + n) * P]

        def heads4(m):
            return m.unsqueeze(1).to_broadcast([P, 4, P])

        def pj_at(name):
            return at({"e": PJ_EVEN, "o": PJ_ODD, "s": PJ_SSM}[name[0]], TT, CH)

        def turned_to(name, c, j):
            if name == "ev_sb":
                return at(2048 * (c // 2) + 1024 * (c % 2) + 512 * j, 2, TOK)
            if name == "od_in":
                return at(6144 * (c // 6) + 2048 * (c % 6 // 2) + 1024 * (c % 2) + 512 * j, 2, TOK)
            return at(2048 * (c // 2) + 1024 * (c % 2) + 512 * j, 2, TOK)

        def att_in(name, layer_half=0):
            o = 6144 * layer_half
            return at(o, HEADS, TOK), at(o + 2048, HEADS, TOK), at(o + 4096, TT, 1024)

        def sbw(hd, k):
            return at(SBW + (3 * (hd % 2) + k) * CH, CH)

        def atw(hd, k):
            return at(ATW + (2 * (hd % 2) + k) * 384, 384)

        @block.tensor
        def _(pe):
            last_reader = {}

            def claim(bank, freed_by, count):
                if bank.name in last_reader:
                    pe.wait_ge(*last_reader[bank.name])
                last_reader[bank.name] = (S(freed_by), count)
                return bank

            def granule(g, ring, pair, lhs_h, lhs_l, k0, first, last):
                pe.wait_ge(S("lo_done"), g + 1)
                for j in range(2):
                    for t in range(TT):
                        tok = slice(t * P, t * P + P)
                        for n, (x, w) in enumerate(((lhs_h, whi), (lhs_h, wlo), (lhs_l, whi))):
                            mm = pe.matmul(acc[2 * pair + t][:], x[:, k0 + j, tok], w[:, ring, j],
                                           start=first and j == 0 and n == 0,
                                           stop=last and j == 1 and n == 2)
                mm.then_inc(S("used"), 1)

            def linear(name, lhs_h, lhs_l, freed, aside=None, first_use=None):
                per = KTS[name] // 2
                for c in range(CHUNKS[name]):
                    pair = (CHUNK0[name] + c) % 2
                    for j in range(per):
                        if aside:
                            aside(c, j)
                        if first_use:
                            first_use(c, j)
                        if j == 0:
                            for t in range(TT):
                                claim(acc[2 * pair + t], *freed(c, t))
                        g = gran(name, c, j)
                        granule(g, g % RING, pair, lhs_h, lhs_l, 2 * j, j == 0, j == per - 1)

            def projected(name):
                return lambda c, t: ("projected", 2 * (PROJ0[name] + c) + t + 1)

            def to_features(name, src):
                base = 8 * TOF[name]
                for r in range(8):
                    if name in ("ev_gdn",):
                        if r == 0:
                            pe.wait_ge(S("x_in"), 16)
                            pe.wait_ge(S("common_in"), 16)
                    elif name in ("ev_out", "s_out"):
                        if r == 0:
                            pe.wait_ge(S("sb_out"), HEADS)
                            pe.wait_ge(S("mixed"), {"ev_out": 4, "s_out": 8}[name])
                            if name == "s_out":
                                pe.wait_ge(S("pool_out"), 4)
                    elif name == "od_out":
                        if r == 0:
                            pe.wait_ge(S("at_out"), 32)
                    else:
                        n = ("up0a", "od_in", "up1a", "s_in", "pg").index(name)
                        pe.wait_ge(S("h_done"), 8 * n + 2 * (r // 2) + 2)
                    b = claim(side[r % 4], "xl_done", 2 * (base + r) + 2)
                    for j in range(2):
                        for t in range(TT):
                            k = 2 * r + j
                            mm = pe.transpose(b[:, j * TOK + t * P:j * TOK + t * P + P],
                                              src[:, t, k * P:k * P + P], ident)
                    mm.then_inc(S("tof_ready"), 1)

            def wait_features(name, n=8):
                pe.wait_ge(S("xl_done"), 2 * (8 * TOF[name] + n))

            def features_use(name):
                def use(c, j):
                    if c == 0:
                        wait_features(name, j + 1)
                return use

            def turn(name, c):
                pe.wait_ge(S("projected"), 2 * (PROJ0[name] + c) + 2)
                pj = pj_at(name)
                for j in range(2):
                    n = 2 * TURN[name, c] + j
                    if name == "ev_gdn":
                        b = claim(side[j], "conv_step", 8 * (n + 1))
                    else:
                        b = claim(side[j], "turn_done", n + 1 - 12)
                    for jb in range(2):
                        for t in range(TT):
                            mm = pe.transpose(b[:, jb * TOK + t * P:jb * TOK + t * P + P],
                                              pj[:, t, (2 * j + jb) * P:(2 * j + jb + 1) * P], ident)
                    mm.then_inc(S("turned"), 1)

            def conv_back(c):
                for j in range(2):
                    n = 2 * c + j
                    pe.wait_ge(S("conv_silu"), n + 1)
                    b = claim(side[2 + j], "qkv_done", n + 1)
                    cs = at(CONV + 1024 + j * CH, 2, TOK)
                    for t in range(TT):
                        for jb in range(2):
                            mm = pe.transpose(b[:, t * TOK + jb * P:t * TOK + jb * P + P],
                                              cs[:, jb, t * P:t * P + P], ident)
                    mm.then_inc(S("conv_back"), 1)

            pe.wait_ge(S("common_in"), 16)
            pe.wait_ge(S("rows_in"), 128)
            rows = at(0, 2, P)
            b = claim(side[0], "cols_done", 1)
            pe.transpose(b[:, 0:96], rows[0:96, 0], ident[0:96, 0:96])
            pe.transpose(b[:, P:P + 96], rows[0:96, 1], ident[0:96, 0:96]).then_inc(S("cols_ready"), 1)

            to_features("ev_gdn", h)

            def gdn_aside(c, j):
                if c == 0 and j == 4:
                    pe.wait_ge(S("gdn_rows_in"), 64)
                    wait_features("ev_gdn")
                    b = claim(side[2], "ab_done", 2)
                    for t in range(TT):
                        for k in range(KM):
                            for n, x in enumerate((xh, xl)):
                                mm = pe.matmul(b[:, 16 * t:16 * t + 16], x[:, k, t * P:t * P + P].bitcast(F32),
                                               wab[:, k], start=(k == 0 and n == 0), stop=(k == KM - 1 and n == 1))
                    mm.then_inc(S("ab_ready"), 1)
                if c > 0 and j == 2:
                    turn("ev_gdn", c - 1)
                if c > 0 and j == 5:
                    conv_back(c - 1)

            linear("ev_gdn", xh, xl, projected("ev_gdn"), gdn_aside, features_use("ev_gdn"))
            turn("ev_gdn", 5)
            conv_back(5)

            pe.wait_ge(S("gate_g"), 1)
            b = claim(side[0], "gcum_done", 2)
            pe.matmul(b[:, 0:16], tri_u, g16(GL), start=True, stop=True).then_inc(S("gcum_ready"), 1)

            def mm4(bank, lhs, rhs):
                for k in range(4):
                    mm = pe.matmul(bank[:, k * P:k * P + P], lhs(k), rhs(k), start=True, stop=True)
                return mm

            for hg in range(2):
                for t in range(TT):
                    n = 2 * hg + t
                    U = lambda k, t=t: unit(t, k)
                    if hg == 0 and t == 0:
                        pe.wait_ge(S("qk_normed"), 4)
                    for s, (o, ready) in enumerate(((1024, "kT_ready"), (0, "qT_ready"))):
                        b = claim(side[2 * t + s], "kT_done" if s == 0 else "qT_done", n + 1)
                        for k in range(4):
                            c0 = o + (4 * hg + k) * P
                            mm = pe.transpose(b[:, k * P:k * P + P], qkv[:, t, c0:c0 + P], ident)
                        mm.then_inc(S(ready), 1)
                    b = claim(acc[t], "decay_arg", 9 * (n + 1))
                    for k in range(4):
                        c0 = t * 8 + 4 * hg + k
                        mm = pe.matmul(b[:, k * P:k * P + P], g16(GL)[:, c0:c0 + 1].to_broadcast([P, P]), tri_u,
                                       start=True, stop=True)
                    mm.then_inc(S("gb_ready"), 1)
                for t in range(TT):
                    n = 2 * hg + t
                    U = lambda k, t=t: unit(t, k)
                    pe.wait_ge(S("kT_done"), n + 1)
                    b = claim(acc[2 + t], "L_done", 5 * n + 4)
                    mm4(b, lambda k: U(KT)[:, k], lambda k: U(KT)[:, k]).then_inc(S("kk_ready"), 1)
                    pe.wait_ge(S("qT_done"), n + 1)
                    b = claim(side[t], "L_done", 5 * n + 5)
                    mm4(b, lambda k: U(KT)[:, k], lambda k: U(QT)[:, k]).then_inc(S("kq_ready"), 1)
                for t in range(TT):
                    n = 2 * hg + t
                    pe.wait_ge(S("L_done"), 5 * n + 4)
                    b = claim(side[2 + t], "LT_done", n + 1)
                    for k in range(4):
                        mm = pe.transpose(b[:, k * P:k * P + P], unit(t, M_)[:, k], ident)
                    mm.then_inc(S("lt_ready"), 1)
                for l in range(1, 7):
                    for t in range(TT):
                        n = 2 * hg + t
                        U = lambda k, t=t: unit(t, k)
                        pe.wait_ge(S(f"inv_step{t}"), 22 * hg + 4 + 3 * (l - 1) + 1)
                        b = claim(side[t], f"T_done{t}", 6 * hg + l)
                        mm4(b, lambda k: U(LM_)[:, k], lambda k: U(M_)[:, k]).then_inc(S("t1_ready"), 1)
                    for t in range(TT):
                        n = 2 * hg + t
                        U = lambda k, t=t: unit(t, k)
                        pe.wait_ge(S(f"T_done{t}"), 6 * hg + l)
                        b = claim(side[2 + t], f"inv_step{t}", 22 * hg + 4 + 3 * (l - 1) + 2)
                        mm4(b, lambda k: U(MT_)[:, k], lambda k: U(T_)[:, k]).then_inc(S("p_ready"), 1)
                        b = claim(acc[t], f"inv_step{t}", 22 * hg + 4 + 3 * (l - 1) + 3)
                        mm4(b, lambda k: U(T_)[:, k], lambda k: U(MT_)[:, k]).then_inc(S("p_ready"), 1)
                U0, U1 = (lambda k: unit(0, k)), (lambda k: unit(1, k))
                pe.wait_ge(S("r_done"), 6 * hg + 1)
                b = claim(side[0], "vn_done", 2 * hg + 1)
                mm4(b, lambda k: U0(MT_)[:, k], lambda k: U0(T_)[:, k]).then_inc(S("vn_ready"), 1)
                pe.wait_ge(S("vn_done"), 2 * hg + 1)
                pe.wait_ge(S("kd_done"), hg + 1)
                b = claim(side[1], "s_done", hg + 1)
                mm4(b, lambda k: qkv[:, 0, 1024 + (4 * hg + k) * P:1024 + (4 * hg + k + 1) * P],
                    lambda k: U0(LM_)[:, k]).then_inc(S("s_ready"), 1)
                b = claim(side[2], "o_raw", 2 * hg + 1)
                mm4(b, lambda k: U0(A_)[:, k], lambda k: U0(LM_)[:, k]).then_inc(S("o_ready"), 1)
                pe.wait_ge(S("s_done"), hg + 1)
                b = claim(side[3], "r_done", 6 * hg + 6)
                mm4(b, lambda k: U1(KT)[:, k], lambda k: U0(KT)[:, k]).then_inc(S("ks_ready"), 1)
                b = claim(acc[2], "qs_done", 4 * (hg + 1))
                mm4(b, lambda k: U1(QT)[:, k], lambda k: U0(KT)[:, k]).then_inc(S("qs_ready"), 1)
                pe.wait_ge(S("r_done"), 6 * hg + 6)
                b = claim(side[0], "vn_done", 2 * hg + 2)
                mm4(b, lambda k: U1(MT_)[:, k], lambda k: U1(T_)[:, k]).then_inc(S("vn_ready"), 1)
                pe.wait_ge(S("vn_done"), 2 * hg + 2)
                b = claim(side[1], "o_raw", 2 * hg + 2)
                mm4(b, lambda k: U1(A_)[:, k], lambda k: U1(LM_)[:, k]).then_inc(S("o_ready"), 1)

            def sb_aside(c, j):
                if 0 < c <= 4 and j == 2:
                    turn("ev_sb", c - 1)

            linear("ev_sb", xh, xl, projected("ev_sb"), sb_aside)

            qT, kT, v = att_in("sb")

            def sb_scores(n):
                b = claim(side[n % 2], "sb_scored", 3 * n + 1)
                for kt in range(2):
                    mm = pe.matmul(b[:, kt * TOK:kt * TOK + TOK], kT[:, n, kt * P:kt * P + P], qT[:, n],
                                   start=True, stop=True)
                mm.then_inc(S("sb_s"), 1)

            def sb_suffix(n):
                pe.wait_ge(S("sb_scored"), 3 * n + 3)
                b = claim(side[2 + n % 2], "sb_arg", n + 1)
                y = sbw(n, 1)
                pe.matmul(b[:, 0:TOK], tri_l, y[:, 0:TOK], start=True, stop=False)
                pe.matmul(b[:, 0:TOK], ones, y[:, TOK:], start=False, stop=True)
                pe.matmul(b[:, TOK:], tri_l, y[:, TOK:], start=True, stop=True).then_inc(S("sb_c"), 1)

            def sb_values(n):
                pe.wait_ge(S("sb_w"), n + 1)
                b = claim(acc[n % 4], "sb_out", n + 1)
                w = sbw(n, 0)
                vh = lambda kt: v[:, kt, n * P:n * P + P]
                pe.matmul(b[:, 0:P], w[:, 0:P], vh(0), start=True, stop=True)
                pe.matmul(b[:, P:TOK], w[:, P:TOK], vh(0), start=True, stop=False)
                pe.matmul(b[:, P:TOK], w[:, TOK + P:], vh(1), start=False, stop=True).then_inc(S("sb_o"), 1)

            pe.wait_ge(S("projected"), 2 * (PROJ0["ev_sb"] + 6))
            pe.wait_ge(S("turn_done"), 2 * TURN["ev_sb", 3] + 2 - 12)
            pe.wait_ge(S("masks_in"), 16)
            for n in range(HEADS + 2):
                if n < HEADS:
                    sb_scores(n)
                if 1 <= n <= HEADS:
                    sb_suffix(n - 1)
                if n >= 2:
                    sb_values(n - 2)

            linear("ev_z", xh, xl, projected("ev_z"))
            to_features("ev_out", u)

            def post(name):
                return lambda c, t: ("ug_done", 8 * POST[name] + 2 * c + t + 1)

            linear("ev_out", xh, xl, post("ev_out"), None, features_use("ev_out"))

            def turn_hidden(n):
                pe.wait_ge(S("hm_done"), 2 * n + 2)
                for b in range(2):
                    for jb in range(2):
                        for t in range(TT):
                            mm = pe.transpose(side[b][:, jb * TOK + t * P:jb * TOK + t * P + P],
                                              hm[:, t, (2 * b + jb) * P:(2 * b + jb + 1) * P], ident)
                    mm.then_inc(S("hid_ready"), 1)

            def hidden(name):
                n0, blocks, g0 = FFB[name], CHUNKS[name] // 2, GRAN0[name]

                def block_of(i, first):
                    for m in range(2):
                        for j in range(8):
                            if m == 0 and j == 2 and not first:
                                pe.wait_ge(S("hTl_done"), 2 * n0 + 2 * i - 2)
                                turn_hidden(i + (n0 - 1))
                            if j == 0:
                                if first:
                                    for t in range(TT):
                                        claim(acc[2 * m + t], "sg_done", 0)
                                else:
                                    pe.wait_ge(S("hm_done" if m else "sg_done"), 2 * n0 + 2 * i)
                            if first and m == 0 and name[3] == "a":
                                wait_features("up0a" if name[2] == "0" else "up1a", j + 1)
                            granule(i * 16 + (g0 + 8 * m + j), j % RING, m, xh, xl, 2 * j, j == 0, j == 7)

                block_of(0, True)
                with pe.Fori(1, blocks) as i:
                    block_of(i, False)
                for t in range(TT):
                    last_reader[acc[t].name] = (S("sg_done"), 2 * (n0 + blocks))
                    last_reader[acc[2 + t].name] = (S("hm_done"), 2 * (n0 + blocks))
                for b in range(2):
                    last_reader[side[b].name] = (S("hTl_done"), 2 * (n0 + blocks - 1))

            def down(name, up):
                n = FFB[up] + CHUNKS[up] // 2 - 1

                def aside(c, j):
                    if c == 0 and j == 2:
                        for b in range(2):
                            claim(side[b], "hTl_done", 2 * n + 2)
                        turn_hidden(n)
                    if c == 0 and j == 0:
                        pe.wait_ge(S("hTl_done"), 2 * n)
                    if c == 0 and j == KTS[name] // 2 - 2:
                        pe.wait_ge(S("hTl_done"), 2 * n + 2)

                if name[3] == "a":
                    freed = lambda c, t: ("half_done", 8 * int(name[2]) + 2 * c + t + 1)
                else:
                    freed = lambda c, t: ("u_done", 8 * int(name[2]) + 2 * c + t + 1)
                linear(name, hTh, hTl, freed, aside)

            def feed_forward(l):
                to_features(f"up{l}a", h)
                hidden(f"up{l}a")
                down(f"dn{l}a", f"up{l}a")
                hidden(f"up{l}b")
                down(f"dn{l}b", f"up{l}b")

            feed_forward(0)

            to_features("od_in", h)

            def od_aside(c, j):
                if ("od_in", c - 1) in TURN and j == 2:
                    turn("od_in", c - 1)

            linear("od_in", xh, xl, projected("od_in"), od_aside, features_use("od_in"))

            def at_scores(n):
                qT, kT, _ = att_in("at", n // HEADS)
                hd = n % HEADS
                b = claim(side[n % 2], "at_scored", 3 * n + 1)
                pe.matmul(b[:, 0:P], qT[:, hd, 0:P], kT[:, hd, 0:P], start=True, stop=True)
                pe.matmul(b[:, P:384], qT[:, hd, P:TOK], kT[:, hd], start=True, stop=True).then_inc(S("at_s"), 1)

            def at_turn(n):
                pe.wait_ge(S("at_exp"), 2 * n + 2)
                b = claim(side[2 + n % 2], "at_pT", n + 1)
                p = atw(n, 0)
                for k in range(3):
                    mm = pe.transpose(b[:, k * P:k * P + P], p[:, k * P:k * P + P], ident)
                mm.then_inc(S("at_turned"), 1)

            def at_values(n):
                _, _, v = att_in("at", n // HEADS)
                hd = n % HEADS
                pe.wait_ge(S("at_pT"), n + 1)
                b = claim(acc[n % 4], "at_out", 2 * n + 2)
                pT = atw(n, 1)
                vh = lambda kt: v[:, kt, hd * P:hd * P + P]
                pe.matmul(b[:, 0:P], pT[:, 0:P], vh(0), start=True, stop=True)
                pe.matmul(b[:, P:TOK], pT[:, P:TOK], vh(0), start=True, stop=False)
                pe.matmul(b[:, P:TOK], pT[:, TOK:384], vh(1), start=False, stop=True).then_inc(S("at_o"), 1)

            pe.wait_ge(S("projected"), 2 * (PROJ0["od_in"] + 12))
            pe.wait_ge(S("turn_done"), 2 * TURN["od_in", 9] + 2 - 12)
            for n in range(2 * HEADS + 2):
                if n < 2 * HEADS:
                    at_scores(n)
                if 1 <= n <= 2 * HEADS:
                    at_turn(n - 1)
                if n >= 2:
                    at_values(n - 2)
            to_features("od_out", u)
            linear("od_out", xh, xl, post("od_out"), None, features_use("od_out"))
            feed_forward(1)

            to_features("s_in", h)

            def parameter_columns():
                pe.wait_ge(S("srow_ready"), 1)
                b = claim(side[2], "scol_done", 1)
                srow = at(SROW, 4, P)
                for n in range(3):
                    mm = pe.transpose(b[:, n * PAIRS:(n + 1) * PAIRS], srow[0:PAIRS, n], ident[0:PAIRS, 0:PAIRS])
                mm.then_inc(S("scol_ready"), 1)

            def turn_wide(o, n, wide_done, ready, freed, counts):
                pe.wait_ge(S(wide_done), 2 * n + 2)
                for half in range(2):
                    b = claim(side[2 + half], freed, counts[half])
                    for k in range(4):
                        ct = 4 * half + k
                        mm = pe.transpose(b[:, k * P:k * P + P], at(o, 2, 1024)[:, n, ct * P:ct * P + P], ident)
                    mm.then_inc(S(ready), 1)

            uT, bt, cts = at(UT, 8, TOK), at(BT, 2, 8, P), at(CT, 3, 8, P)

            def ssm_in(n):
                ct, r = n // 4, n % 4
                b = claim(side[n % 3], "rotated", 5 * n + 4)
                rows = slice(32 * r, 32 * r + 32)
                for m in range(2):
                    mm = pe.matmul(b[:, m * TOK:m * TOK + TOK], bt[rows, m, ct], uT[rows, ct], start=True, stop=True)
                mm.then_inc(S("bu_ready"), 1)

            def ssm_out(n):
                ct, r = n // 4, n % 4
                y = claim(side[3], "y_done", ct + 1) if r == 0 else side[3]
                pe.wait_ge(S("unrotated"), 2 * n + 2)
                q = products(n)
                o = y[32 * r:32 * r + 32, 0:TOK]
                cw = lambda k: cts[:, k, ct, 32 * r:32 * r + 32]
                pe.matmul(o, cw(0), q[:, 0, 0:TOK], start=True, stop=False)
                pe.matmul(o, cw(2), q[:, 0, TOK:], start=False, stop=False)
                pe.matmul(o, cw(1), q[:, 1, TOK:], start=False, stop=False)
                pe.matmul(o, cw(2), q[:, 1, 0:TOK], start=False, stop=True).then_inc(S("y_part"), 1)

            def s_aside(c, j):
                at_ = 8 * c + j
                if at_ in (10, 18, 26, 36):
                    turn("s_in", (10, 18, 26, 36).index(at_))
                if at_ == 9:
                    parameter_columns()
                if at_ == 12:
                    turn_wide(SGS, 0, "c_wide", "ct_ready", "ct_done", (2, 4))
                if at_ == 14:
                    turn_wide(SGS, 1, "c_wide", "ct_ready", "ct_done", (5, 6))
                if at_ == 19:
                    turn_wide(SGP, 0, "b_wide", "bt_ready", "bt_done", (1, 2))
                if at_ == 21:
                    turn_wide(SGP, 1, "b_wide", "bt_ready", "bt_done", (3, 4))
                if at_ == SSM_AT[0]:
                    pe.wait_ge(S("bt_done"), 4)
                    pe.wait_ge(S("turn_done"), 2 * TURN["s_in", 1] + 2 - 12)
                for ct in range(8):
                    if at_ == SSM_AT[ct]:
                        if ct:
                            for r in range(2):
                                ssm_out(4 * ct - 4 + r)
                        for r in range(3):
                            ssm_in(4 * ct + r)
                    if at_ == SSM_AT[ct] + 2:
                        ssm_in(4 * ct + 3)
                        if ct:
                            for r in range(2, 4):
                                ssm_out(4 * ct - 4 + r)
                if at_ == SSM_AT[7] + 5:
                    for r in range(2):
                        ssm_out(28 + r)

            linear("s_in", xh, xl, projected("s_in"), s_aside, features_use("s_in"))
            for r in range(2, 4):
                ssm_out(28 + r)

            pooled, wp = at(POOLED, 8, TOK), at(WPOOL, 8, 256)

            def glu_aside(c, j):
                if (c, j) in POOL_AT:
                    g = POOL_AT.index((c, j))
                    if g == 0:
                        pe.wait_ge(S("wpool_in"), 16)
                    pe.wait_ge(S("pooled"), g + 1)
                    b = claim(side[g], "pool_out", g + 1)
                    for t in range(TT):
                        for kt in range(2):
                            mm = pe.matmul(b[:, t * 256:t * 256 + 256], pooled[:, 2 * g + kt, t * P:t * P + P],
                                           wp[:, 2 * g + kt], start=(kt == 0), stop=(kt == 1))
                    mm.then_inc(S("pool_mixed"), 1)

            def glu_use(c, j):
                if c == 0:
                    pe.wait_ge(S("gl_done"), 2 * j + 2)

            linear("glu", xh, xl, lambda c, t: ("glu_sig", 2 * (c // 2) + t + 1) if c % 2 else ("glu_out", 2 * (c // 2) + t + 1),
                   glu_aside, glu_use)
            to_features("s_out", u)
            linear("s_out", xh, xl, lambda c, t: ("h_done", 8 * 4 + 2 * c + t + 1), None, features_use("s_out"))
            pe.wait_ge(S("p_in"), 16)
            for t in range(TT):
                b = claim(side[t], "pl_done", t + 1)
                for k in range(2):
                    mm = pe.transpose(b[:, k * P:k * P + P], at(13312, TT, 256)[:, t, k * P:k * P + P], ident)
                mm.then_inc(S("p_turned"), 1)
            to_features("pg", h)
            pe.wait_ge(S("pl_done"), 2)
            linear("ple", hTh, hTl, lambda c, t: ("ple_out", 2 * c + t + 1))
            linear("pg", xh, xl, lambda c, t: ("pg_sig", 2 * c + t + 1), None, features_use("pg"))

        NORM = {"ev_gdn": 0, "up0a": 1, "od_in": 2, "up1a": 3, "s_in": 4}
        GAIN = {"ev_gdn": 0, "up0a": 1, "od_in": 2, "up1a": 3, "s_in": 4}

        @block.scalar
        def _(act):
            act.dma_start(h[:], A["x"][0].rearrange("(t p) n -> p t n", p=P)).then_inc(S("x_in"), 16)

            def run(o, i, f, done, **kw):
                act.activation(o, i, f, **kw).then_inc(S(done), 1)

            def split(g, place=None):
                if place is None:
                    place = g % (2 * RING)
                    if g % 2 == 0 or GRAN0["ple"] <= g < GRAN0["pg"]:
                        landed(act, g)
                if not isinstance(g, int) or g >= RING:
                    act.wait_ge(S("used"), g - (RING - 1))
                act.activation(whi[:, place % RING], raw_granule(place), ACT.Copy).then_inc(S("hi_done"), 1)

            def linear(name, evac, lead, aside=None):
                per = KTS[name] // 2
                for c in range(CHUNKS[name]):
                    for j in range(per):
                        split(gran(name, c, j))
                        if j == min(2, per - 1):
                            if c == 0:
                                lead()
                            else:
                                evac(c - 1)
                        if aside:
                            aside(c, j)

            def chunk_done(name, c):
                act.wait_ge(S("used"), gran(name, c) + KTS[name] // 2)

            def project(name, c):
                if c == 0:
                    act.wait_ge(S("rstd_done"), NORM["ev_gdn" if name[0] == "e" else name] + 1)
                chunk_done(name, c)
                pair = (CHUNK0[name] + c) % 2
                f = ACT.Copy
                if (name, c) in TURN:
                    act.wait_ge(S("turned"), 2 * TURN[name, c])
                    dst = pj_at(name)
                    if (name, c) == ("ev_gdn", 0):
                        act.wait_ge(S("cols_done"), 1)
                    if (name, c) == ("ev_sb", 0):
                        act.wait_ge(S("gdn_out"), 20)
                elif name == "ev_sb":
                    dst = at(4096, TT, 1024)[:, :, CH * (c - 4):CH * (c - 3)]
                elif name == "od_in":
                    dst = at(6144 * (c // 6) + 4096, TT, 1024)[:, :, CH * (c % 2):CH * (c % 2) + CH]
                else:
                    f = ACT.Silu
                    if name == "ev_z":
                        dst = pj_at(name)
                        if c == 0:
                            act.wait_ge(S("turned"), 2 * 10)
                        if c == 1:
                            act.wait_ge(S("mixed"), 2)
                    else:
                        dst = at(SGP if c < 6 else SGS, TT, 1024)[:, :, CH * (c % 2):CH * (c % 2) + CH]
                for t in range(TT):
                    run(dst[:, t], acc[2 * pair + t][:], f, "projected", scale=rstd[:, t:t + 1])

            def turn_out(name, c):
                for j in range(2):
                    n = 2 * TURN[name, c] + j
                    act.wait_ge(S("turned"), n + 1)
                    if (name, c) == ("ev_sb", 0) and j == 0:
                        act.wait_ge(S("gdn_out"), 20)
                    run(turned_to(name, c, j), side[j][:], ACT.Copy, "turn_done")

            def features_hi(name):
                base = 8 * TOF[name]
                if name != "ev_gdn":
                    act.wait_ge(S("used"), GRAN0["ple" if name == "pg" else name])
                for r in range(8):
                    act.wait_ge(S("tof_ready"), base + r + 1)
                    if r == 0 and name == "ev_gdn":
                        act.wait_ge(S("cols_done"), 1)
                    for j in range(2):
                        k = 2 * r + j
                        if name in GAIN:
                            sc = gain_col(GAIN[name], k)
                        elif name == "s_out" and k < 8:
                            sc = pool_col(k)
                        else:
                            sc = 1.0
                        run(xh[:, k], side[r % 4][:, j * TOK:(j + 1) * TOK], ACT.Copy, "xh_done", scale=sc)

            def stats(n, src, junk):
                for t in range(TT):
                    if n > 0:
                        act.wait_ge(S("rms_done"), n)
                    if t:
                        act.wait_ge(S("ssq_done"), 2 * n + t)
                    run(junk, src[:, t], ACT.Square, "ssq_done", accum_out=ssh[:, t:t + 1])
                act.wait_ge(S("ssq_done"), 2 * n + 2)
                if n > 0:
                    act.wait_ge(S("rstd_done"), n)
                run(rms_h, ssh, ACT.Sqrt, "rms_done", scale=1.0 / DM, bias=EPS)

            JUNK = at(12288, DM)

            def lead():
                features_hi("ev_gdn")
                act.wait_ge(S("x_in"), 16)
                stats(0, h, JUNK)

            def conv_silu(c):
                for j in range(2):
                    n = 2 * c + j
                    act.wait_ge(S("conv_step"), 8 * n + 8)
                    if n >= 2:
                        act.wait_ge(S("conv_back"), n - 1)
                    run(at(CONV + 1024 + j * CH, CH), at(CONV + j * CH, CH), ACT.Silu, "conv_silu")

            def conv_out(c):
                for j in range(2):
                    n = 2 * c + j
                    act.wait_ge(S("conv_back"), n + 1)
                    run(qkv[:, :, (4 * c + 2 * j) * P:(4 * c + 2 * j + 2) * P],
                        side[2 + j][:].rearrange("p (t n) -> p t n", t=TT), ACT.Copy, "qkv_done")

            def gdn_aside(c, j):
                if c == 0 and j == 6:
                    act.wait_ge(S("ab_ready"), 1)
                    act.wait_ge(S("rstd_done"), 1)
                    for t in range(TT):
                        run(ab[:, t], side[2][:, 16 * t:16 * t + 16], ACT.Copy, "ab_done", scale=rstd[:, t:t + 1])
                if c > 0 and j == 5:
                    conv_silu(c - 1)
                if c > 0 and j == 7:
                    conv_out(c - 1)

            linear("ev_gdn", lambda c: project("ev_gdn", c), lead, gdn_aside)

            def gdn():
                act.wait_ge(S("gate_a"), 1)
                run(g16(T1_), g16(AV), ACT.Abs, "gate_act")
                act.wait_ge(S("gate_act"), 1)
                run(g16(T2_), g16(T1_), ACT.Exp, "gate_act", scale=-1.0)
                act.wait_ge(S("gate_act"), 2)
                run(g16(T3_), g16(T2_), ACT.Ln, "gate_act", bias=1.0)
                run(g16(EG)[:, 0:8], alog, ACT.Exp, "gate_act")
                run(g16t(BE), ab[:, :, 8:16], ACT.Exp, "gate_act", scale=-1.0)
                act.wait_ge(S("gcum_ready"), 1)
                run(g16(GC), side[0][:, 0:16], ACT.Copy, "gcum_done")
                run(g16(EG), side[0][:, 0:16], ACT.Exp, "gcum_done")
                act.wait_ge(S("qk_sum"), 8)
                run(rn2, rn, ACT.Sqrt, "qk_rms", bias=EPS)

                for hg in range(2):
                    for t in range(TT):
                        n = 2 * hg + t
                        act.wait_ge(S("kT_ready"), n + 1)
                        if n == 0:
                            act.wait_ge(S("conv_back"), 12)
                        run(unit(t, KT), side[2 * t][:].rearrange("p (h n) -> p h n", h=4), ACT.Copy, "kT_done")
                        act.wait_ge(S("qT_ready"), n + 1)
                        if hg:
                            act.wait_ge(S("o_raw"), 2 * hg)
                        run(unit(t, QT), side[2 * t + 1][:].rearrange("p (h n) -> p h n", h=4), ACT.Copy, "qT_done")
                    for t in range(TT):
                        n = 2 * hg + t
                        act.wait_ge(S("decay_arg"), 9 * n + 9)
                        run(unit(t, M_), unit(t, M_), ACT.Exp, "dec_done")
                        run(unit(t, A_), unit(t, A_), ACT.Exp, "dec_done")
                        ka = slice(8 * t + 4 * hg, 8 * t + 4 * hg + 4)
                        run(g16(EKA)[:, ka], g16(KA)[:, ka], ACT.Exp, "dec_done")
                    for t in range(TT):
                        n = 2 * hg + t
                        act.wait_ge(S("lt_ready"), n + 1)
                        run(unit(t, LT_), side[2 + t][:].rearrange("p (h n) -> p h n", h=4), ACT.Copy, "LT_done")
                    for l in range(1, 7):
                        for t in range(TT):
                            act.wait_ge(S("t1_ready"), (6 * hg + l - 1) * 2 + t + 1)
                            run(unit(t, T_), side[t][:].rearrange("p (h n) -> p h n", h=4), ACT.Copy, f"T_done{t}")
                    act.wait_ge(S("vn_ready"), 2 * hg + 1)
                    run(unit(0, LM_), side[0][:].rearrange("p (h n) -> p h n", h=4), ACT.Copy, "vn_done")
                    act.wait_ge(S("s_ready"), hg + 1)
                    run(unit(0, KT), side[1][:].rearrange("p (h n) -> p h n", h=4), ACT.Copy, "s_done")
                    act.wait_ge(S("qs_ready"), hg + 1)
                    for k in range(4):
                        c0 = 8 + 4 * hg + k
                        run(unit(0, QT)[:, k], acc[2][:, k * P:k * P + P], ACT.Copy, "qs_done",
                            scale=g16(EG)[:, c0:c0 + 1])
                    act.wait_ge(S("vn_ready"), 2 * hg + 2)
                    run(unit(1, LM_), side[0][:].rearrange("p (h n) -> p h n", h=4), ACT.Copy, "vn_done")
                    for t in range(TT):
                        n = 2 * hg + t
                        act.wait_ge(S("gdn_out"), 5 * n + 2)
                        c0 = slice(8 * t + 4 * hg, 8 * t + 4 * hg + 4)
                        run(g16(ORR)[:, c0], g16(OSS)[:, c0], ACT.Sqrt, "o_rms", scale=1.0 / HD, bias=EPS)

            def lead():
                project("ev_gdn", 5)
                conv_silu(5)
                conv_out(5)
                gdn()

            def sb_aside(c, j):
                if 0 < c <= 4 and j == 4:
                    turn_out("ev_sb", c - 1)

            linear("ev_sb", lambda c: project("ev_sb", c), lead, sb_aside)

            def stick_breaking():
                def scored(n):
                    x, y = sbw(n, 0), sbw(n, 1)
                    act.wait_ge(S("sb_s"), n + 1)
                    if n >= 2:
                        act.wait_ge(S("sb_o"), n - 1)
                        act.wait_ge(S("sb_c"), n - 1)
                    b = side[n % 2][:]
                    run(x, b, ACT.Abs, "sb_act", scale=SCALE)
                    act.wait_ge(S("sb_act"), 4 * n + 1)
                    run(x, x, ACT.Exp, "sb_act", scale=-1.0)
                    act.wait_ge(S("sb_act"), 4 * n + 2)
                    run(x, x, ACT.Ln, "sb_act", bias=1.0)
                    run(y, b, ACT.Relu, "sb_act", scale=SCALE)

                def weights(n):
                    act.wait_ge(S("sb_arg"), n + 1)
                    run(sbw(n, 0), sbw(n, 2), ACT.Exp, "sb_w")

                for n in range(HEADS + 1):
                    if n < HEADS:
                        scored(n)
                    if n >= 1:
                        weights(n - 1)

            def lead():
                project("ev_sb", 5)
                stick_breaking()

            linear("ev_z", lambda c: project("ev_z", c), lead)

            def square_out(name, c):
                n = 8 * POST[name] + 2 * c
                if name[:2] != "dn":
                    chunk_done(name, c)
                pair = (CHUNK0[name] + c) % 2
                for t in range(TT):
                    if name[:2] == "dn":
                        act.wait_ge(S("u_done"), 8 * int(name[2]) + 2 * c + t + 1)
                        src = u[:, t, c * CH:c * CH + CH]
                    else:
                        src = acc[2 * pair + t][:]
                    if n + t:
                        act.wait_ge(S("sq_done"), n + t)
                    if n + t and POST[name] and c == 0:
                        act.wait_ge(S("ssum_done"), POST[name])
                    run(at(14336, CH), src, ACT.Square, "sq_done", accum_out=ss[:, 4 * t + c:4 * t + c + 1])

            def rms_out(name):
                act.wait_ge(S("ssum_done"), POST[name] + 1)
                if POST[name]:
                    act.wait_ge(S("rstdu_done"), POST[name])
                run(rms_u, ssum, ACT.Sqrt, "rmsu_done", scale=1.0 / DM, bias=EPS)

            def lead():
                project("ev_z", 1)
                features_hi("ev_out")

            linear("ev_out", lambda c: square_out("ev_out", c), lead)

            def turn_hidden(n, k):
                for b in range(2):
                    act.wait_ge(S("hid_ready"), 2 * n + b + 1)
                    act.activation(hTh[:, bass.ds(4 * k + 2 * b, 2)] if not isinstance(k, int)
                                   else hTh[:, 4 * k + 2 * b:4 * k + 2 * b + 2],
                                   side[b][:].rearrange("p (a b) -> p a b", a=2), ACT.Copy).then_inc(S("hTh_done"), 1)

            def hidden(name, lead):
                n0, blocks, g0 = FFB[name], CHUNKS[name] // 2, GRAN0[name]

                def block_of(i, first):
                    for m in range(2):
                        for j in range(8):
                            if j % 2 == 0:
                                n = (g0 + 8 * m + j) // 2
                                act.wait_ge(S(f"landed{n % RING}"), i * 32 + 16 * (n // RING + 1))
                            split(i * 16 + (g0 + 8 * m + j), j)
                            if first and m == 0 and j == 2:
                                lead()
                            if not first and m == 0 and j == 5:
                                turn_hidden(i + (n0 - 1), i - 1)
                            if m == 1 and j == 2:
                                act.wait_ge(S("used"), i * 16 + (g0 + 8))
                                if not first:
                                    act.wait_ge(S("hm_done"), 2 * n0 + 2 * i)
                                elif n0:
                                    act.wait_ge(S("hm_done"), 2 * n0)
                                if first and name[3] == "a":
                                    act.wait_ge(S("rstd_done"), NORM[name] + 1)
                                for t in range(TT):
                                    act.activation(sg[:, t], acc[t][:], ACT.Silu, scale=rstd[:, t:t + 1])\
                                        .then_inc(S("sg_done"), 1)

                block_of(0, True)
                with act.Fori(1, blocks) as i:
                    block_of(i, False)

            def down(name, up, evac):
                n, blocks = FFB[up] + CHUNKS[up] // 2 - 1, CHUNKS[up] // 2

                def aside(c, j):
                    if c == 0 and j == 5:
                        turn_hidden(n, blocks - 1)

                linear(name, evac, lambda: None, aside)

            def half_out(l, c):
                chunk_done(f"dn{l}a", c)
                pair = (CHUNK0[f"dn{l}a"] + c) % 2
                for t in range(TT):
                    if c == 0:
                        act.wait_ge(S("h_done"), 8 * (2 * l + 1))
                    run(u[:, t, c * CH:c * CH + CH], acc[2 * pair + t][:], ACT.Copy, "half_done")

            def feed_forward(l, before):
                def lead():
                    square_out(before, 3)
                    rms_out(before)
                    features_hi(f"up{l}a")
                    stats(NORM[f"up{l}a"], h, JUNK)

                hidden(f"up{l}a", lead)
                down(f"dn{l}a", f"up{l}a", lambda c: half_out(l, c))
                hidden(f"up{l}b", lambda: half_out(l, 3))
                down(f"dn{l}b", f"up{l}b", lambda c: square_out(f"dn{l}b", c))

            feed_forward(0, "ev_out")

            def lead():
                square_out("dn0b", 3)
                rms_out("dn0b")
                features_hi("od_in")
                stats(NORM["od_in"], h, JUNK)

            def od_aside(c, j):
                if ("od_in", c - 1) in TURN and j == 4:
                    turn_out("od_in", c - 1)

            linear("od_in", lambda c: project("od_in", c), lead, od_aside)

            def attention():
                def exps(n):
                    act.wait_ge(S("at_scored"), 3 * n + 3)
                    p = atw(n, 0)
                    for t, cl in enumerate((slice(0, P), slice(P, 384))):
                        run(p[:, cl], p[:, cl], ACT.Exp, "at_exp", bias=st[:, 24 + 2 * (n % 2) + t:25 + 2 * (n % 2) + t],
                            accum_out=st[:, 32 + 2 * (n % 2) + t:33 + 2 * (n % 2) + t])

                def turned(n):
                    act.wait_ge(S("at_turned"), n + 1)
                    if n >= 2:
                        act.wait_ge(S("at_o"), n - 1)
                    run(atw(n, 1), side[2 + n % 2][:, 0:384], ACT.Copy, "at_pT")

                def values(n):
                    act.wait_ge(S("at_o"), n + 1)
                    act.wait_ge(S("at_recip"), n + 1)
                    for t in range(TT):
                        run(u[:, t, n * P:n * P + P], acc[n % 4][:, t * P:t * P + P], ACT.Copy, "at_out",
                            scale=st[:, 40 + 2 * (n % 2) + t:41 + 2 * (n % 2) + t])

                for n in range(2 * HEADS + 2):
                    if n < 2 * HEADS:
                        if n >= 2:
                            act.wait_ge(S("at_recip"), n - 1)
                        exps(n)
                    if 1 <= n <= 2 * HEADS:
                        turned(n - 1)
                    if n >= 2:
                        values(n - 2)

            def lead():
                project("od_in", 11)
                attention()
                features_hi("od_out")

            linear("od_out", lambda c: square_out("od_out", c), lead)
            feed_forward(1, "od_out")

            def lead():
                square_out("dn1b", 3)
                rms_out("dn1b")
                features_hi("s_in")
                stats(NORM["s_in"], h, JUNK)

            def turned_wide(n, ready, done, outs):
                for half in range(2):
                    act.wait_ge(S(ready), 2 * n + half + 1)
                    b = side[2 + half][:].rearrange("p (a b) -> p a b", a=4)
                    buf = at(CT, 3, 8, P) if ready == "ct_ready" else at(BT, 2, 8, P)
                    for k, sc in outs:
                        run(buf[:, k, 4 * half:4 * half + 4], b, ACT.Copy, done, scale=sc)

            def tables(ct):
                act.wait_ge(S("tab_arg"), 5 * ct + 5)
                c, s = tab(ct)[:, 0], tab(ct)[:, 1]
                run(c, s, ACT.Abs, "tab_abs")
                act.wait_ge(S("tab_abs"), ct + 1)
                run(c, c, ACT.Sin, "tab_done", scale=-TWO_PI, bias=math.pi / 2)
                run(s, s, ACT.Sin, "tab_done", scale=TWO_PI)

            def gelu(ct):
                act.wait_ge(S("y_done"), ct + 1)
                y = at(UT, 8, TOK)[:, ct]
                run(y, y, ACT.Gelu_apprx_tanh, "gelu_done")

            def s_aside(c, j):
                at_ = 8 * c + j
                if at_ in (12, 20, 28, 38):
                    if at_ == 28:
                        act.wait_ge(S("c_wide"), 4)
                        act.wait_ge(S("b_wide"), 4)
                    turn_out("s_in", (12, 20, 28, 38).index(at_))
                if at_ == 11:
                    act.wait_ge(S("scol_ready"), 1)
                    run(at(SCOL, 96), side[2][:, 0:96], ACT.Copy, "scol_done")
                    act.wait_ge(S("scol_done"), 1)
                    run(par(DTP), scol(2), ACT.Exp, "dt_done")
                if at_ == 14:
                    turned_wide(0, "ct_ready", "ct_done", ((0, 1.0), (1, -1.0)))
                if at_ == 15:
                    act.wait_ge(S("par"), ANGLES)
                    run(par(MAG), par(LR), ACT.Exp, "mag_done")
                    for o, i in ((SN, AS), (CS, AC), (S128, AS2), (C128, AC2)):
                        run(par(o), par(i), ACT.Sin, "sines")
                if at_ == 16:
                    turned_wide(1, "ct_ready", "ct_done", ((2, -1.0),))
                if at_ == 21:
                    turned_wide(0, "bt_ready", "bt_done", ((0, 1.0),))
                if at_ == 23:
                    turned_wide(1, "bt_ready", "bt_done", ((1, 1.0),))
                if at_ == 19:
                    tables(0)
                for ct in range(8):
                    if ct and at_ == SSM_AT[ct]:
                        tables(ct)
                    if at_ == SSM_AT[ct] + 10:
                        gelu(ct)

            def s_evac(c):
                if c == 4:
                    act.wait_ge(S("bt_ready"), 4)
                project("s_in", c)

            linear("s_in", s_evac, lead, s_aside)

            def lead():
                project("s_in", 7)
                act.wait_ge(S("used"), GRAN0["glu"])
                for ct in range(8):
                    if ct == 4:
                        gelu(7)
                    act.wait_ge(S("gelu_done"), ct + 1)
                    run(xh[:, ct], at(UT, 8, TOK)[:, ct], ACT.Copy, "gh_done")

            def glu_out(c):
                if c % 2:
                    chunk_done("glu", c)
                    m = c // 2
                    if m:
                        act.wait_ge(S("mixed"), 4 + 2 * m)
                    for t in range(TT):
                        run(spare[:, CH * t:CH * t + CH], acc[2 + t][:], ACT.Sigmoid, "glu_sig")

            assert CHUNK0["glu"] % 2 == 0 and CHUNK0["pg"] % 2 == 0
            linear("glu", glu_out, lead)

            def lead():
                glu_out(3)
                features_hi("s_out")

            linear("s_out", lambda c: None, lead)

            def lead():
                act.wait_ge(S("p_turned"), 2)
                for k in range(2):
                    for t in range(TT):
                        run(hTh[:, k, t * P:t * P + P], side[t][:, k * P:k * P + P], ACT.Copy, "ph_done")
                features_hi("pg")

            for c in range(4):
                split(gran("ple", c))
                if c == 2:
                    lead()
            for c in range(4):
                act.wait_ge(S("used"), gran("ple", c) + 1)
                pair = (CHUNK0["ple"] + c) % 2
                for t in range(TT):
                    run(u[:, t, c * CH:c * CH + CH], acc[2 * pair + t][:], ACT.Copy, "ple_out")

            def gate_out(c):
                chunk_done("pg", c)
                pair = (CHUNK0["pg"] + c) % 2
                for t in range(TT):
                    if c:
                        act.wait_ge(S("gated"), 2 * (2 * c + t) - 2)
                    run(sg[:, t], acc[2 * pair + t][:], ACT.Sigmoid, "pg_sig")

            linear("pg", gate_out, lambda: None)
            gate_out(3)
            act.wait_ge(S("gated"), 16)
            stats(5, h, u[:, 0])
            act.wait_ge(S("final"), 8)
            act.dma_start(out[0].rearrange("(t p) n -> p t n", p=P), h[:]).then_inc(S("out_done"), 16)
            act.wait_ge(S("out_done"), 16)

        @block.vector
        def _(dve):
            def tt(o, a, b, op, done):
                dve.tensor_tensor(o, a, b, op).then_inc(S(done), 1)

            def stt(o, a, sc, b, op0, op1, done, **kw):
                dve.scalar_tensor_tensor(o, a, sc, b, op0, op1, **kw).then_inc(S(done), 1)

            def ts(o, a, s0, s1, op0, op1, done):
                dve.tensor_scalar(o, a, s0, s1, op0, op1).then_inc(S(done), 1)

            def split(g, place=None):
                place = g % (2 * RING) if place is None else place
                dve.wait_ge(S("hi_done"), g + 1)
                dve.tensor_tensor(wlo[:, place % RING], raw_granule(place), whi[:, place % RING].bitcast(F32),
                                  ALU.subtract).then_inc(S("lo_done"), 1)

            def linear(name, evac, lead, aside=None):
                per = KTS[name] // 2
                for c in range(CHUNKS[name]):
                    for j in range(per):
                        split(gran(name, c, j))
                        if j == min(2, per - 1):
                            if c == 0:
                                lead()
                            else:
                                evac(c - 1)
                        if aside:
                            aside(c, j)

            def chunk_done(name, c):
                dve.wait_ge(S("used"), gran(name, c) + KTS[name] // 2)

            def features_lo(name):
                base = 8 * TOF[name]
                for r in range(8):
                    for j in range(2):
                        k = 2 * r + j
                        dve.wait_ge(S("xh_done"), 2 * (base + r) + 2)
                        b = side[r % 4][:, j * TOK:(j + 1) * TOK]
                        hi = xh[:, k].bitcast(F32)
                        if name in GAIN:
                            stt(xl[:, k], b, gain_col(GAIN[name], k), hi, ALU.mult, ALU.subtract, "xl_done")
                        elif name == "s_out" and k < 8:
                            stt(xl[:, k], b, pool_col(k), hi, ALU.mult, ALU.subtract, "xl_done")
                        else:
                            tt(xl[:, k], b, hi, ALU.subtract, "xl_done")

            def reciprocal_rms(n):
                dve.wait_ge(S("rms_done"), n + 1)
                dve.reciprocal(rstd, rms_h).then_inc(S("rstd_done"), 1)

            dve.wait_ge(S("cols_ready"), 1)
            dve.tensor_copy(cols[:].rearrange("p (a b) -> p a b", a=2)[:, :, 0:96],
                            side[0][:, 0:2 * P].rearrange("p (a b) -> p a b", a=2)[:, :, 0:96])\
                .then_inc(S("cols_done"), 1)

            def conv(c):
                for j in range(2):
                    n = 2 * c + j
                    dve.wait_ge(S("turned"), n + 1)
                    if n >= 2:
                        dve.wait_ge(S("conv_silu"), n - 1)
                    x = side[j][:].rearrange("p (a b) -> p a b", a=2)
                    y = at(CONV + j * CH, 2, TOK)
                    for back in range(4):
                        for jb in range(2):
                            w = conv_col(3 - back, 4 * c + 2 * j + jb)
                            if back == 0:
                                ts(y[:, jb], x[:, jb], w, None, ALU.mult, ALU.bypass, "conv_step")
                            else:
                                dve.wait_ge(S("conv_step"), 8 * n + 2 * back + jb - 1)
                                stt(y[:, jb, back:], x[:, jb, 0:TOK - back], w, y[:, jb, back:],
                                    ALU.mult, ALU.add, "conv_step")

            def lead():
                features_lo("ev_gdn")
                reciprocal_rms(0)

            linear("ev_gdn", lambda c: None, lead, lambda c, j: conv(c - 1) if c > 0 and j == 4 else None)

            def four(x):
                return x.rearrange("p (h n) -> p h n", h=4)

            def gdn():
                dve.wait_ge(S("ab_done"), 2)
                dve.wait_ge(S("gdn_rows_in"), 64)
                tt(g16t(AV), ab[:, :, 0:8], dtb.unsqueeze(1).to_broadcast([P, TT, 8]), ALU.add, "gate_a")
                dve.wait_ge(S("gate_act"), 4)
                stt(g16(SPL), g16(AV), 0.0, g16(T3_), ALU.max, ALU.add, "gate_v")
                dve.wait_ge(S("gate_v"), 1)
                stt(g16t(GL), g16t(SPL), -1.0, g16(EG)[:, 0:8].unsqueeze(1).to_broadcast([P, TT, 8]),
                    ALU.mult, ALU.mult, "gate_g")
                dve.wait_ge(S("gate_act"), 5)
                ts(g16(BE), g16(BE), 1.0, None, ALU.add, ALU.bypass, "gate_v")
                dve.wait_ge(S("gate_v"), 2)
                dve.reciprocal(g16(BE), g16(BE)).then_inc(S("gate_v"), 1)
                sq = at(CONV + 2048, HEADS, HD)
                dve.wait_ge(S("qkv_done"), 12)
                for t in range(TT):
                    for m in range(2):
                        n = 2 * t + m
                        x = qkv[:, t, 1024 * m:1024 * m + 1024].rearrange("p (h n) -> p h n", h=HEADS)
                        if n:
                            dve.wait_ge(S("qk_sum"), 2 * n)
                        tt(sq, x, x, ALU.mult, "qk_sum")
                        dve.wait_ge(S("qk_sum"), 2 * n + 1)
                        dve.tensor_reduce(rn[:, 8 * n:8 * n + 8], sq, AX_X, ALU.add).then_inc(S("qk_sum"), 1)
                dve.wait_ge(S("gcum_done"), 2)
                dve.wait_ge(S("gate_v"), 3)
                stt(g16(NBEG), g16(BE), -1.0, g16(EG), ALU.mult, ALU.mult, "gate_v")
                dve.wait_ge(S("qk_rms"), 1)
                dve.reciprocal(rn, rn2).then_inc(S("gate_v"), 1)
                dve.wait_ge(S("gate_v"), 5)
                for t in range(TT):
                    for m in range(2):
                        n = 2 * t + m
                        x = qkv[:, t, 1024 * m:1024 * m + 1024].rearrange("p (h n) -> p h n", h=HEADS)
                        f = rn[:, 8 * n:8 * n + 8].unsqueeze(2).to_broadcast([P, HEADS, HD])
                        if m == 0:
                            stt(x, x, SCALE, f, ALU.mult, ALU.mult, "qk_normed")
                        else:
                            tt(x, x, f, ALU.mult, "qk_normed")

                mult, add, sub = ALU.mult, ALU.add, ALU.subtract
                for hg in range(2):
                    def beta(t, k):
                        c0 = 8 * t + 4 * hg + k
                        return g16(BE)[:, c0:c0 + 1]

                    for t in range(TT):
                        n = 2 * hg + t
                        dve.wait_ge(S("gb_ready"), n + 1)
                        if hg:
                            dve.wait_ge(S("gdn_out"), 5 * 2 * hg)
                        for k in range(4):
                            c0 = 8 * t + 4 * hg + k
                            G = g16(GC)[:, c0:c0 + 1]
                            gb = acc[t][:, k * P:k * P + P]
                            stt(unit(t, M_)[:, k], gb, G, mask(0), sub, sub, "decay_arg", reverse1=True)
                            stt(unit(t, A_)[:, k], gb, G, mask(1), sub, add, "decay_arg")
                        ka = slice(8 * t + 4 * hg, 8 * t + 4 * hg + 4)
                        tt(g16(KA)[:, ka], four(acc[t][:])[:, :, P - 1], g16(GC)[:, ka], sub, "decay_arg")
                    for t in range(TT):
                        n = 2 * hg + t
                        dve.wait_ge(S("dec_done"), 3 * n + 3)
                        dve.wait_ge(S("kk_ready"), n + 1)
                        for k in range(4):
                            M = unit(t, M_)[:, k]
                            stt(M, acc[2 + t][:, k * P:k * P + P], beta(t, k), M, mult, mult, "L_done")
                        dve.wait_ge(S("kq_ready"), n + 1)
                        tt(unit(t, A_), four(side[t][:]), unit(t, A_), mult, "L_done")
                    for t in range(TT):
                        n = 2 * hg + t
                        inv = f"inv_step{t}"
                        dve.wait_ge(S("L_done"), 5 * n + 4)
                        stt(unit(t, T_), unit(t, M_), -1.0, heads4(mask(2)), mult, mult, inv)
                        dve.wait_ge(S("LT_done"), n + 1)
                        dve.wait_ge(S(inv), 22 * hg + 1)
                        tt(unit(t, M_), unit(t, T_), heads4(ident), add, inv)
                        stt(unit(t, LM_), unit(t, LT_), -1.0, heads4(mask(3)), mult, mult, inv)
                        dve.wait_ge(S(inv), 22 * hg + 3)
                        tt(unit(t, MT_), unit(t, LM_), heads4(ident), add, inv)
                    for l in range(1, 7):
                        for t in range(TT):
                            inv, b0 = f"inv_step{t}", 22 * hg + 4 + 3 * (l - 1)
                            dve.wait_ge(S(inv), b0)
                            tt(unit(t, LM_), unit(t, LT_), heads4(mask(3 + l)), mult, inv)
                        for t in range(TT):
                            inv, b0 = f"inv_step{t}", 22 * hg + 4 + 3 * (l - 1)
                            dve.wait_ge(S("p_ready"), 2 * (2 * (6 * hg + l - 1) + t) + 1)
                            tt(unit(t, M_), unit(t, M_), four(side[2 + t][:]), sub, inv)
                            dve.wait_ge(S("p_ready"), 2 * (2 * (6 * hg + l - 1) + t) + 2)
                            tt(unit(t, MT_), unit(t, MT_), four(acc[t][:]), sub, inv)
                    for t in range(TT):
                        v = qkv[:, t, 2048 + CH * hg:2048 + CH * hg + CH]
                        b = g16(BE)[:, 8 * t + 4 * hg:8 * t + 4 * hg + 4].unsqueeze(2).to_broadcast([P, 4, P])
                        tt(unit(t, T_), four(v), b, mult, "r_done")
                        if t == 0:
                            k0 = four(qkv[:, 0, 1024 + CH * hg:1024 + CH * hg + CH])
                            tt(k0, k0, g16(EKA)[:, 4 * hg:4 * hg + 4].unsqueeze(2).to_broadcast([P, 4, P]),
                               mult, "kd_done")
                    dve.wait_ge(S("o_ready"), 2 * hg + 1)
                    dve.tensor_copy(unit(0, M_), four(side[2][:])).then_inc(S("o_raw"), 1)
                    dve.wait_ge(S("ks_ready"), hg + 1)
                    dve.wait_ge(S("r_done"), 6 * hg + 2)
                    for k in range(4):
                        c0 = 8 + 4 * hg + k
                        R = unit(1, T_)[:, k]
                        stt(R, side[3][:, k * P:k * P + P], g16(NBEG)[:, c0:c0 + 1], R, mult, add, "r_done")
                    dve.wait_ge(S("o_ready"), 2 * hg + 2)
                    dve.wait_ge(S("qs_done"), 4 * hg + 4)
                    tt(unit(1, M_), four(side[1][:]), unit(0, QT), add, "o_raw")
                    for t in range(TT):
                        n = 2 * hg + t
                        O, Q = unit(t, M_), unit(t, T_)
                        c0 = slice(8 * t + 4 * hg, 8 * t + 4 * hg + 4)
                        dve.wait_ge(S("o_raw"), n + 1)
                        tt(Q, O, O, mult, "gdn_out")
                        dve.wait_ge(S("gdn_out"), 5 * n + 1)
                        dve.tensor_reduce(g16(OSS)[:, c0], Q, AX_X, add).then_inc(S("gdn_out"), 1)
                        dve.wait_ge(S("o_rms"), n + 1)
                        dve.reciprocal(g16(ORR)[:, c0], g16(ORR)[:, c0]).then_inc(S("gdn_out"), 1)
                        dve.wait_ge(S("gdn_out"), 5 * n + 3)
                        tt(O, O, g16(ORR)[:, c0].unsqueeze(2).to_broadcast([P, 4, P]), mult, "gdn_out")
                        dve.wait_ge(S("gdn_out"), 5 * n + 4)
                        tt(four(u[:, t, 1024 + CH * hg:1024 + CH * hg + CH]), O, heads4(onorm), mult, "gdn_out")

            def lead():
                conv(5)
                dve.wait_ge(S("masks_in"), 16)
                gdn()

            linear("ev_sb", lambda c: None, lead)

            def stick_breaking():
                past, neg = pc[:, 10 * P:10 * P + CH], pc[:, 10 * P + CH:10 * P + 2 * CH]

                def scored(n):
                    x, y, z = (sbw(n, k) for k in range(3))
                    dve.wait_ge(S("sb_act"), 4 * n + 4)
                    if n >= 2:
                        dve.wait_ge(S("sb_w"), n - 1)
                    stt(z, side[n % 2][:], SCALE, neg, ALU.mult, ALU.add, "sb_scored")
                    tt(y, y, x, ALU.add, "sb_scored")
                    dve.wait_ge(S("sb_scored"), 3 * n + 2)
                    tt(y, y, past, ALU.mult, "sb_scored")

                def argument(n):
                    dve.wait_ge(S("sb_c"), n + 1)
                    z = sbw(n, 2)
                    tt(z, z, side[2 + n % 2][:], ALU.subtract, "sb_arg")

                def out_(n):
                    dve.wait_ge(S("sb_o"), n + 1)
                    dve.tensor_copy(u[:, :, n * P:n * P + P],
                                    acc[n % 4][:, 0:TOK].rearrange("p (t n) -> p t n", t=TT)).then_inc(S("sb_out"), 1)

                for n in range(HEADS + 2):
                    if n < HEADS:
                        scored(n)
                    if 1 <= n <= HEADS:
                        argument(n - 1)
                    if n >= 2:
                        out_(n - 2)

            def z_gate(c):
                for t in range(TT):
                    dve.wait_ge(S("projected"), 2 * (PROJ0["ev_z"] + c) + t + 1)
                    x = u[:, t, 1024 + CH * c:1024 + CH * c + CH]
                    tt(x, x, pj_at("ev_z")[:, t], ALU.mult, "mixed")

            def lead():
                stick_breaking()

            linear("ev_z", z_gate, lead)

            def gained(name, c):
                n = POST[name]
                if n < 4 and c == 0:
                    dve.wait_ge(S("grow_in"), 16 * (n + 1))
                    if n:
                        dve.wait_ge(S("h_done"), 8 * n)
                pair = (CHUNK0[name] + c) % 2
                cl = slice(c * CH, c * CH + CH)
                if name[:2] == "dn":
                    l = int(name[2])
                    chunk_done(name, c)
                    dve.wait_ge(S("half_done"), 8 * (l + 1))
                    for t in range(TT):
                        tt(u[:, t, cl], acc[2 * pair + t][:], u[:, t, cl], ALU.add, "u_done")
                for t in range(TT):
                    dve.wait_ge(S("sq_done"), 8 * n + 2 * c + t + 1)
                    src = u[:, t, cl] if name[:2] == "dn" else acc[2 * pair + t][:]
                    tt(u[:, t, cl], src, grow[:, cl], ALU.mult, "ug_done")

            def into_stream(name):
                n = POST[name]
                dve.wait_ge(S("sq_done"), 8 * n + 8)
                if n:
                    dve.wait_ge(S("rmsu_done"), n)
                dve.tensor_reduce(ssum, ss.rearrange("p (t c) -> p t c", t=TT), AX_X, ALU.add)\
                    .then_inc(S("ssum_done"), 1)
                dve.wait_ge(S("rmsu_done"), n + 1)
                dve.reciprocal(rstd_u, rms_u).then_inc(S("rstdu_done"), 1)
                dve.wait_ge(S("rstdu_done"), n + 1)
                dve.wait_ge(S("ug_done"), 8 * n + 8)
                for c in range(4):
                    for t in range(TT):
                        cl = slice(c * CH, c * CH + CH)
                        stt(h[:, t, cl], u[:, t, cl], rstd_u[:, t:t + 1], h[:, t, cl], ALU.mult, ALU.add, "h_done")

            linear("ev_out", lambda c: gained("ev_out", c), lambda: (z_gate(1), features_lo("ev_out")))

            def hidden_product(n):
                dve.wait_ge(S("sg_done"), 2 * n + 2)
                for t in range(TT):
                    dve.scalar_tensor_tensor(hm[:, t], acc[2 + t][:], rstd[:, t:t + 1], sg[:, t],
                                             ALU.mult, ALU.mult).then_inc(S("hm_done"), 1)

            def hidden_lo(n, k):
                for b in range(2):
                    dve.wait_ge(S("hTh_done"), 2 * n + b + 1)
                    kk = slice(4 * k + 2 * b, 4 * k + 2 * b + 2) if isinstance(k, int) else bass.ds(4 * k + 2 * b, 2)
                    dve.tensor_tensor(hTl[:, kk], side[b][:].rearrange("p (a b) -> p a b", a=2),
                                      hTh[:, kk].bitcast(F32), ALU.subtract).then_inc(S("hTl_done"), 1)

            def hidden(name, lead):
                n0, blocks, g0 = FFB[name], CHUNKS[name] // 2, GRAN0[name]

                def block_of(i, first):
                    for m in range(2):
                        for j in range(8):
                            split(i * 16 + (g0 + 8 * m + j), j)
                            if m == 0 and j == 2:
                                if first:
                                    lead()
                                else:
                                    dve.wait_ge(S("used"), i * 16 + g0)
                                    hidden_product(i + (n0 - 1))
                            if not first and m == 0 and j == 6:
                                hidden_lo(i + (n0 - 1), i - 1)

                block_of(0, True)
                with dve.Fori(1, blocks) as i:
                    block_of(i, False)

            def down(name, up, evac):
                n, blocks = FFB[up] + CHUNKS[up] // 2 - 1, CHUNKS[up] // 2

                def lead():
                    dve.wait_ge(S("used"), GRAN0[name])
                    hidden_product(n)

                linear(name, evac, lead, lambda c, j: hidden_lo(n, blocks - 1) if c == 0 and j == 6 else None)

            def feed_forward(l, before):
                def lead():
                    gained(before, 3)
                    into_stream(before)
                    features_lo(f"up{l}a")
                    reciprocal_rms(NORM[f"up{l}a"])

                hidden(f"up{l}a", lead)
                down(f"dn{l}a", f"up{l}a", lambda c: None)
                hidden(f"up{l}b", lambda: None)
                down(f"dn{l}b", f"up{l}b", lambda c: gained(f"dn{l}b", c))

            feed_forward(0, "ev_out")

            def lead():
                gained("dn0b", 3)
                into_stream("dn0b")
                features_lo("od_in")
                reciprocal_rms(NORM["od_in"])

            linear("od_in", lambda c: None, lead)

            def attention():
                def scored(n):
                    dve.wait_ge(S("at_s"), n + 1)
                    if n == 0:
                        dve.wait_ge(S("masks_in"), 32)
                        dve.wait_ge(S("turned"), 36)
                    if n >= 2:
                        dve.wait_ge(S("at_turned"), n - 1)
                    m = pc[:, 0:384] if n < HEADS else pc[:, 384:768]
                    p = atw(n, 0)
                    stt(p, side[n % 2][:, 0:384], SCALE, m, ALU.mult, ALU.add, "at_scored")
                    dve.wait_ge(S("at_scored"), 3 * n + 1)
                    for t, cl in enumerate((slice(0, P), slice(P, 384))):
                        o = st[:, 24 + 2 * (n % 2) + t:25 + 2 * (n % 2) + t]
                        dve.tensor_reduce(o, p[:, cl], AX_X, ALU.max, negate=True).then_inc(S("at_scored"), 1)

                def recip(n):
                    dve.wait_ge(S("at_exp"), 2 * n + 2)
                    if n >= 2:
                        dve.wait_ge(S("at_out"), 2 * n - 2)
                    k = 2 * (n % 2)
                    dve.reciprocal(st[:, 40 + k:42 + k], st[:, 32 + k:34 + k]).then_inc(S("at_recip"), 1)

                for n in range(2 * HEADS + 1):
                    if n < 2 * HEADS:
                        scored(n)
                    if n >= 1:
                        recip(n - 1)

            linear("od_out", lambda c: gained("od_out", c), lambda: (attention(), features_lo("od_out")))
            feed_forward(1, "od_out")

            def lead():
                gained("dn1b", 3)
                into_stream("dn1b")
                features_lo("s_in")
                reciprocal_rms(NORM["s_in"])

            mult, add, sub = ALU.mult, ALU.add, ALU.subtract
            count = [0]

            def done(ins, name="par"):
                ins.then_inc(S(name), 1)
                count[0] += 1

            def own():
                dve.wait_ge(S("par"), count[0])

            def angles():
                dve.wait_ge(S("dt_done"), 1)
                done(dve.tensor_scalar(par(LAM), scol(0), -1e-4, None, ALU.min))
                done(dve.tensor_tensor(par(ANG), scol(1), par(DTP), mult))
                own()
                done(dve.tensor_tensor(par(LR), par(LAM), par(DTP), mult))

                def reduce_angle(s, c, x, k):
                    ops = [
                        lambda: dve.tensor_scalar(k, x, 1 / TWO_PI, MAGIC, mult, add),
                        lambda: dve.tensor_scalar(k, k, -MAGIC, None, add),
                        lambda: dve.scalar_tensor_tensor(s, k, -CW1, x, mult, add),
                        lambda: dve.scalar_tensor_tensor(s, k, -CW2, s, mult, add),
                        lambda: dve.tensor_scalar(k, s, math.pi / 2, -TWO_PI, ALU.is_gt, mult),
                        lambda: dve.scalar_tensor_tensor(c, s, math.pi / 2, k, add, add),
                        lambda: dve.tensor_scalar(c, c, PI_IN, -PI_IN, ALU.min, ALU.max),
                        lambda: dve.tensor_scalar(s, s, PI_IN, -PI_IN, ALU.min, ALU.max),
                    ]
                    for op in ops:
                        own()
                        done(op())

                reduce_angle(par(AS), par(AC), par(ANG), par(K_))
                own()
                done(dve.tensor_scalar(par(TA), par(AS), float(P), None, mult))
                reduce_angle(par(AS2), par(AC2), par(TA), par(K_))
                assert count[0] == ANGLES, count[0]
                own()
                done(dve.tensor_scalar(par(TURNS), par(AS), 1 / TWO_PI, None, mult))

            def factors():
                dve.wait_ge(S("mag_done"), 1)
                dve.wait_ge(S("sines"), 4)
                T, B = par(TA), par(TB)
                for op in (
                    lambda: dve.tensor_tensor(par(NRE), par(MAG), par(CS), mult),
                    lambda: dve.tensor_scalar(par(NRE), par(NRE), -1.0, None, add),
                    lambda: dve.tensor_tensor(par(NIM), par(MAG), par(SN), mult),
                    lambda: dve.tensor_tensor(T, par(LAM), par(LAM), mult),
                    lambda: dve.tensor_tensor(B, scol(1), scol(1), mult),
                    lambda: dve.tensor_tensor(T, T, B, add),
                    lambda: dve.reciprocal(par(DEN), T),
                    lambda: dve.tensor_tensor(T, par(NRE), par(LAM), mult),
                    lambda: dve.tensor_tensor(B, par(NIM), scol(1), mult),
                    lambda: dve.tensor_tensor(T, T, B, add),
                    lambda: dve.tensor_tensor(par(QRE), T, par(DEN), mult),
                    lambda: dve.tensor_tensor(T, par(NIM), par(LAM), mult),
                    lambda: dve.tensor_tensor(B, par(NRE), scol(1), mult),
                    lambda: dve.tensor_tensor(T, T, B, sub),
                    lambda: dve.tensor_tensor(par(QIM), T, par(DEN), mult),
                ):
                    own()
                    done(op())

            def widen_c():
                craw = at(PT + 1024, 2, 8, 64)
                dve.wait_ge(S("c_in"), 32)
                dve.wait_ge(S("masks_in"), 48)
                for n in range(2):
                    w = at(SGS, 2, 1024)[:, n].rearrange("p (a g n) -> p a g n", a=8, g=2)
                    for g in range(2):
                        c0 = 4 * TOK + P + g
                        ts(w[:, :, g], craw[:, n], pc[:, c0:c0 + 1], None, mult, ALU.bypass, "c_wide")

            def widen_b(n):
                braw, wide = at(PT, 2, PAIRS, 16), at(SGP, 2, 1024)
                t1, t2 = (spare[:, CH * k:CH * k + CH].rearrange("p (a c) -> p a c", a=PAIRS) for k in range(2))
                q = lambda k: par(k).unsqueeze(2).to_broadcast([P, PAIRS, 16])
                dve.wait_ge(S("b_in"), 32)
                own()
                if n == 0:
                    done(dve.memset(wide, 0.0))
                else:
                    dve.wait_ge(S("b_wide"), 2)
                done(dve.tensor_tensor(t1, braw[:, n], q(QRE), mult))
                done(dve.tensor_tensor(t2, braw[:, 1 - n], q(QIM), mult))
                own()
                w = wide[:, n].rearrange("p (a g c) -> p a g c", a=PAIRS, g=2)
                for g in range(2):
                    r = slice(64 * g, 64 * g + 64)
                    tt(w[r, :, g], t1[r], t2[r], add if n else sub, "b_wide")

            def magnitude(n):
                return par(MAG)[:, n:n + 1].to_broadcast([P, P])

            def rotate(n):
                ct, r = n // 4, n % 4
                t1, t2 = (spare[:, CH * k:CH * k + CH].rearrange("p (a b) -> p a b", a=4) for k in range(2))
                b = side[n % 3][:].rearrange("p (a b) -> p a b", a=4)
                c = tab(ct)[:, 0, r:r + 1].to_broadcast([P, 4, P])
                s2 = tab(ct)[:, 1, r:r + 1].to_broadcast([P, 2, P])
                if r == 0:
                    dve.wait_ge(S("tab_done"), 2 * ct + 2)
                dve.wait_ge(S("bu_ready"), n + 1)
                if n:
                    dve.wait_ge(S("rotated"), 5 * n)
                else:
                    dve.wait_ge(S("b_wide"), 4)
                    dve.wait_ge(S("h_done"), 8 * 4)
                tt(t1, b, c, mult, "rotated")
                tt(t2[:, 0:2], b[:, 2:4], s2, mult, "rotated")
                tt(t2[:, 2:4], b[:, 0:2], s2, mult, "rotated")
                dve.wait_ge(S("rotated"), 5 * n + 3)
                if ct and r == 0:
                    dve.wait_ge(S("unrotated"), 8 * ct)
                o = states[:, r].rearrange("p (a b) -> p a b", a=4)
                tt(o[:, 0:2], t1[:, 0:2], t2[:, 0:2], add, "rotated")
                tt(o[:, 2:4], t1[:, 2:4], t2[:, 2:4], sub, "rotated")

            def scan_tiles(ct):
                dve.wait_ge(S("rotated"), 5 * 4 * (ct + 1))

                def scan(t, start):
                    for r in range(4):
                        for m in range(2):
                            x = states[:, r, 256 * m + P * t:256 * m + P * t + P]
                            dve.tensor_tensor_scan(x, magnitude(4 * ct + r), x, start(r, m), mult, add)\
                                .then_inc(S("scanned"), 1)

                scan(0, lambda r, m: 0.0)
                dve.wait_ge(S("scanned"), 16 * ct + 8)
                er, ei = states[:, :, P - 1], states[:, :, 256 + P - 1]
                c4, s4 = par(C128)[:, 4 * ct:4 * ct + 4], par(S128)[:, 4 * ct:4 * ct + 4]
                w = lambda k: st[:, 56 + 4 * k:60 + 4 * k]
                tt(w(0), er, c4, mult, "turned_on")
                tt(w(1), ei, s4, mult, "turned_on")
                tt(w(2), ei, c4, mult, "turned_on")
                tt(w(3), er, s4, mult, "turned_on")
                dve.wait_ge(S("turned_on"), 6 * ct + 4)
                tt(w(4), w(0), w(1), sub, "turned_on")
                tt(w(5), w(2), w(3), add, "turned_on")
                dve.wait_ge(S("turned_on"), 6 * ct + 6)
                scan(1, lambda r, m: st[:, 72 + 4 * m + r:73 + 4 * m + r])

            def unrotate(n):
                ct, r = n // 4, n % 4
                if r == 0:
                    dve.wait_ge(S("scanned"), 16 * ct + 16)
                if n >= 2:
                    dve.wait_ge(S("y_part"), n - 1)
                x = states[:, r].rearrange("p (a b) -> p a b", a=4)
                for m in range(2):
                    f = tab(ct)[:, m, r:r + 1].to_broadcast([P, 4, P])
                    tt(products(n)[:, m].rearrange("p (a b) -> p a b", a=4), x, f, mult, "unrotated")

            def skip(ct):
                uT = at(UT, 8, TOK)[:, ct]
                dve.wait_ge(S("y_part"), 4 * ct + 4)
                stt(uT, uT, dskip_col(ct), side[3][:, 0:TOK], mult, add, "y_done")

            def s_aside(c, j):
                at_ = 8 * c + j
                if at_ == 7:
                    srow = at(SROW, 4, P)
                    dve.wait_ge(S("srow_in"), 48)
                    dve.tensor_copy(srow[0:PAIRS, 2].rearrange("p (a b) -> p a b", a=2),
                                    srow[0:PAIRS, 3, 0:2].unsqueeze(2).to_broadcast([PAIRS, 2, 64]))\
                        .then_inc(S("srow_ready"), 1)
                if at_ == 10:
                    widen_c()
                if at_ == 12:
                    angles()
                if at_ == 16:
                    factors()
                if at_ == 18:
                    widen_b(0)
                if at_ == 20:
                    widen_b(1)
                for ct in range(8):
                    if at_ == SSM_AT[ct] + 2:
                        for r in range(3):
                            rotate(4 * ct + r)
                    if at_ == SSM_AT[ct] + 3:
                        rotate(4 * ct + 3)
                        scan_tiles(ct)
                        if ct:
                            skip(ct - 1)
                    if at_ == SSM_AT[ct] + 4:
                        unrotate(4 * ct)
                        unrotate(4 * ct + 1)
                    if at_ == SSM_AT[ct] + 6:
                        unrotate(4 * ct + 2)
                        unrotate(4 * ct + 3)

            linear("s_in", lambda c: None, lead, s_aside)

            pool_steps = [0]

            def pool_group(g):
                def step(o, a, b, op):
                    dve.tensor_tensor(o, a, b, op).then_inc(S("pool_step"), 1)
                    pool_steps[0] += 1
                    dve.wait_ge(S("pool_step"), pool_steps[0])

                if g == 0:
                    dve.wait_ge(S("turn_done"), 2 * TURN["s_in", 3] + 2 - 12)
                    dve.wait_ge(S("y_part"), 32)
                v = at(PT, 8, TOK)[:, 2 * g:2 * g + 2]
                src = v
                if g:
                    dve.wait_ge(S("pooled"), g)
                for k in range(g + 1):
                    o = at(POOLT + CH * (k % 2), 2, TOK)
                    step(o[:, :, 1 << k:], src[:, :, 1 << k:], src[:, :, 0:TOK - (1 << k)], ALU.add)
                    step(o[:, :, 0:1 << k], src[:, :, 0:1 << k], src[:, :, 0:1 << k], ALU.max)
                    src = o
                inv = pc[:, g * TOK:(g + 1) * TOK].unsqueeze(1).to_broadcast([P, 2, TOK])
                step(src, src, inv, ALU.mult)
                tt(at(POOLED, 8, TOK)[:, 2 * g:2 * g + 2], src, v, ALU.subtract, "pooled")

            def pool_gate(g):
                dve.wait_ge(S("pool_mixed"), g + 1)
                dve.wait_ge(S("projected"), 2 * (PROJ0["s_in"] + 6))
                cl = slice(g * 256, g * 256 + 256)
                tt(u[:, :, cl], side[g][:].rearrange("p (t n) -> p t n", t=TT),
                   at(SGP, TT, 1024)[:, :, cl], ALU.mult, "pool_out")

            def low(ct):
                dve.wait_ge(S("gh_done"), ct + 1)
                tt(xl[:, ct], at(UT, 8, TOK)[:, ct], xh[:, ct].bitcast(F32), ALU.subtract, "gl_done")

            def glu_out(c):
                if c % 2:
                    m = c // 2
                    for t in range(TT):
                        dve.wait_ge(S("glu_sig"), 2 * m + t + 1)
                        x = at(UT, TT, CH)[:, t]
                        if m:
                            dve.wait_ge(S("mixed"), 4 + 2 * m)
                        else:
                            dve.wait_ge(S("gl_done"), 8)
                        tt(x, acc[t][:], spare[:, CH * t:CH * t + CH], ALU.mult, "glu_out")
                        dve.wait_ge(S("glu_out"), 2 * m + t + 1)
                        tt(u[:, t, 1024 + CH * m:1024 + CH * m + CH], x,
                           at(SGS, TT, 1024)[:, t, CH * m:CH * m + CH], ALU.mult, "mixed")

            def lead():
                for ct in range(8):
                    if ct == 2:
                        skip(7)
                    low(ct)

            def glu_aside(c, j):
                at_ = (c, j)
                for k, where in enumerate(POOL_AT):
                    if at_ == (where[0] - (where[1] < 1), (where[1] - 1) % 4):
                        pool_group(k)
                    if at_ == (where[0], where[1] + 1):
                        pool_gate(k)

            linear("glu", glu_out, lead, glu_aside)

            def s_out(c):
                chunk_done("s_out", c)
                pair = (CHUNK0["s_out"] + c) % 2
                for t in range(TT):
                    x = h[:, t, CH * c:CH * c + CH]
                    tt(x, acc[2 * pair + t][:], x, ALU.add, "h_done")

            linear("s_out", s_out, lambda: (glu_out(3), features_lo("s_out")))

            for c in range(4):
                split(gran("ple", c))
                if c == 2:
                    s_out(3)
                    for t in range(TT):
                        dve.wait_ge(S("ph_done"), 4)
                        tt(hTl[:, 0:2, t * P:t * P + P],
                           side[t][:, 0:256].rearrange("p (k n) -> p k n", k=2),
                           hTh[:, 0:2, t * P:t * P + P].bitcast(F32), ALU.subtract, "pl_done")
                    features_lo("pg")

            def gate_out(c):
                for t in range(TT):
                    n = 2 * c + t
                    dve.wait_ge(S("pg_sig"), n + 1)
                    cl = slice(CH * c, CH * c + CH)
                    x = at(13312, TT, CH)[:, t]
                    dve.wait_ge(S("ple_out"), 8)
                    tt(x, sg[:, t], u[:, t, cl], ALU.mult, "gated")
                    dve.wait_ge(S("gated"), 2 * n + 1)
                    tt(h[:, t, cl], h[:, t, cl], x, ALU.add, "gated")

            linear("pg", gate_out, lambda: None)
            gate_out(3)
            dve.wait_ge(S("grow_in"), 80)
            reciprocal_rms(5)
            dve.wait_ge(S("rstd_done"), 6)
            for c in range(4):
                for t in range(TT):
                    cl = slice(CH * c, CH * c + CH)
                    stt(h[:, t, cl], h[:, t, cl], rstd[:, t:t + 1], grow[:, cl], ALU.mult, ALU.mult, "final")


_INS = ["x", "mix_norm_pre", "mix_norm_post", "ffn_norm_pre", "ffn_norm_post", "ev_w_in", "ev_conv_w", "ev_a_log",
        "ev_dt_bias", "ev_onorm", "ev_w_out", "od_w_in", "od_w_out", "ffn_w_gate", "ffn_w_up", "ffn_w_down", "p_2",
        "norm_gain_2", "w_in_2", "w_pool_2", "pool_scale_2", "a_re_2", "a_im_2", "log_dt_2", "b_re_2", "b_im_2",
        "c_re_2", "c_im_2", "d_skip_2", "w_glu_2", "w_out_2", "w_ple_2", "w_ple_gate_2", "final_gain_2"]


def kernel(**inputs):
    import concourse.bacc as _bacc
    from concourse.bass_utils import run_bass_kernel_spmd as _run

    nc = _bacc.Bacc("TRN2", target_bir_lowering=False, num_devices=1)
    arrays = {n: np.ascontiguousarray(inputs[n]) for n in _INS}
    arrays.update(shape_constants())
    A = {n: nc.dram_tensor(f"in_{n}", a.shape, F32, kind="ExternalInput").ap() for n, a in arrays.items()}
    out = nc.dram_tensor("out", (1, TOK, DM), F32, kind="ExternalOutput").ap()
    build(nc, A, out)
    r = _run(nc, [{f"in_{n}": a for n, a in arrays.items()}], core_ids=[0])
    return r.results[0]["out"]
```

```python
from contextlib import ExitStack
import math

import numpy as np

import concourse.bass as bass
from concourse import mybir

ALU = mybir.AluOpType
ACT = mybir.ActivationFunctionType
AX_X = mybir.AxisListType.X
F32 = mybir.dt.float32
F32R = mybir.dt.float32r

P = 128
TOK = 256
TT = TOK // P
DM = 2048
KM = DM // P
DFF = 5632
FF_IT = DFF // 512
FF_A, FF_B = 6, 5
HEADS = 8
HD = 128
EPS = 1e-6
SCALE = HD ** -0.5
CH = 512
NEG = -1e30
AR = 15104
RING = 4
PAIRS = 32
TWO_PI = 2 * math.pi
CW1 = 6.28125
CW2 = TWO_PI - CW1
PI_IN = 3.1415925
HALF_IN = 0.49999997
MAGIC = 1.5 * 2 ** 23

LINEARS = [
    ("ev_gdn", 6, 16), ("ev_sb", 6, 16), ("ev_z", 2, 16), ("ev_out", 4, 16),
    ("up0a", 2 * FF_A, 16), ("dn0a", 4, 4 * FF_A), ("up0b", 2 * FF_B, 16), ("dn0b", 4, 4 * FF_B),
    ("od_in", 12, 16), ("od_out", 4, 16),
    ("up1a", 2 * FF_A, 16), ("dn1a", 4, 4 * FF_A), ("up1b", 2 * FF_B, 16), ("dn1b", 4, 4 * FF_B),
    ("s_in", 8, 16), ("glu", 4, 8), ("s_out", 4, 16), ("ple", 4, 2), ("pg", 4, 16),
]
PROJ0 = {"ev_gdn": 0, "ev_sb": 6, "ev_z": 12, "od_in": 14, "s_in": 26}
TURN = {("ev_gdn", c): c for c in range(6)}
TURN |= {("ev_sb", c): 6 + c for c in range(4)}
TURN |= {("od_in", c): 10 + n for n, c in enumerate((0, 1, 2, 3, 6, 7, 8, 9))}
TURN |= {("s_in", c): 18 + c for c in range(4)}
TOF = {n: k for k, n in enumerate(("ev_gdn", "ev_out", "up0a", "od_in", "od_out", "up1a", "s_in", "s_out", "pg"))}
FFB = {"up0a": 0, "up0b": FF_A, "up1a": FF_IT, "up1b": FF_IT + FF_A}
POST = {"ev_out": 0, "dn0b": 1, "od_out": 2, "dn1b": 3}
PJ_EVEN, PJ_ODD, PJ_SSM = 6144, 12288, 8192
CONV, UNIT = 7168, 6144
SBW, ATW = 7168, 13312
POOLED, POOLT, WPOOL = 9216, 11264, 12288
UT, PT, SGP, SGS, BT, CT, SPAR, SCOL = 0, 2048, 4096, 6144, 9216, 11264, 14336, 14848
SROW = SPAR
SSM_AT = [22 + 5 * ct for ct in range(8)]
POOL_AT = [7, 9, 11, 13]
LEAD = 7
STATS = 5
CHUNKS = {n: c for n, c, _ in LINEARS}
KTS = {n: k for n, _, k in LINEARS}
GRAN0, CHUNK0 = {}, {}
_g = _c = 0
for _n, _nc, _k in LINEARS:
    GRAN0[_n], CHUNK0[_n] = _g, _c
    _g += _nc * _k // 2
    _c += _nc


def gran(name, c, j=0):
    return GRAN0[name] + c * (KTS[name] // 2) + j


def shape_constants():
    i = np.arange(P)
    row, col = i[:, None], i[None, :]
    common = [np.eye(P), (row <= col), (row >= col), np.ones((P, P))]
    neg_strict = np.where(col < row, 0.0, NEG)
    neg_incl_t = np.where(col >= row, 0.0, NEG)
    level = [((row >> (l + 1)) == (col >> (l + 1))) & ((row >> l) & 1 == 1) & ((col >> l) & 1 == 0)
             for l in range(7)]
    key = (i[:, None, None] + P * np.arange(2)[None, :, None])
    qry = np.arange(TOK)[None, None, :]
    past = (key < qry).reshape(P, 2 * TOK)
    even = [neg_strict, neg_incl_t, level[0]] + [m.T for m in level] + [past, np.where(past, 0.0, NEG)]
    q = np.concatenate([np.repeat(i[:, None], P, 1), np.repeat(i[:, None] + P, TOK, 1)], 1)
    k = np.concatenate([np.repeat(i[None], P, 0), np.repeat(np.arange(TOK)[None], P, 0)], 1)
    causal = np.where(k <= q, 0.0, NEG)
    seen = ((q - k <= 128).astype(int) + ((q - k) % 4 == 0) + ((q - k) % 16 == 0)) * (k <= q)
    dil = np.where(seen > 0, np.log(np.maximum(seen, 1)), NEG)
    odd = [causal, dil]
    t = np.arange(TOK)
    inv = [np.repeat((1.0 / np.minimum(t + 1, w))[None], P, 0) for w in (2, 4, 8, 16)]
    parity = np.stack([(i // 16) % 2 == 0, (i // 16) % 2 == 1], 1)
    second = inv + [np.repeat(i[None], P, 0), parity]
    cat = lambda xs: np.ascontiguousarray(np.concatenate([x.astype(np.float32) for x in xs], 1))
    return {"c_common": cat(common), "c_even": cat(even), "c_odd": cat(odd), "c_second": cat(second)}


def build(nc, A, out):
    ctx = ExitStack()
    with ctx:
        def sb(name, shape, dt=F32, scope=ctx):
            return scope.enter_context(nc.sbuf_tensor(name, [P] + shape, dt))

        raw = sb("raw", [RING, 4, CH])
        whi = sb("whi", [RING, 2, CH], F32R)
        wlo = sb("wlo", [RING, 2, CH], F32R)
        h = sb("h", [TT, DM])
        u = sb("u", [TT, DM])
        cc = sb("cc", [4 * P])
        pc = sb("pc", [2304])
        with nc.sbuf_tensor("before_wab", [P, 864], F32), nc.sbuf_tensor("wab_h", [P, KM, 16], F32R) as wab_h, \
                nc.sbuf_tensor("wab_l", [P, KM, 16], F32R) as wab_l:
            pass
        grow = sb("grow", [DM])
        cols = sb("cols", [2 * P])
        st = sb("st", [192])
        ident, tri_u, tri_l, ones = (cc[:, k * P:(k + 1) * P] for k in range(4))
        xh = sb("xh", [KM, TOK], F32R)
        xl = sb("xl", [KM, TOK], F32R)
        with nc.sbuf_tensor("hTh", [P, 4 * FF_A, TOK], F32R) as hTh, \
                nc.sbuf_tensor("hTl", [P, 4 * FF_A, TOK], F32R) as hTl:
            pass
        ar = sb("ar", [AR])

        def at(o, *shape):
            n = math.prod(shape)
            assert o + n <= AR, (o, n)
            v = ar[:, o:o + n]
            if len(shape) == 2:
                v = v.rearrange("p (a b) -> p a b", a=shape[0])
            if len(shape) == 3:
                v = v.rearrange("p (a b c) -> p a b c", a=shape[0], b=shape[1])
            return v

        sg, hm = at(12288, TT, CH), at(12288 + 1024, TT, CH)
        acc = [ctx.enter_context(nc.psum_tensor(f"acc{i}", [P, CH], F32)) for i in range(4)]
        side = [ctx.enter_context(nc.psum_tensor(f"side{i}", [P, CH], F32)) for i in range(4)]

        ss = st[:, 0:8]
        ssum, rms_u, rstd_u = st[:, 8:10], st[:, 10:12], st[:, 12:14]
        ssh, rms_h, rstd = st[:, 14:16], st[:, 16:18], st[:, 18:20]

        def conv_col(tap, blk):
            return cols[:, tap * 24 + blk:tap * 24 + blk + 1]

        def gain_col(n, k):
            return cols[:, P + n * KM + k:P + n * KM + k + 1]

        def dskip_col(k):
            return cols[:, P + 80 + k:P + 81 + k]

        def pool_col(k):
            return cols[:, P + 88 + k:P + 89 + k]

        sems = {}

        def S(name):
            if name not in sems:
                sems[name] = ctx.enter_context(nc.semaphore(name))
            return sems[name]

        block = ctx.enter_context(nc.Block())

        def kview(w):
            return w.rearrange("(k p) n -> p k n", p=P)

        ev_in, od_in, s_in = kview(A["ev_w_in"][0]), kview(A["od_w_in"][0]), kview(A["w_in_2"][0])
        WEIGHTS = {
            "ev_gdn": (ev_in, [3072 + CH * c for c in range(6)]), "ev_z": (ev_in, [6144, 6656]),
            "ev_sb": (ev_in, [CH * c for c in range(6)]), "ev_out": (kview(A["ev_w_out"][0]), None),
            "od_in": (od_in, None), "od_out": (kview(A["od_w_out"][0]), None),
            "s_in": (s_in, [2048, 2560, 0, 512, 1024, 1536, 3072, 3584]),
            "glu": (kview(A["w_glu_2"][0]), [0, 1024, 512, 1536]),
            "s_out": (kview(A["w_out_2"][0]), None), "pg": (kview(A["w_ple_gate_2"][0]), None),
        }
        for l in range(2):
            down = kview(A["ffn_w_down"][l])
            WEIGHTS[f"dn{l}a"] = (down[:, 0:4 * FF_A, :], None)
            WEIGHTS[f"dn{l}b"] = (down[:, 4 * FF_A:, :], None)

        @block.sync
        def _(sp):
            def slot(n, src, ring=None):
                ring = n % RING if ring is None else ring
                if not isinstance(n, int) or n >= RING:
                    sp.wait_ge(S("lo_done"), 2 * n - 2 * RING + 2)
                sp.dma_start(raw[:, ring], src).then_inc(S(f"landed{ring}"), 16)

            sp.dma_start(cc[:], A["c_common"]).then_inc(S("common_in"), 16)
            rows = at(0, 2, P)
            sp.dma_start(rows[0:96, 0], A["ev_conv_w"][0].rearrange("t (b p) -> (t b) p", p=P))\
                .then_inc(S("rows_in"), 16)
            for n, g in ((0, A["mix_norm_pre"]), (2, A["ffn_norm_pre"]), (4, A["norm_gain_2"])):
                g = g.rearrange("l (k p) -> (l k) p", p=P)
                sp.dma_start(rows[KM * n:KM * n + g.shape[0], 1], g).then_inc(S("rows_in"), 16)
            sp.dma_start(rows[80:88, 1], A["d_skip_2"][0].rearrange("(k p) -> k p", p=P))\
                .then_inc(S("rows_in"), 16)
            sp.dma_start(rows[88:96, 1], A["pool_scale_2"][0].rearrange("(k p) -> k p", p=P))\
                .then_inc(S("rows_in"), 16)
            for c in range(4):
                sp.dma_start(h[:, :, CH * c:CH * c + CH], A["x"][0][:, CH * c:CH * c + CH].rearrange("(t p) n -> p t n", p=P))\
                    .then_inc(S(f"x_in{c}"), 16)

            for name, nch, nk in LINEARS:
                n0 = GRAN0[name] // 2
                if name[:2] == "up":
                    l, first = int(name[2]), 0 if name[3] == "a" else FF_A
                    g, w = kview(A["ffn_w_gate"][l]), kview(A["ffn_w_up"][l])
                    with sp.Fori(0, nch // 2) as i:
                        for m in range(8):
                            src = (g if m < 4 else w)[:, 4 * (m % 4):4 * (m % 4) + 4,
                                                      bass.ds(first * CH + i * CH, CH)]
                            slot(n0 + m + 8 * i, src, m % RING)
                elif name == "ple":
                    w = A["w_ple_2"][0].rearrange("(k p) (c n) -> p c k n", p=P, n=CH)
                    for m in range(2):
                        for c in range(2):
                            if c == 0:
                                sp.wait_ge(S("lo_done"), 2 * (n0 + m) - 2 * RING + 2)
                            sp.dma_start(raw[:, (n0 + m) % RING, 2 * c:2 * c + 2], w[:, 2 * m + c])\
                              .then_inc(S("ple_landed"), 16)
                else:
                    w, at_col = WEIGHTS[name]
                    per = nk // 4
                    for c in range(nch):
                        o = at_col[c] if at_col else c * CH
                        for m in range(per):
                            slot(n0 + c * per + m, w[:, 4 * m:4 * m + 4, o:o + CH])

        def raw_granule(place):
            return raw[:, place // 2, 2 * (place % 2):2 * (place % 2) + 2]

        def landed(eng, g):
            n = g // 2
            if GRAN0["ple"] <= g < GRAN0["pg"]:
                eng.wait_ge(S("ple_landed"), 64)
            else:
                before = sum(1 for k in range(GRAN0["ple"] // 2, GRAN0["pg"] // 2) if k < n and k % RING == n % RING)
                eng.wait_ge(S(f"landed{n % RING}"), 16 * (n // RING + 1 - before))

        def tab(ct):
            return grow[:, 1024 * (ct % 2):1024 * (ct % 2) + 1024].rearrange("p (m r t) -> p m r t", m=2, r=4)

        def products(n):
            return u[:, 1, 1024 * (n % 2):1024 * (n % 2) + 1024].rearrange("p (m x) -> p m x", m=2)

        states = u[:, 0].rearrange("p (r x) -> p r x", r=4)
        spare = pc[:, 1154:2178]

        def par(k):
            o = SPAR + PAIRS * k if k < 16 else SCOL + 96 + PAIRS * (k - 16)
            return at(o, PAIRS)

        (LAM, LR, ANG, AS, AC, MAG, SN, CS, AS2, AC2, S128, C128, K_, NRE, NIM, DEN, QRE, QIM, DTP, TA, TB) = range(21)
        TURNS = K_
        ANGLES = 20

        def scol(k):
            return at(SCOL + PAIRS * k, PAIRS)

        @block.gpsimd
        def _(pool):
            pool.wait_ge(S("x_in3"), 16)
            pool.dma_start(grow[:, 0:8], A["ev_dt_bias"].to_broadcast([P, 8])).then_inc(S("gdn_rows_in"), 16)
            pool.dma_start(grow[:, 8:16], A["ev_a_log"].to_broadcast([P, 8])).then_inc(S("gdn_rows_in"), 16)
            pool.dma_start(grow[:, 128:256], A["ev_onorm"].to_broadcast([P, P])).then_inc(S("gdn_rows_in"), 16)
            pool.dma_start(grow[:, 256:512].rearrange("p (k n) -> p k n", n=16), ev_in[:, :, 7168:7184])\
                .then_inc(S("gdn_rows_in"), 16)

            pool.dma_start(pc[:], A["c_even"]).then_inc(S("masks_in"), 16)

            def gain_row(n, row, wait, count):
                pool.wait_ge(S(wait), count)
                pool.dma_start(grow[:], row.unsqueeze(0).to_broadcast([P, DM])).then_inc(S("grow_in"), 16)

            pool.wait_ge(S("turned"), 20)
            gain_row(0, A["mix_norm_post"][0], "gdn_out", 20)
            pool.wait_ge(S("sb_s"), HEADS)
            pool.dma_start(h[:], A["x"][0].rearrange("(t p) n -> p t n", p=P)).then_inc(S("x_back"), 16)
            pool.wait_ge(S("sb_scored"), 3 * HEADS)
            pool.dma_start(pc[:, 0:768], A["c_odd"]).then_inc(S("masks_in"), 16)
            gain_row(1, A["ffn_norm_post"][0], "ug_done", 8)
            gain_row(2, A["mix_norm_post"][1], "ug_done", 16)
            gain_row(3, A["ffn_norm_post"][1], "ug_done", 24)
            pool.wait_ge(S("at_scored"), 3 * 16)
            pool.dma_start(pc[:, 0:1154], A["c_second"]).then_inc(S("masks_in"), 16)
            pool.wait_ge(S("sq_done"), 32)
            pool.wait_ge(S("used"), GRAN0["s_in"])
            ssm_rows = at(SROW, 4, P)
            for n, w in enumerate((A["a_re_2"][0], A["a_im_2"][0])):
                pool.dma_start(ssm_rows[0:PAIRS, n], w.rearrange("(a b) n -> a (b n)", b=2)).then_inc(S("srow_in"), 16)
            pool.dma_start(ssm_rows[0:PAIRS, 3, 0:2], A["log_dt_2"][0].rearrange("(a b) -> a b", b=2))\
                .then_inc(S("srow_in"), 16)
            braw, craw = at(PT, 2, PAIRS, 16), at(PT + 1024, 2, 8, 64)
            for n, w in enumerate((A["c_re_2"][0], A["c_im_2"][0])):
                pool.dma_start(craw[:, n], w.rearrange("(a g) c n -> (g c) a n", g=8)).then_inc(S("c_in"), 16)
            for n, w in enumerate((A["b_re_2"][0], A["b_im_2"][0])):
                pool.dma_start(braw[:, n], w.rearrange("(a b) n c -> (b n) a c", b=2)).then_inc(S("b_in"), 16)
            iota = pc[:, 4 * TOK:4 * TOK + P].unsqueeze(1).to_broadcast([P, 4, P])
            pool.wait_ge(S("par"), ANGLES + 1)
            pool.wait_ge(S("masks_in"), 48)
            pool.wait_ge(S("ug_done"), 32)
            for ct in range(8):
                nearest, angle = tab(ct)[:, 0], tab(ct)[:, 1]
                if ct >= 2:
                    pool.wait_ge(S("unrotated"), 8 * (ct - 1))
                f = par(TURNS)[:, 4 * ct:4 * ct + 4].unsqueeze(2).to_broadcast([P, 4, P])
                pool.tensor_tensor(angle, iota, f, ALU.mult).then_inc(S("tab_arg"), 1)
                pool.wait_ge(S("tab_arg"), 5 * ct + 1)
                pool.tensor_scalar(nearest, angle, MAGIC, None, ALU.add, ALU.bypass).then_inc(S("tab_arg"), 1)
                pool.wait_ge(S("tab_arg"), 5 * ct + 2)
                pool.tensor_scalar(nearest, nearest, -MAGIC, None, ALU.add, ALU.bypass).then_inc(S("tab_arg"), 1)
                pool.wait_ge(S("tab_arg"), 5 * ct + 3)
                pool.tensor_tensor(angle, angle, nearest, ALU.subtract).then_inc(S("tab_arg"), 1)
                pool.wait_ge(S("tab_arg"), 5 * ct + 4)
                pool.tensor_scalar(angle, angle, HALF_IN, -HALF_IN, ALU.min, ALU.max).then_inc(S("tab_arg"), 1)
            pool.wait_ge(S("y_part"), 32)
            pool.dma_start(at(WPOOL, 8, 256), A["w_pool_2"][0].rearrange("g (k p) d -> p (g k) d", p=P))\
                .then_inc(S("wpool_in"), 16)
            gain_row(4, A["final_gain_2"], "unrotated", 64)
            pool.wait_ge(S("pool_mixed"), 4)
            pool.dma_start(at(13312, TT, 256), A["p_2"][0, 0].rearrange("(t p) n -> p t n", p=P))\
                .then_inc(S("p_in"), 16)

        dtb, alog, onorm = grow[:, 0:8], grow[:, 8:16], grow[:, 128:256]
        wab = grow[:, 256:512].rearrange("p (k n) -> p k n", n=16)
        ab_rows = grow[:, 1376:1376 + TOK]
        ab = grow[:, 512:544].rearrange("p (t n) -> p t n", t=TT)

        def g16(k):
            return grow[:, 544 + 16 * k:560 + 16 * k]

        def g16t(k):
            return g16(k).rearrange("p (t n) -> p t n", t=TT)

        AV, T1_, T2_, T3_, SPL, GL, BE, GC, EG, NBEG, KA, EKA, OSS, ORR = range(14)
        rn = grow[:, 800:832]
        rn2 = grow[:, 832:864]

        qkv = at(0, TT, 3072)

        def unit(t, k):
            o = UNIT + (8 * t + k) * CH
            return ar[:, o:o + CH].rearrange("p (h n) -> p h n", h=4)

        KT, QT, M_, A_, LT_, MT_, T_, LM_ = range(8)

        def lower(n):
            return 10 * (n // 2) + 4 * (n % 2) + 4

        def inner(n):
            return 10 * (n // 2) + 9 + n % 2

        def mask(k, n=1):
            return pc[:, k * P:(k + n) * P]

        def heads4(m):
            return m.unsqueeze(1).to_broadcast([P, 4, P])

        def pj_at(name):
            if name == "ev_sb":
                return grow[:, 864:1888].rearrange("p (t n) -> p t n", t=TT)
            return at({"e": PJ_EVEN, "o": PJ_ODD, "s": PJ_SSM}[name[0]], TT, CH)

        def turned_to(name, c, j):
            if name == "ev_sb":
                o = 1024 * (c % 2) + 512 * j
                return h[:, c // 2, o:o + CH].rearrange("p (a b) -> p a b", a=2)
            if name == "od_in":
                return at(6144 * (c // 6) + 2048 * (c % 6 // 2) + 1024 * (c % 2) + 512 * j, 2, TOK)
            return at(2048 * (c // 2) + 1024 * (c % 2) + 512 * j, 2, TOK)

        def sb_in():
            return (h[:, 0].rearrange("p (a b) -> p a b", a=HEADS), h[:, 1].rearrange("p (a b) -> p a b", a=HEADS),
                    u[:, :, 0:1024])

        def att_in(name, layer_half=0):
            o = 6144 * layer_half
            return at(o, HEADS, TOK), at(o + 2048, HEADS, TOK), at(o + 4096, TT, 1024)

        def sbw(hd, k):
            return at(SBW + (3 * (hd % 2) + k) * CH, CH)

        def atw(hd, k):
            return at(ATW + (2 * (hd % 2) + k) * 384, 384)

        @block.tensor
        def _(pe):
            last_reader = {}

            def claim(bank, freed_by, count):
                if bank.name in last_reader:
                    pe.wait_ge(*last_reader[bank.name])
                last_reader[bank.name] = (S(freed_by), count)
                return bank

            def granule(g, ring, pair, lhs_h, lhs_l, k0, first, last):
                pe.wait_ge(S("lo_done"), g + 1)
                for j in range(2):
                    for t in range(TT):
                        tok = slice(t * P, t * P + P)
                        for n, (x, w) in enumerate(((lhs_h, whi), (lhs_h, wlo), (lhs_l, whi))):
                            mm = pe.matmul(acc[2 * pair + t][:], x[:, k0 + j, tok], w[:, ring, j],
                                           start=first and j == 0 and n == 0,
                                           stop=last and j == 1 and n == 2)
                mm.then_inc(S("used"), 1)

            def linear(*args):
                for _ in granules(*args):
                    pass

            def granules(name, lhs_h, lhs_l, freed, aside=None, first_use=None):
                per = KTS[name] // 2
                for c in range(CHUNKS[name]):
                    pair = (CHUNK0[name] + c) % 2
                    for j in range(per):
                        if aside:
                            aside(c, j)
                        if first_use:
                            first_use(c, j)
                        if j == 0:
                            for t in range(TT):
                                claim(acc[2 * pair + t], *freed(c, t))
                        g = gran(name, c, j)
                        granule(g, g % RING, pair, lhs_h, lhs_l, 2 * j, j == 0, j == per - 1)
                        yield

            def projected(name):
                return lambda c, t: ("projected", 2 * (PROJ0[name] + c) + t + 1)

            def to_features(name, src, rounds=range(8)):
                base = 8 * TOF[name]
                for r in rounds:
                    if name in ("ev_gdn",):
                        if r % 2 == 0:
                            pe.wait_ge(S(f"x_in{r // 2}"), 16)
                    elif name == "ev_out":
                        if r < 4:
                            pe.wait_ge(S("sb_out"), 2 * r + 2)
                        else:
                            pe.wait_ge(S("mixed"), 2 * (r // 2 - 1))
                    elif name == "s_out":
                        if r < 4:
                            pe.wait_ge(S("pool_out"), r + 1)
                        else:
                            pe.wait_ge(S("mixed"), 4 + 2 * (r // 2 - 1))
                    elif name == "od_out":
                        pe.wait_ge(S("at_out"), 4 * r + 4)
                    else:
                        n = ("up0a", "od_in", "up1a", "s_in", "pg").index(name)
                        pe.wait_ge(S("h_done"), 8 * n + 2 * (r // 2) + 2)
                    b = claim(side[r % 4], "xl_done", 2 * (base + r) + 2)
                    for j in range(2):
                        for t in range(TT):
                            k = 2 * r + j
                            mm = pe.transpose(b[:, j * TOK + t * P:j * TOK + t * P + P],
                                              src[:, t, k * P:k * P + P], ident)
                    mm.then_inc(S("tof_ready"), 1)

            def wait_features(name, n=8):
                pe.wait_ge(S("xl_done"), 2 * (8 * TOF[name] + n))

            def features_use(name, src=None):
                def use(c, j):
                    if c == 0:
                        if src is not None and j < 3:
                            to_features(name, src, (range(4), range(4, 6), range(6, 8))[j])
                        wait_features(name, j + 1)
                return use

            def turn(name, c):
                pe.wait_ge(S("projected"), 2 * (PROJ0[name] + c) + 2)
                pj = pj_at(name)
                for j in range(2):
                    n = 2 * TURN[name, c] + j
                    if name == "ev_gdn":
                        b = claim(side[j], "conv_step", 8 * (n + 1))
                    else:
                        b = claim(side[j], "turn_done", n + 1 - 12)
                    for jb in range(2):
                        for t in range(TT):
                            mm = pe.transpose(b[:, jb * TOK + t * P:jb * TOK + t * P + P],
                                              pj[:, t, (2 * j + jb) * P:(2 * j + jb + 1) * P], ident)
                    mm.then_inc(S("turned"), 1)

            def conv_back(c):
                for j in range(2):
                    n = 2 * c + j
                    pe.wait_ge(S("conv_silu"), n + 1)
                    b = claim(side[2 + j], "qkv_done", n + 1)
                    cs = at(CONV + 1024 + j * CH, 2, TOK)
                    for t in range(TT):
                        for jb in range(2):
                            mm = pe.transpose(b[:, t * TOK + jb * P:t * TOK + jb * P + P],
                                              cs[:, jb, t * P:t * P + P], ident)
                    mm.then_inc(S("conv_back"), 1)

            pe.wait_ge(S("common_in"), 16)
            pe.wait_ge(S("rows_in"), 96)
            rows = at(0, 2, P)
            b = claim(side[0], "cols_done", 1)
            pe.transpose(b[:, 0:96], rows[0:96, 0], ident[0:96, 0:96])
            pe.transpose(b[:, P:P + 96], rows[0:96, 1], ident[0:96, 0:96]).then_inc(S("cols_ready"), 1)

            to_features("ev_gdn", h)

            def gdn_aside(c, j):
                if (c, j) == (0, 7):
                    pe.wait_ge(S("wab_lo"), 1)
                    b = claim(side[2], "ab_copied", 1)
                    for k in range(KM):
                        for n, (w, x) in enumerate(((wab_h, xh), (wab_l, xh), (wab_h, xl))):
                            mm = pe.matmul(b[0:16, 0:TOK], w[:, k], x[:, k], start=(k == 0 and n == 0),
                                           stop=(k == KM - 1 and n == 2))
                    mm.then_inc(S("ab_ready"), 1)
                if (c, j) == (1, 3):
                    pe.wait_ge(S("ab_copied"), 1)
                    b = claim(side[2], "ab_done", 2)
                    for t in range(TT):
                        mm = pe.transpose(b[:, 16 * t:16 * t + 16], ab_rows[0:16, t * P:t * P + P], ident[0:16, 0:16])
                    mm.then_inc(S("ab_turned"), 1)
                if (c, j) == (4, 0):
                    pe.wait_ge(S("gate_g"), 1)
                    b = claim(side[0], "gcum_done", 2)
                    pe.matmul(b[:, 0:16], tri_u, g16(GL), start=True, stop=True).then_inc(S("gcum_ready"), 1)
                if c > 0 and j == 2:
                    turn("ev_gdn", c - 1)
                if c > 0 and j == 5:
                    conv_back(c - 1)

            linear("ev_gdn", xh, xl, projected("ev_gdn"), gdn_aside, features_use("ev_gdn"))

            def sb_stage(k):
                qT, kT, v = sb_in()
                if k == 0:
                    pe.wait_ge(S("turn_done"), 2 * TURN["ev_sb", 3] + 2 - 12)
                    pe.wait_ge(S("masks_in"), 16)
                if 1 <= k <= HEADS:
                    n = k - 1
                    pe.wait_ge(S("sb_scored"), 3 * n + 3)
                    b = claim(side[2], "sb_arg", n + 1)
                    y = sbw(n, 1)
                    pe.matmul(b[:, 0:TOK], tri_l, y[:, 0:TOK], start=True, stop=False)
                    pe.matmul(b[:, 0:TOK], ones, y[:, TOK:], start=False, stop=True)
                    pe.matmul(b[:, TOK:], tri_l, y[:, TOK:], start=True, stop=True).then_inc(S("sb_c"), 1)
                if k >= 2:
                    n = k - 2
                    pe.wait_ge(S("projected"), 2 * (PROJ0["ev_sb"] + 5 + n // 4))
                    pe.wait_ge(S("sb_w"), n + 1)
                    b = claim(side[3], "sb_out", n + 1)
                    w = sbw(n, 0)
                    vh = lambda kt: v[:, kt, n * P:n * P + P]
                    pe.matmul(b[:, 0:P], w[:, 0:P], vh(0), start=True, stop=True)
                    pe.matmul(b[:, P:TOK], w[:, P:TOK], vh(0), start=True, stop=False)
                    pe.matmul(b[:, P:TOK], w[:, TOK + P:], vh(1), start=False, stop=True).then_inc(S("sb_o"), 1)
                if k < HEADS:
                    b = claim(side[k % 2], "sb_scored", 3 * k + 1)
                    for kt in range(2):
                        mm = pe.matmul(b[:, kt * TOK:kt * TOK + TOK], kT[:, k, kt * P:kt * P + P], qT[:, k],
                                       start=True, stop=True)
                    mm.then_inc(S("sb_s"), 1)

            def sb_aside(c, j):
                if 0 < c <= 4 and j == 2:
                    turn("ev_sb", c - 1)
                if (c, j) == (5, 6):
                    sb_stage(0)

            sb_granules = granules("ev_sb", xh, xl, projected("ev_sb"), sb_aside)
            beside = lambda n=1: [next(sb_granules) for _ in range(n)]

            turn("ev_gdn", 5)
            beside(3)
            conv_back(5)
            beside()

            def mm4(bank, lhs, rhs):
                for k in range(4):
                    mm = pe.matmul(bank[:, k * P:k * P + P], lhs(k), rhs(k), start=True, stop=True)
                return mm

            pe.wait_ge(S("qk_normed"), 4)
            for hg in range(2):
                for t in range(TT):
                    n = 2 * hg + t
                    for s, (o, ready) in enumerate(((1024, "kT_ready"), (0, "qT_ready"))):
                        b = claim(side[2 * t + s], "kT_done" if s == 0 else "qT_done", n + 1)
                        for k in range(4):
                            c0 = o + (4 * hg + k) * P
                            mm = pe.transpose(b[:, k * P:k * P + P], qkv[:, t, c0:c0 + P], ident)
                        mm.then_inc(S(ready), 1)
                beside()
                for t in range(TT):
                    b = claim(side[2 * t], "decay_arg", 9 * (2 * hg + t + 1))
                    for k in range(4):
                        c0 = t * 8 + 4 * hg + k
                        mm = pe.matmul(b[:, k * P:k * P + P], g16(GL)[:, c0:c0 + 1].to_broadcast([P, P]), tri_u,
                                       start=True, stop=True)
                    mm.then_inc(S("gb_ready"), 1)
                beside()
                for t in range(TT):
                    n = 2 * hg + t
                    U = lambda k, t=t: unit(t, k)
                    pe.wait_ge(S("kT_done"), n + 1)
                    b = claim(side[2 * t + 1], "L_done", lower(n))
                    mm4(b, lambda k: U(KT)[:, k], lambda k: U(KT)[:, k]).then_inc(S("kk_ready"), 1)
                    pe.wait_ge(S("qT_done"), n + 1)
                    b = claim(side[2 * t], "L_done", inner(n))
                    mm4(b, lambda k: U(KT)[:, k], lambda k: U(QT)[:, k]).then_inc(S("kq_ready"), 1)
                beside(2)
                for t in range(TT):
                    n = 2 * hg + t
                    pe.wait_ge(S("L_done"), lower(n))
                    b = claim(side[2 * t + 1], "LT_done", n + 1)
                    for k in range(4):
                        mm = pe.transpose(b[:, k * P:k * P + P], unit(t, M_)[:, k], ident)
                    mm.then_inc(S("lt_ready"), 1)
                beside(2)
                for l in range(1, 7):
                    for t in range(TT):
                        U = lambda k, t=t: unit(t, k)
                        pe.wait_ge(S(f"inv_step{t}"), 21 * hg + 4 + 3 * (l - 1) + 1)
                        b = claim(side[t], f"T_done{t}", 6 * hg + l)
                        mm4(b, lambda k: U(LM_)[:, k], lambda k: U(M_)[:, k]).then_inc(S("t1_ready"), 1)
                    for t in range(TT):
                        U = lambda k, t=t: unit(t, k)
                        pe.wait_ge(S(f"T_done{t}"), 6 * hg + l)
                        if l < 6:
                            b = claim(side[2 + t], f"inv_step{t}", 21 * hg + 4 + 3 * (l - 1) + 2)
                            mm4(b, lambda k: U(MT_)[:, k], lambda k: U(T_)[:, k]).then_inc(S("p_ready"), 1)
                        b = claim(side[t], f"inv_step{t}", 21 * hg + 4 + 3 * (l - 1) + (3 if l < 6 else 2))
                        mm4(b, lambda k: U(T_)[:, k], lambda k: U(MT_)[:, k]).then_inc(S("p_ready"), 1)
                    beside()
                U0, U1 = (lambda k: unit(0, k)), (lambda k: unit(1, k))
                pe.wait_ge(S("r_done"), 6 * hg + 1)
                b = claim(side[0], "vn_done", 2 * hg + 1)
                mm4(b, lambda k: U0(MT_)[:, k], lambda k: U0(T_)[:, k]).then_inc(S("vn_ready"), 1)
                beside()
                pe.wait_ge(S("vn_done"), 2 * hg + 1)
                pe.wait_ge(S("kd_done"), hg + 1)
                b = claim(side[1], "s_done", hg + 1)
                mm4(b, lambda k: qkv[:, 0, 1024 + (4 * hg + k) * P:1024 + (4 * hg + k + 1) * P],
                    lambda k: U0(LM_)[:, k]).then_inc(S("s_ready"), 1)
                b = claim(side[2], "o_raw", 2 * hg + 1)
                mm4(b, lambda k: U0(A_)[:, k], lambda k: U0(LM_)[:, k]).then_inc(S("o_ready"), 1)
                beside()
                pe.wait_ge(S("s_done"), hg + 1)
                b = claim(side[3], "r_done", 6 * hg + 6)
                mm4(b, lambda k: U1(KT)[:, k], lambda k: U0(KT)[:, k]).then_inc(S("ks_ready"), 1)
                b = claim(side[1], "qs_done", 4 * (hg + 1))
                mm4(b, lambda k: U1(QT)[:, k], lambda k: U0(KT)[:, k]).then_inc(S("qs_ready"), 1)
                beside()
                pe.wait_ge(S("r_done"), 6 * hg + 6)
                b = claim(side[0], "vn_done", 2 * hg + 2)
                mm4(b, lambda k: U1(MT_)[:, k], lambda k: U1(T_)[:, k]).then_inc(S("vn_ready"), 1)
                beside()
                pe.wait_ge(S("vn_done"), 2 * hg + 2)
                b = claim(side[2], "o_raw", 2 * hg + 2)
                mm4(b, lambda k: U1(A_)[:, k], lambda k: U1(LM_)[:, k]).then_inc(S("o_ready"), 1)
                beside()

            for _ in sb_granules:
                pass

            def z_aside(c, j):
                if j % 2 == 0:
                    sb_stage(1 + 4 * c + j // 2)

            linear("ev_z", xh, xl, projected("ev_z"), z_aside)
            sb_stage(9)

            def post(name):
                return lambda c, t: ("ug_done", 8 * POST[name] + 2 * c + t + 1)

            linear("ev_out", xh, xl, post("ev_out"), None, features_use("ev_out", u))

            def turn_hidden(n):
                pe.wait_ge(S("hm_done"), 2 * n + 2)
                for b in range(2):
                    for jb in range(2):
                        for t in range(TT):
                            mm = pe.transpose(side[b][:, jb * TOK + t * P:jb * TOK + t * P + P],
                                              hm[:, t, (2 * b + jb) * P:(2 * b + jb + 1) * P], ident)
                    mm.then_inc(S("hid_ready"), 1)

            def hidden(name):
                n0, blocks, g0 = FFB[name], CHUNKS[name] // 2, GRAN0[name]

                def block_of(i, first):
                    for m in range(2):
                        for j in range(8):
                            if m == 0 and j == 2 and not first:
                                pe.wait_ge(S("hTl_done"), 2 * n0 + 2 * i - 2)
                                turn_hidden(i + (n0 - 1))
                            if j == 0:
                                if first:
                                    for t in range(TT):
                                        claim(acc[2 * m + t], "sg_done", 0)
                                else:
                                    pe.wait_ge(S("hm_done" if m else "sg_done"), 2 * n0 + 2 * i)
                            if first and m == 0 and name[3] == "a":
                                features_use(name, h)(0, j)
                            granule(i * 16 + (g0 + 8 * m + j), j % RING, m, xh, xl, 2 * j, j == 0, j == 7)

                block_of(0, True)
                with pe.Fori(1, blocks) as i:
                    block_of(i, False)
                for t in range(TT):
                    last_reader[acc[t].name] = (S("sg_done"), 2 * (n0 + blocks))
                    last_reader[acc[2 + t].name] = (S("hm_done"), 2 * (n0 + blocks))
                for b in range(2):
                    last_reader[side[b].name] = (S("hTl_done"), 2 * (n0 + blocks - 1))

            def down(name, up):
                n = FFB[up] + CHUNKS[up] // 2 - 1

                def aside(c, j):
                    if c == 0 and j == 2:
                        for b in range(2):
                            claim(side[b], "hTl_done", 2 * n + 2)
                        turn_hidden(n)
                    if c == 0 and j == 0:
                        pe.wait_ge(S("hTl_done"), 2 * n)
                    if c == 0 and j == KTS[name] // 2 - 2:
                        pe.wait_ge(S("hTl_done"), 2 * n + 2)

                if name[3] == "a":
                    freed = lambda c, t: ("half_done", 8 * int(name[2]) + 2 * c + t + 1)
                else:
                    freed = lambda c, t: ("u_done", 8 * int(name[2]) + 2 * c + t + 1)
                linear(name, hTh, hTl, freed, aside)

            def feed_forward(l):
                hidden(f"up{l}a")
                down(f"dn{l}a", f"up{l}a")
                hidden(f"up{l}b")
                down(f"dn{l}b", f"up{l}b")

            feed_forward(0)


            def od_aside(c, j):
                if ("od_in", c - 1) in TURN and j == 2:
                    turn("od_in", c - 1)

            linear("od_in", xh, xl, projected("od_in"), od_aside, features_use("od_in", h))

            def at_scores(n):
                qT, kT, _ = att_in("at", n // HEADS)
                hd = n % HEADS
                b = claim(side[n % 2], "at_scored", 3 * n + 1)
                pe.matmul(b[:, 0:P], qT[:, hd, 0:P], kT[:, hd, 0:P], start=True, stop=True)
                pe.matmul(b[:, P:384], qT[:, hd, P:TOK], kT[:, hd], start=True, stop=True).then_inc(S("at_s"), 1)

            def at_turn(n):
                pe.wait_ge(S("at_exp"), 2 * n + 2)
                b = claim(side[2 + n % 2], "at_pT", n + 1)
                p = atw(n, 0)
                for k in range(3):
                    mm = pe.transpose(b[:, k * P:k * P + P], p[:, k * P:k * P + P], ident)
                mm.then_inc(S("at_turned"), 1)

            def at_values(n):
                _, _, v = att_in("at", n // HEADS)
                hd = n % HEADS
                pe.wait_ge(S("at_pT"), n + 1)
                b = claim(acc[n % 4], "at_out", 2 * n + 2)
                pT = atw(n, 1)
                vh = lambda kt: v[:, kt, hd * P:hd * P + P]
                pe.matmul(b[:, 0:P], pT[:, 0:P], vh(0), start=True, stop=True)
                pe.matmul(b[:, P:TOK], pT[:, P:TOK], vh(0), start=True, stop=False)
                pe.matmul(b[:, P:TOK], pT[:, TOK:384], vh(1), start=False, stop=True).then_inc(S("at_o"), 1)

            pe.wait_ge(S("projected"), 2 * (PROJ0["od_in"] + 12))
            pe.wait_ge(S("turn_done"), 2 * TURN["od_in", 9] + 2 - 12)
            for n in range(2 * HEADS + 2):
                if n < 2 * HEADS:
                    at_scores(n)
                if 1 <= n <= 2 * HEADS:
                    at_turn(n - 1)
                if n >= 2:
                    at_values(n - 2)
            linear("od_out", xh, xl, post("od_out"), None, features_use("od_out", u))
            feed_forward(1)


            def parameter_columns():
                pe.wait_ge(S("srow_ready"), 1)
                b = claim(side[2], "scol_done", 1)
                srow = at(SROW, 4, P)
                for n in range(3):
                    mm = pe.transpose(b[:, n * PAIRS:(n + 1) * PAIRS], srow[0:PAIRS, n], ident[0:PAIRS, 0:PAIRS])
                mm.then_inc(S("scol_ready"), 1)

            def turn_wide(o, n, wide_done, ready, freed, counts):
                pe.wait_ge(S(wide_done), 2 * n + 2)
                for half in range(2):
                    b = claim(side[2 + half], freed, counts[half])
                    for k in range(4):
                        ct = 4 * half + k
                        mm = pe.transpose(b[:, k * P:k * P + P], at(o, 2, 1024)[:, n, ct * P:ct * P + P], ident)
                    mm.then_inc(S(ready), 1)

            uT, bt, cts = at(UT, 8, TOK), at(BT, 2, 8, P), at(CT, 3, 8, P)

            def ssm_in(n):
                ct, r = n // 4, n % 4
                b = claim(side[n % 3], "rotated", 5 * n + 4)
                rows = slice(32 * r, 32 * r + 32)
                for m in range(2):
                    mm = pe.matmul(b[:, m * TOK:m * TOK + TOK], bt[rows, m, ct], uT[rows, ct], start=True, stop=True)
                mm.then_inc(S("bu_ready"), 1)

            def ssm_out(n):
                ct, r = n // 4, n % 4
                y = claim(side[3], "y_done", ct + 1) if r == 0 else side[3]
                pe.wait_ge(S("unrotated"), 2 * n + 2)
                q = products(n)
                o = y[32 * r:32 * r + 32, 0:TOK]
                cw = lambda k: cts[:, k, ct, 32 * r:32 * r + 32]
                pe.matmul(o, cw(0), q[:, 0, 0:TOK], start=True, stop=False)
                pe.matmul(o, cw(2), q[:, 0, TOK:], start=False, stop=False)
                pe.matmul(o, cw(1), q[:, 1, TOK:], start=False, stop=False)
                pe.matmul(o, cw(2), q[:, 1, 0:TOK], start=False, stop=True).then_inc(S("y_part"), 1)

            def s_aside(c, j):
                at_ = 8 * c + j
                if at_ in (10, 18, 30, 35):
                    turn("s_in", (10, 18, 30, 35).index(at_))
                if at_ == 9:
                    parameter_columns()
                if at_ == 12:
                    turn_wide(SGS, 0, "c_wide", "ct_ready", "ct_done", (2, 4))
                if at_ == 14:
                    turn_wide(SGS, 1, "c_wide", "ct_ready", "ct_done", (5, 6))
                if at_ == 19:
                    turn_wide(SGP, 0, "b_wide", "bt_ready", "bt_done", (1, 2))
                if at_ == 21:
                    turn_wide(SGP, 1, "b_wide", "bt_ready", "bt_done", (3, 4))
                if at_ == SSM_AT[0]:
                    pe.wait_ge(S("bt_done"), 4)
                    pe.wait_ge(S("turn_done"), 2 * TURN["s_in", 1] + 2 - 12)
                for ct in range(8):
                    if at_ == SSM_AT[ct] - (ct > 0):
                        for r in range(3):
                            ssm_in(4 * ct + r)
                    if ct and at_ == SSM_AT[ct]:
                        for r in range(2):
                            ssm_out(4 * ct - 4 + r)
                    if at_ == SSM_AT[ct] + 2:
                        if ct:
                            for r in range(2, 4):
                                ssm_out(4 * ct - 4 + r)
                        ssm_in(4 * ct + 3)
                if at_ == SSM_AT[7] + 5:
                    for r in range(2):
                        ssm_out(28 + r)

            linear("s_in", xh, xl, projected("s_in"), s_aside, features_use("s_in", h))
            for r in range(2, 4):
                ssm_out(28 + r)

            pooled, wp = at(POOLED, 8, TOK), at(WPOOL, 8, 256)

            def glu_aside(c, j):
                if 4 * c + j in POOL_AT:
                    g = POOL_AT.index(4 * c + j)
                    if g == 0:
                        pe.wait_ge(S("wpool_in"), 16)
                    pe.wait_ge(S("pooled"), g + 1)
                    b = claim(side[g], "pool_out", g + 1)
                    for t in range(TT):
                        for kt in range(2):
                            mm = pe.matmul(b[:, t * 256:t * 256 + 256], pooled[:, 2 * g + kt, t * P:t * P + P],
                                           wp[:, 2 * g + kt], start=(kt == 0), stop=(kt == 1))
                    mm.then_inc(S("pool_mixed"), 1)

            def glu_use(c, j):
                if c == 0:
                    pe.wait_ge(S("gl_done"), 2 * j + 2)

            linear("glu", xh, xl, lambda c, t: ("glu_sig", 2 * (c // 2) + t + 1) if c % 2 else ("glu_out", 2 * (c // 2) + t + 1),
                   glu_aside, glu_use)
            def s_out_aside(c, j):
                if (c, j) == (2, 2):
                    pe.wait_ge(S("p_in"), 16)
                    for t in range(TT):
                        b = claim(side[t], "pl_done", t + 1)
                        for k in range(2):
                            mm = pe.transpose(b[:, k * P:k * P + P], at(13312, TT, 256)[:, t, k * P:k * P + P], ident)
                        mm.then_inc(S("p_turned"), 1)

            linear("s_out", xh, xl, lambda c, t: ("h_done", 8 * 4 + 2 * c + t + 1), s_out_aside, features_use("s_out", u))
            pe.wait_ge(S("pl_done"), 2)
            ple_granules = granules("ple", hTh, hTl, lambda c, t: ("ple_out", 2 * c + t + 1))
            next(ple_granules)
            next(ple_granules)
            to_features("pg", h)
            for _ in ple_granules:
                pass
            linear("pg", xh, xl, lambda c, t: ("pg_sig", 2 * c + t + 1), None, features_use("pg"))

        NORM = {"ev_gdn": 0, "up0a": 1, "od_in": 2, "up1a": 3, "s_in": 4}
        GAIN = {"ev_gdn": 0, "od_in": 1, "up0a": 2, "up1a": 3, "s_in": 4}

        @block.scalar
        def _(act):

            def run(o, i, f, done, **kw):
                act.activation(o, i, f, **kw).then_inc(S(done), 1)

            def split(g, place=None):
                if place is None:
                    place = g % (2 * RING)
                    if g % 2 == 0 or GRAN0["ple"] <= g < GRAN0["pg"]:
                        landed(act, g)
                if not isinstance(g, int) or g >= RING:
                    act.wait_ge(S("used"), g - (RING - 1))
                act.activation(whi[:, place % RING], raw_granule(place), ACT.Copy).then_inc(S("hi_done"), 1)

            def linear(*args):
                for _ in granules(*args):
                    pass

            def granules(name, evac, lead, aside=None, after=2):
                per = KTS[name] // 2
                for c in range(CHUNKS[name]):
                    for j in range(per):
                        split(gran(name, c, j))
                        if j == min(after, per - 1):
                            if c == 0:
                                lead()
                            else:
                                evac(c - 1)
                        if aside:
                            aside(c, j)
                        yield

            def chunk_done(name, c):
                act.wait_ge(S("used"), gran(name, c) + KTS[name] // 2)

            def project(name, c):
                if c == 0:
                    act.wait_ge(S("rstd_done"), NORM["ev_gdn" if name[0] == "e" else name] + 1)
                chunk_done(name, c)
                pair = (CHUNK0[name] + c) % 2
                f = ACT.Copy
                if (name, c) in TURN:
                    act.wait_ge(S("turned"), 2 * TURN[name, c])
                    dst = pj_at(name)
                    if (name, c) == ("ev_gdn", 0):
                        act.wait_ge(S("cols_done"), 1)
                elif name == "ev_sb":
                    dst = sb_in()[2][:, :, CH * (c - 4):CH * (c - 3)]
                elif name == "od_in":
                    dst = at(6144 * (c // 6) + 4096, TT, 1024)[:, :, CH * (c % 2):CH * (c % 2) + CH]
                else:
                    f = ACT.Silu
                    if name == "ev_z":
                        dst = pj_at(name)
                        if c == 0:
                            act.wait_ge(S("gdn_out"), 20)
                        if c == 1:
                            act.wait_ge(S("mixed"), 2)
                    else:
                        dst = at(SGP if c < 6 else SGS, TT, 1024)[:, :, CH * (c % 2):CH * (c % 2) + CH]
                for t in range(TT):
                    run(dst[:, t], acc[2 * pair + t][:], f, "projected", scale=rstd[:, t:t + 1])

            def turn_out(name, c):
                for j in range(2):
                    n = 2 * TURN[name, c] + j
                    act.wait_ge(S("turned"), n + 1)
                    run(turned_to(name, c, j), side[j][:], ACT.Copy, "turn_done")

            def features_hi(name, rounds=range(8)):
                base = 8 * TOF[name]
                if name != "ev_gdn":
                    act.wait_ge(S("used"), GRAN0["ple" if name == "pg" else name])
                for r in rounds:
                    act.wait_ge(S("tof_ready"), base + r + 1)
                    if r == 0 and name == "ev_gdn":
                        act.wait_ge(S("cols_done"), 1)
                    for j in range(2):
                        k = 2 * r + j
                        if name in GAIN:
                            sc = gain_col(GAIN[name], k)
                        elif name == "s_out" and k < 8:
                            sc = pool_col(k)
                        else:
                            sc = 1.0
                        run(xh[:, k], side[r % 4][:, j * TOK:(j + 1) * TOK], ACT.Copy, "xh_done", scale=sc)

            def stats(n, src, junk):
                for t in range(TT):
                    if n > 0:
                        act.wait_ge(S("rms_done"), n)
                    if t:
                        act.wait_ge(S("ssq_done"), 2 * n + t)
                    run(junk, src[:, t], ACT.Square, "ssq_done", accum_out=ssh[:, t:t + 1])
                act.wait_ge(S("ssq_done"), 2 * n + 2)
                if n > 0:
                    act.wait_ge(S("rstd_done"), n)
                run(rms_h, ssh, ACT.Sqrt, "rms_done", scale=1.0 / DM, bias=EPS)

            JUNK = at(12288, DM)

            features_hi("ev_gdn", range(LEAD))

            def lead():
                for c in range(4):
                    act.wait_ge(S(f"x_in{c}"), 16)
                stats(0, h, JUNK)

            def conv_silu(c):
                for j in range(2):
                    n = 2 * c + j
                    act.wait_ge(S("conv_step"), 8 * n + 8)
                    if n >= 2:
                        act.wait_ge(S("conv_back"), n - 1)
                    run(at(CONV + 1024 + j * CH, CH), at(CONV + j * CH, CH), ACT.Silu, "conv_silu")

            def conv_out(c):
                for j in range(2):
                    n = 2 * c + j
                    act.wait_ge(S("conv_back"), n + 1)
                    run(qkv[:, :, (4 * c + 2 * j) * P:(4 * c + 2 * j + 2) * P],
                        side[2 + j][:].rearrange("p (t n) -> p t n", t=TT), ACT.Copy, "qkv_done")

            def gates():
                act.wait_ge(S("gate_a"), 1)
                run(g16(T1_), g16(AV), ACT.Abs, "gate_act")
                act.wait_ge(S("gate_act"), 1)
                run(g16(T2_), g16(T1_), ACT.Exp, "gate_act", scale=-1.0)
                act.wait_ge(S("gate_act"), 2)
                run(g16(EG)[:, 0:8], alog, ACT.Exp, "gate_act")
                run(g16t(BE), ab[:, :, 8:16], ACT.Exp, "gate_act", scale=-1.0)
                run(g16(T3_), g16(T2_), ACT.Ln, "gate_act", bias=1.0)

            def gdn_aside(c, j):
                if (c, j) == (0, 0):
                    features_hi("ev_gdn", range(LEAD, 8))
                if (c, j) == (0, 3):
                    act.wait_ge(S("gdn_rows_in"), 64)
                    run(wab_h[:], wab, ACT.Copy, "wab_hi")
                if (c, j) == (1, 1):
                    act.wait_ge(S("ab_ready"), 1)
                    run(ab_rows[0:16], side[2][0:16, 0:TOK], ACT.Copy, "ab_copied")
                if (c, j) == (3, 6):
                    gates()
                if (c, j) == (4, 2):
                    act.wait_ge(S("gcum_ready"), 1)
                    run(g16(GC), side[0][:, 0:16], ACT.Copy, "gcum_done")
                    run(g16(EG), side[0][:, 0:16], ACT.Exp, "gcum_done")
                if (c, j) == (5, 5):
                    act.wait_ge(S("qk_sum"), 8)
                    run(rn2, rn, ACT.Sqrt, "qk_rms", bias=EPS)
                if (c, j) == (1, 5):
                    act.wait_ge(S("ab_turned"), 1)
                    act.wait_ge(S("rstd_done"), 1)
                    for t in range(TT):
                        run(ab[:, t], side[2][:, 16 * t:16 * t + 16], ACT.Copy, "ab_done", scale=rstd[:, t:t + 1])
                if c > 0 and j == 5:
                    conv_silu(c - 1)
                if c > 0 and j == 7:
                    conv_out(c - 1)

            linear("ev_gdn", lambda c: project("ev_gdn", c), lead, gdn_aside)

            def sb_aside(c, j):
                if 0 < c <= 4 and j == 6:
                    turn_out("ev_sb", c - 1)

            sb_granules = granules("ev_sb", lambda c: project("ev_sb", c), lambda: None, sb_aside, 3)
            beside = lambda n=1: [next(sb_granules) for _ in range(n)]

            beside(3)
            project("ev_gdn", 5)
            beside(2)
            conv_silu(5)
            beside(2)
            conv_out(5)

            def o_root(hg, t):
                act.wait_ge(S("gdn_out"), 5 * (2 * hg + t) + 2)
                c0 = slice(8 * t + 4 * hg, 8 * t + 4 * hg + 4)
                run(g16(ORR)[:, c0], g16(OSS)[:, c0], ACT.Sqrt, "o_rms", scale=1.0 / HD, bias=EPS)

            def heads_of(bank):
                return bank[:].rearrange("p (h n) -> p h n", h=4)

            for hg in range(2):
                beside()
                for t in range(TT):
                    n = 2 * hg + t
                    act.wait_ge(S("kT_ready"), n + 1)
                    if n == 0:
                        act.wait_ge(S("conv_back"), 12)
                    run(unit(t, KT), heads_of(side[2 * t]), ACT.Copy, "kT_done")
                    act.wait_ge(S("qT_ready"), n + 1)
                    if hg:
                        act.wait_ge(S("o_raw"), 2 * hg)
                    run(unit(t, QT), heads_of(side[2 * t + 1]), ACT.Copy, "qT_done")
                beside()
                for t in range(TT):
                    n = 2 * hg + t
                    act.wait_ge(S("decay_arg"), 9 * n + 9)
                    run(unit(t, M_), unit(t, M_), ACT.Exp, "dec_done")
                    run(unit(t, A_), unit(t, A_), ACT.Exp, "dec_done")
                    ka = slice(8 * t + 4 * hg, 8 * t + 4 * hg + 4)
                    run(g16(EKA)[:, ka], g16(KA)[:, ka], ACT.Exp, "dec_done")
                beside(3)
                for t in range(TT):
                    act.wait_ge(S("lt_ready"), 2 * hg + t + 1)
                    run(unit(t, LT_), heads_of(side[2 * t + 1]), ACT.Copy, "LT_done")
                for l in range(1, 7):
                    beside(2 if l == 1 else 1)
                    for t in range(TT):
                        act.wait_ge(S("t1_ready"), (6 * hg + l - 1) * 2 + t + 1)
                        run(unit(t, T_), heads_of(side[t]), ACT.Copy, f"T_done{t}")
                    if hg and l in (2, 4):
                        o_root(0, l // 2 - 1)
                beside()
                act.wait_ge(S("vn_ready"), 2 * hg + 1)
                run(unit(0, LM_), heads_of(side[0]), ACT.Copy, "vn_done")
                beside()
                act.wait_ge(S("s_ready"), hg + 1)
                run(unit(0, KT), heads_of(side[1]), ACT.Copy, "s_done")
                beside()
                act.wait_ge(S("qs_ready"), hg + 1)
                for k in range(4):
                    c0 = 8 + 4 * hg + k
                    run(unit(0, QT)[:, k], side[1][:, k * P:k * P + P], ACT.Copy, "qs_done",
                        scale=g16(EG)[:, c0:c0 + 1])
                beside()
                act.wait_ge(S("vn_ready"), 2 * hg + 2)
                run(unit(1, LM_), heads_of(side[0]), ACT.Copy, "vn_done")
                beside()
            for t in range(TT):
                o_root(1, t)
            for _ in sb_granules:
                pass

            def sb_stage(k):
                if k >= 1:
                    act.wait_ge(S("sb_arg"), k)
                    run(sbw(k - 1, 0), sbw(k - 1, 2), ACT.Exp, "sb_w")
                if k < HEADS:
                    x, y = sbw(k, 0), sbw(k, 1)
                    act.wait_ge(S("sb_s"), k + 1)
                    if k == 0:
                        act.wait_ge(S("gdn_out"), 20)
                    if k >= 2:
                        act.wait_ge(S("sb_o"), k - 1)
                        act.wait_ge(S("sb_c"), k - 1)
                    b = side[k % 2][:]
                    run(x, b, ACT.Abs, "sb_act", scale=SCALE)
                    act.wait_ge(S("sb_act"), 4 * k + 1)
                    run(x, x, ACT.Exp, "sb_act", scale=-1.0)
                    act.wait_ge(S("sb_act"), 4 * k + 2)
                    run(x, x, ACT.Ln, "sb_act", bias=1.0)
                    run(y, b, ACT.Relu, "sb_act", scale=SCALE)

            def z_aside(c, j):
                if j % 2 == 0:
                    sb_stage(4 * c + j // 2)

            linear("ev_z", lambda c: project("ev_z", c), lambda: project("ev_sb", 5), z_aside)

            def square_out(name, c):
                n = 8 * POST[name] + 2 * c
                if name[:2] != "dn":
                    chunk_done(name, c)
                pair = (CHUNK0[name] + c) % 2
                for t in range(TT):
                    if name[:2] == "dn":
                        act.wait_ge(S("u_done"), 8 * int(name[2]) + 2 * c + t + 1)
                        src = u[:, t, c * CH:c * CH + CH]
                    else:
                        src = acc[2 * pair + t][:]
                    if n + t:
                        act.wait_ge(S("sq_done"), n + t)
                    if n + t and POST[name] and c == 0:
                        act.wait_ge(S("ssum_done"), POST[name])
                    run(at(14336, CH), src, ACT.Square, "sq_done", accum_out=ss[:, 4 * t + c:4 * t + c + 1])

            def before_root():
                run(st[0:1, 100:101], ones[0:1, 0:1], ACT.Sqrt, "table_in")

            def rms_out(name):
                act.wait_ge(S("ssum_done"), POST[name] + 1)
                if POST[name]:
                    act.wait_ge(S("rstdu_done"), POST[name])
                run(rms_u, ssum, ACT.Sqrt, "rmsu_done", scale=1.0 / DM, bias=EPS)

            def lead():
                project("ev_z", 1)
                features_hi("ev_out")

            linear("ev_out", lambda c: square_out("ev_out", c), lead,
                   lambda c, j: sb_stage(HEADS) if (c, j) == (0, 0) else None)

            def turn_hidden(n, k):
                for b in range(2):
                    act.wait_ge(S("hid_ready"), 2 * n + b + 1)
                    act.activation(hTh[:, bass.ds(4 * k + 2 * b, 2)] if not isinstance(k, int)
                                   else hTh[:, 4 * k + 2 * b:4 * k + 2 * b + 2],
                                   side[b][:].rearrange("p (a b) -> p a b", a=2), ACT.Copy).then_inc(S("hTh_done"), 1)

            def hidden(name, lead):
                n0, blocks, g0 = FFB[name], CHUNKS[name] // 2, GRAN0[name]

                def block_of(i, first):
                    for m in range(2):
                        for j in range(8):
                            if j % 2 == 0:
                                n = (g0 + 8 * m + j) // 2
                                act.wait_ge(S(f"landed{n % RING}"), i * 32 + 16 * (n // RING + 1))
                            split(i * 16 + (g0 + 8 * m + j), j)
                            if first and m == 0 and j == 2:
                                lead()
                            if first and m == 0 and j == STATS and name[3] == "a":
                                stats(NORM[name], h, JUNK)
                            if not first and m == 0 and j == 5:
                                turn_hidden(i + (n0 - 1), i - 1)
                            if m == 1 and j == 2:
                                act.wait_ge(S("used"), i * 16 + (g0 + 8))
                                if not first:
                                    act.wait_ge(S("hm_done"), 2 * n0 + 2 * i)
                                elif n0:
                                    act.wait_ge(S("hm_done"), 2 * n0)
                                if first and name[3] == "a":
                                    act.wait_ge(S("rstd_done"), NORM[name] + 1)
                                for t in range(TT):
                                    act.activation(sg[:, t], acc[t][:], ACT.Silu, scale=rstd[:, t:t + 1])\
                                        .then_inc(S("sg_done"), 1)

                block_of(0, True)
                with act.Fori(1, blocks) as i:
                    block_of(i, False)

            def down(name, up, evac):
                n, blocks = FFB[up] + CHUNKS[up] // 2 - 1, CHUNKS[up] // 2

                def aside(c, j):
                    if c == 0 and j == 5:
                        turn_hidden(n, blocks - 1)

                linear(name, evac, lambda: None, aside)

            def half_out(l, c):
                chunk_done(f"dn{l}a", c)
                pair = (CHUNK0[f"dn{l}a"] + c) % 2
                for t in range(TT):
                    if c == 0:
                        act.wait_ge(S("h_done"), 8 * (2 * l + 1))
                    run(u[:, t, c * CH:c * CH + CH], acc[2 * pair + t][:], ACT.Copy, "half_done")

            def feed_forward(l, before):
                def lead():
                    before_root()
                    square_out(before, 3)
                    rms_out(before)
                    features_hi(f"up{l}a")

                hidden(f"up{l}a", lead)
                down(f"dn{l}a", f"up{l}a", lambda c: half_out(l, c))
                hidden(f"up{l}b", lambda: half_out(l, 3))
                down(f"dn{l}b", f"up{l}b", lambda c: square_out(f"dn{l}b", c))

            feed_forward(0, "ev_out")

            def lead():
                before_root()
                square_out("dn0b", 3)
                rms_out("dn0b")
                features_hi("od_in")

            def od_aside(c, j):
                if (c, j) == (0, STATS):
                    stats(NORM["od_in"], h, JUNK)
                if ("od_in", c - 1) in TURN and j == 4:
                    turn_out("od_in", c - 1)

            linear("od_in", lambda c: project("od_in", c), lead, od_aside)

            def attention():
                def exps(n):
                    act.wait_ge(S("at_scored"), 3 * n + 3)
                    p = atw(n, 0)
                    for t, cl in enumerate((slice(0, P), slice(P, 384))):
                        run(p[:, cl], p[:, cl], ACT.Exp, "at_exp", bias=st[:, 24 + 2 * (n % 2) + t:25 + 2 * (n % 2) + t],
                            accum_out=st[:, 32 + 2 * (n % 2) + t:33 + 2 * (n % 2) + t])

                def turned(n):
                    act.wait_ge(S("at_turned"), n + 1)
                    if n >= 2:
                        act.wait_ge(S("at_o"), n - 1)
                    run(atw(n, 1), side[2 + n % 2][:, 0:384], ACT.Copy, "at_pT")

                def values(n):
                    act.wait_ge(S("at_o"), n + 1)
                    act.wait_ge(S("at_recip"), n + 1)
                    for t in range(TT):
                        run(u[:, t, n * P:n * P + P], acc[n % 4][:, t * P:t * P + P], ACT.Copy, "at_out",
                            scale=st[:, 40 + 2 * (n % 2) + t:41 + 2 * (n % 2) + t])

                for n in range(2 * HEADS + 2):
                    if n < 2 * HEADS:
                        if n >= 2:
                            act.wait_ge(S("at_recip"), n - 1)
                        exps(n)
                    if 1 <= n <= 2 * HEADS:
                        turned(n - 1)
                    if n >= 2:
                        values(n - 2)

            def lead():
                project("od_in", 11)
                attention()
                features_hi("od_out")

            linear("od_out", lambda c: square_out("od_out", c), lead)
            feed_forward(1, "od_out")

            def lead():
                before_root()
                square_out("dn1b", 3)
                rms_out("dn1b")
                features_hi("s_in")

            def turned_wide(n, ready, done, outs):
                for half in range(2):
                    act.wait_ge(S(ready), 2 * n + half + 1)
                    b = side[2 + half][:].rearrange("p (a b) -> p a b", a=4)
                    buf = at(CT, 3, 8, P) if ready == "ct_ready" else at(BT, 2, 8, P)
                    for k, sc in outs:
                        run(buf[:, k, 4 * half:4 * half + 4], b, ACT.Copy, done, scale=sc)

            def tables(ct):
                act.wait_ge(S("tab_arg"), 5 * ct + 5)
                c, s = tab(ct)[:, 0], tab(ct)[:, 1]
                run(c, s, ACT.Abs, "tab_abs")
                act.wait_ge(S("tab_abs"), ct + 1)
                run(c, c, ACT.Sin, "tab_done", scale=-TWO_PI, bias=math.pi / 2)
                run(s, s, ACT.Sin, "tab_done", scale=TWO_PI)

            def gelu(ct):
                act.wait_ge(S("y_done"), ct + 1)
                y = at(UT, 8, TOK)[:, ct]
                run(y, y, ACT.Gelu_apprx_tanh, "gelu_done")

            def s_aside(c, j):
                at_ = 8 * c + j
                if at_ == STATS:
                    stats(NORM["s_in"], h, JUNK)
                if at_ in (12, 20, 31, 36):
                    if at_ == 31:
                        act.wait_ge(S("c_wide"), 4)
                        act.wait_ge(S("b_wide"), 4)
                    turn_out("s_in", (12, 20, 31, 36).index(at_))
                if at_ == 11:
                    act.wait_ge(S("scol_ready"), 1)
                    run(at(SCOL, 96), side[2][:, 0:96], ACT.Copy, "scol_done")
                    act.wait_ge(S("scol_done"), 1)
                    run(par(DTP), scol(2), ACT.Exp, "dt_done")
                if at_ == 14:
                    turned_wide(0, "ct_ready", "ct_done", ((0, 1.0), (1, -1.0)))
                if at_ == 15:
                    act.wait_ge(S("par"), ANGLES)
                    run(par(MAG), par(LR), ACT.Exp, "mag_done")
                    for o, i in ((SN, AS), (CS, AC), (S128, AS2), (C128, AC2)):
                        run(par(o), par(i), ACT.Sin, "sines")
                if at_ == 16:
                    turned_wide(1, "ct_ready", "ct_done", ((2, -1.0),))
                if at_ == 21:
                    turned_wide(0, "bt_ready", "bt_done", ((0, 1.0),))
                if at_ == 23:
                    turned_wide(1, "bt_ready", "bt_done", ((1, 1.0),))
                if at_ == 19:
                    tables(0)
                for ct in range(8):
                    if ct and at_ == SSM_AT[ct]:
                        tables(ct)
                    if at_ == SSM_AT[ct] + 10:
                        gelu(ct)

            def s_evac(c):
                if c == 4:
                    act.wait_ge(S("bt_ready"), 4)
                project("s_in", c)

            linear("s_in", s_evac, lead, s_aside)

            def lead():
                project("s_in", 7)
                act.wait_ge(S("used"), GRAN0["glu"])
                for ct in range(8):
                    if ct == 4:
                        gelu(7)
                    act.wait_ge(S("gelu_done"), ct + 1)
                    run(xh[:, ct], at(UT, 8, TOK)[:, ct], ACT.Copy, "gh_done")

            def glu_out(c):
                if c % 2:
                    chunk_done("glu", c)
                    m = c // 2
                    if m:
                        act.wait_ge(S("mixed"), 4 + 2 * m)
                    for t in range(TT):
                        run(spare[:, CH * t:CH * t + CH], acc[2 + t][:], ACT.Sigmoid, "glu_sig")

            assert CHUNK0["glu"] % 2 == 0 and CHUNK0["pg"] % 2 == 0
            linear("glu", glu_out, lead)

            def lead():
                glu_out(3)
                features_hi("s_out")

            def s_out_aside(c, j):
                if (c, j) == (2, 4):
                    act.wait_ge(S("mixed"), 8)
                    act.wait_ge(S("p_turned"), 2)
                    for k in range(2):
                        for t in range(TT):
                            run(hTh[:, k, t * P:t * P + P], side[t][:, k * P:k * P + P], ACT.Copy, "ph_done")

            linear("s_out", lambda c: None, lead, s_out_aside)

            def lead():
                features_hi("pg")

            for c in range(4):
                split(gran("ple", c))
                if c == 2:
                    lead()
            for c in range(4):
                act.wait_ge(S("used"), gran("ple", c) + 1)
                pair = (CHUNK0["ple"] + c) % 2
                for t in range(TT):
                    run(u[:, t, c * CH:c * CH + CH], acc[2 * pair + t][:], ACT.Copy, "ple_out")

            def gate_out(c):
                chunk_done("pg", c)
                pair = (CHUNK0["pg"] + c) % 2
                for t in range(TT):
                    if c:
                        act.wait_ge(S("gated"), 3 * (2 * c + t) - 4)
                    run(sg[:, t], acc[2 * pair + t][:], ACT.Sigmoid, "pg_sig")

            def squares(c):
                for t in range(TT):
                    n = 2 * c + t
                    act.wait_ge(S("gated"), 3 * n + 2)
                    act.wait_ge(S("ssum_done"), 4)
                    if n:
                        act.wait_ge(S("final_sq"), n)
                    run(at(14336, CH), h[:, t, CH * c:CH * c + CH], ACT.Square, "final_sq",
                        accum_out=ss[:, 4 * t + c:4 * t + c + 1])

            linear("pg", gate_out, lambda: None, lambda c, j: squares(c - 1) if c and j == 5 else None)
            gate_out(3)
            before_root()
            squares(3)
            act.wait_ge(S("ssum_done"), 5)
            act.wait_ge(S("rstdu_done"), 4)
            run(rms_u, ssum, ACT.Sqrt, "rmsu_done", scale=1.0 / DM, bias=EPS)
            act.wait_ge(S("rstdu_done"), 5)
            for c in range(4):
                run(u[:, 1, CH * c:CH * c + CH], u[:, 1, CH * c:CH * c + CH], ACT.Copy, "final1", scale=rstd_u[:, 1:2])
            act.wait_ge(S("out_done"), 64)

        @block.sync
        def _(sp):
            for c in range(4):
                cl = slice(CH * c, CH * c + CH)
                sp.wait_ge(S("final0"), c + 1)
                sp.wait_ge(S("final1"), c + 1)
                sp.dma_start(out[0][:, cl].rearrange("(t p) n -> p t n", p=P), u[:, :, cl]).then_inc(S("out_done"), 16)

        @block.vector
        def _(dve):
            def tt(o, a, b, op, done):
                dve.tensor_tensor(o, a, b, op).then_inc(S(done), 1)

            def stt(o, a, sc, b, op0, op1, done, **kw):
                dve.scalar_tensor_tensor(o, a, sc, b, op0, op1, **kw).then_inc(S(done), 1)

            def ts(o, a, s0, s1, op0, op1, done):
                dve.tensor_scalar(o, a, s0, s1, op0, op1).then_inc(S(done), 1)

            def split(g, place=None):
                place = g % (2 * RING) if place is None else place
                dve.wait_ge(S("hi_done"), g + 1)
                dve.tensor_tensor(wlo[:, place % RING], raw_granule(place), whi[:, place % RING].bitcast(F32),
                                  ALU.subtract).then_inc(S("lo_done"), 1)

            def linear(*args):
                for _ in granules(*args):
                    pass

            def granules(name, evac, lead, aside=None, after=2):
                per = KTS[name] // 2
                for c in range(CHUNKS[name]):
                    for j in range(per):
                        split(gran(name, c, j))
                        if j == min(after, per - 1):
                            if c == 0:
                                lead()
                            else:
                                evac(c - 1)
                        if aside:
                            aside(c, j)
                        yield

            def chunk_done(name, c):
                dve.wait_ge(S("used"), gran(name, c) + KTS[name] // 2)

            def features_lo(name, rounds=range(8)):
                base = 8 * TOF[name]
                for r in rounds:
                    for j in range(2):
                        k = 2 * r + j
                        dve.wait_ge(S("xh_done"), 2 * (base + r) + 2)
                        b = side[r % 4][:, j * TOK:(j + 1) * TOK]
                        hi = xh[:, k].bitcast(F32)
                        if name in GAIN:
                            stt(xl[:, k], b, gain_col(GAIN[name], k), hi, ALU.mult, ALU.subtract, "xl_done")
                        elif name == "s_out" and k < 8:
                            stt(xl[:, k], b, pool_col(k), hi, ALU.mult, ALU.subtract, "xl_done")
                        else:
                            tt(xl[:, k], b, hi, ALU.subtract, "xl_done")

            def reciprocal_rms(n):
                dve.wait_ge(S("rms_done"), n + 1)
                dve.reciprocal(rstd, rms_h).then_inc(S("rstd_done"), 1)

            dve.wait_ge(S("cols_ready"), 1)
            dve.tensor_copy(cols[:].rearrange("p (a b) -> p a b", a=2)[:, :, 0:96],
                            side[0][:, 0:2 * P].rearrange("p (a b) -> p a b", a=2)[:, :, 0:96])\
                .then_inc(S("cols_done"), 1)

            def conv(c):
                for j in range(2):
                    n = 2 * c + j
                    dve.wait_ge(S("turned"), n + 1)
                    if n >= 2:
                        dve.wait_ge(S("conv_silu"), n - 1)
                    x = side[j][:].rearrange("p (a b) -> p a b", a=2)
                    y = at(CONV + j * CH, 2, TOK)
                    for back in range(4):
                        for jb in range(2):
                            w = conv_col(3 - back, 4 * c + 2 * j + jb)
                            if back == 0:
                                ts(y[:, jb], x[:, jb], w, None, ALU.mult, ALU.bypass, "conv_step")
                            else:
                                dve.wait_ge(S("conv_step"), 8 * n + 2 * back + jb - 1)
                                stt(y[:, jb, back:], x[:, jb, 0:TOK - back], w, y[:, jb, back:],
                                    ALU.mult, ALU.add, "conv_step")

            features_lo("ev_gdn", range(LEAD))

            def lead():
                reciprocal_rms(0)

            def gates():
                dve.wait_ge(S("ab_done"), 2)
                dve.wait_ge(S("gdn_rows_in"), 64)
                tt(g16t(AV), ab[:, :, 0:8], dtb.unsqueeze(1).to_broadcast([P, TT, 8]), ALU.add, "gate_a")
                dve.wait_ge(S("gate_act"), 5)
                stt(g16(SPL), g16(AV), 0.0, g16(T3_), ALU.max, ALU.add, "gate_v")
                dve.wait_ge(S("gate_v"), 1)
                stt(g16t(GL), g16t(SPL), -1.0, g16(EG)[:, 0:8].unsqueeze(1).to_broadcast([P, TT, 8]),
                    ALU.mult, ALU.mult, "gate_g")
                dve.wait_ge(S("gate_act"), 5)
                ts(g16(BE), g16(BE), 1.0, None, ALU.add, ALU.bypass, "gate_v")
                dve.wait_ge(S("gate_v"), 2)
                dve.reciprocal(g16(BE), g16(BE)).then_inc(S("gate_v"), 1)

            def square_sum(k):
                t, m = k % 2, k // 2
                n = 2 * t + m
                sq = at(CONV + 2048, HEADS, HD)
                dve.wait_ge(S("qkv_done"), 4 * m + 4)
                x = qkv[:, t, 1024 * m:1024 * m + 1024].rearrange("p (h n) -> p h n", h=HEADS)
                if k:
                    dve.wait_ge(S("qk_sum"), 2 * k)
                tt(sq, x, x, ALU.mult, "qk_sum")
                dve.wait_ge(S("qk_sum"), 2 * k + 1)
                dve.tensor_reduce(rn[:, 8 * n:8 * n + 8], sq, AX_X, ALU.add).then_inc(S("qk_sum"), 1)

            def normalise(t, m):
                n = 2 * t + m
                x = qkv[:, t, 1024 * m:1024 * m + 1024].rearrange("p (h n) -> p h n", h=HEADS)
                f = rn[:, 8 * n:8 * n + 8].unsqueeze(2).to_broadcast([P, HEADS, HD])
                if m == 0:
                    stt(x, x, SCALE, f, ALU.mult, ALU.mult, "qk_normed")
                else:
                    tt(x, x, f, ALU.mult, "qk_normed")

            def gdn_aside(c, j):
                if (c, j) == (0, 0):
                    features_lo("ev_gdn", range(LEAD, 8))
                if (c, j) == (0, 3):
                    dve.wait_ge(S("wab_hi"), 1)
                    tt(wab_l[:], wab, wab_h[:].bitcast(F32), ALU.subtract, "wab_lo")
                if c > 0 and j == 4:
                    conv(c - 1)
                if (c, j) in ((3, 1), (3, 3), (5, 1), (5, 3)):
                    square_sum(((3, 1), (3, 3), (5, 1), (5, 3)).index((c, j)))
                if (c, j) == (3, 6):
                    gates()
                if (c, j) == (4, 5):
                    dve.wait_ge(S("gcum_done"), 2)
                    dve.wait_ge(S("gate_v"), 3)
                    stt(g16(NBEG), g16(BE), -1.0, g16(EG), ALU.mult, ALU.mult, "gate_v")
                if (c, j) == (5, 6):
                    dve.wait_ge(S("qk_rms"), 1)
                    dve.reciprocal(rn, rn2).then_inc(S("gate_v"), 1)
                    dve.wait_ge(S("gate_v"), 5)
                    normalise(0, 0)
                if (c, j) == (5, 7):
                    normalise(1, 0)

            linear("ev_gdn", lambda c: None, lead, gdn_aside)

            def four(x):
                return x.rearrange("p (h n) -> p h n", h=4)

            sb_granules = granules("ev_sb", lambda c: None, lambda: None)
            beside = lambda n=1: [next(sb_granules) for _ in range(n)]

            beside(4)
            conv(5)
            dve.wait_ge(S("masks_in"), 16)
            beside()
            for t in range(TT):
                normalise(t, 1)
            beside(2)

            mult, add, sub = ALU.mult, ALU.add, ALU.subtract

            def gdn_u(hg, t):
                return four(u[:, t, 1024 + CH * hg:1024 + CH * hg + CH])

            def gdn_norm(hg, t):
                n = 2 * hg + t
                O, Q = gdn_u(hg, t), four(qkv[:, t, CH * hg:CH * hg + CH])
                c0 = slice(8 * t + 4 * hg, 8 * t + 4 * hg + 4)
                dve.wait_ge(S("o_raw"), n + 1)
                tt(Q, O, O, mult, "gdn_out")
                dve.wait_ge(S("gdn_out"), 5 * n + 1)
                dve.tensor_reduce(g16(OSS)[:, c0], Q, AX_X, add).then_inc(S("gdn_out"), 1)
                dve.wait_ge(S("o_rms"), n + 1)
                dve.reciprocal(g16(ORR)[:, c0], g16(ORR)[:, c0]).then_inc(S("gdn_out"), 1)
                dve.wait_ge(S("gdn_out"), 5 * n + 3)
                tt(O, O, g16(ORR)[:, c0].unsqueeze(2).to_broadcast([P, 4, P]), mult, "gdn_out")
                dve.wait_ge(S("gdn_out"), 5 * n + 4)
                tt(O, O, heads4(onorm), mult, "gdn_out")

            for hg in range(2):
                def beta(t, k):
                    c0 = 8 * t + 4 * hg + k
                    return g16(BE)[:, c0:c0 + 1]

                beside(2)
                for t in range(TT):
                    n = 2 * hg + t
                    dve.wait_ge(S("gb_ready"), n + 1)
                    if n == 0:
                        dve.wait_ge(S("conv_silu"), 12)
                    for k in range(4):
                        c0 = 8 * t + 4 * hg + k
                        G = g16(GC)[:, c0:c0 + 1]
                        gb = side[2 * t][:, k * P:k * P + P]
                        stt(unit(t, M_)[:, k], gb, G, mask(0), sub, sub, "decay_arg", reverse1=True)
                        stt(unit(t, A_)[:, k], gb, G, mask(1), sub, add, "decay_arg")
                    ka = slice(8 * t + 4 * hg, 8 * t + 4 * hg + 4)
                    tt(g16(KA)[:, ka], four(side[2 * t][:])[:, :, P - 1], g16(GC)[:, ka], sub, "decay_arg")
                beside()
                for t in range(TT):
                    n = 2 * hg + t
                    dve.wait_ge(S("dec_done"), 3 * n + 3)
                    dve.wait_ge(S("kk_ready"), n + 1)
                    for k in range(4):
                        M = unit(t, M_)[:, k]
                        stt(M, side[2 * t + 1][:, k * P:k * P + P], beta(t, k), M, mult, mult, "L_done")
                for t in range(TT):
                    n = 2 * hg + t
                    dve.wait_ge(S("kq_ready"), n + 1)
                    tt(unit(t, A_), four(side[2 * t][:]), unit(t, A_), mult, "L_done")
                beside(2)
                for t in range(TT):
                    n = 2 * hg + t
                    inv = f"inv_step{t}"
                    dve.wait_ge(S("L_done"), lower(n))
                    stt(unit(t, T_), unit(t, M_), -1.0, heads4(mask(2)), mult, mult, inv)
                    dve.wait_ge(S("LT_done"), n + 1)
                    dve.wait_ge(S(inv), 21 * hg + 1)
                    tt(unit(t, M_), unit(t, T_), heads4(ident), add, inv)
                    stt(unit(t, LM_), unit(t, LT_), -1.0, heads4(mask(3)), mult, mult, inv)
                    dve.wait_ge(S(inv), 21 * hg + 3)
                    tt(unit(t, MT_), unit(t, LM_), heads4(ident), add, inv)

                def masked(l, t):
                    dve.wait_ge(S(f"inv_step{t}"), 21 * hg + 4 + 3 * (l - 1))
                    tt(unit(t, LM_), unit(t, LT_), heads4(mask(3 + l)), mult, f"inv_step{t}")

                for t in range(TT):
                    masked(1, t)
                for l in range(1, 7):
                    beside(2 if l == 1 else 1)
                    for t in range(TT):
                        inv = f"inv_step{t}"
                        ready = 22 * hg + (4 * (l - 1) + 2 * t if l < 6 else 19 + t)
                        if l < 6:
                            dve.wait_ge(S("p_ready"), ready + 1)
                            tt(unit(t, M_), unit(t, M_), four(side[2 + t][:]), sub, inv)
                        dve.wait_ge(S("p_ready"), ready + 2)
                        tt(unit(t, MT_), unit(t, MT_), four(side[t][:]), sub, inv)
                        if l < 6:
                            masked(l + 1, t)
                    if hg and l in (2, 4):
                        gdn_norm(0, l // 2 - 1)
                dve.wait_ge(S("qkv_done"), 12)
                for t in range(TT):
                    v = qkv[:, t, 2048 + CH * hg:2048 + CH * hg + CH]
                    b = g16(BE)[:, 8 * t + 4 * hg:8 * t + 4 * hg + 4].unsqueeze(2).to_broadcast([P, 4, P])
                    tt(unit(t, T_), four(v), b, mult, "r_done")
                    if t == 0:
                        k0 = four(qkv[:, 0, 1024 + CH * hg:1024 + CH * hg + CH])
                        tt(k0, k0, g16(EKA)[:, 4 * hg:4 * hg + 4].unsqueeze(2).to_broadcast([P, 4, P]),
                           mult, "kd_done")
                beside(2)
                dve.wait_ge(S("o_ready"), 2 * hg + 1)
                dve.tensor_copy(gdn_u(hg, 0), four(side[2][:])).then_inc(S("o_raw"), 1)
                beside()
                dve.wait_ge(S("ks_ready"), hg + 1)
                dve.wait_ge(S("r_done"), 6 * hg + 2)
                for k in range(4):
                    c0 = 8 + 4 * hg + k
                    R = unit(1, T_)[:, k]
                    stt(R, side[3][:, k * P:k * P + P], g16(NBEG)[:, c0:c0 + 1], R, mult, add, "r_done")
                beside(2)
                dve.wait_ge(S("o_ready"), 2 * hg + 2)
                dve.wait_ge(S("qs_done"), 4 * hg + 4)
                tt(gdn_u(hg, 1), four(side[2][:]), unit(0, QT), add, "o_raw")
            for t in range(TT):
                gdn_norm(1, t)
            for _ in sb_granules:
                pass

            def sb_stage(k):
                past, neg = pc[:, 10 * P:10 * P + CH], pc[:, 10 * P + CH:10 * P + 2 * CH]
                if 1 <= k <= HEADS:
                    dve.wait_ge(S("sb_c"), k)
                    z = sbw(k - 1, 2)
                    tt(z, z, side[2][:], ALU.subtract, "sb_arg")
                if k >= 2:
                    n = k - 2
                    dve.wait_ge(S("sb_o"), n + 1)
                    dve.tensor_copy(u[:, :, n * P:n * P + P],
                                    side[3][:, 0:TOK].rearrange("p (t n) -> p t n", t=TT)).then_inc(S("sb_out"), 1)
                if k < HEADS:
                    x, y, z = (sbw(k, i) for i in range(3))
                    dve.wait_ge(S("sb_act"), 4 * k + 4)
                    if k >= 2:
                        dve.wait_ge(S("sb_w"), k - 1)
                    stt(z, side[k % 2][:], SCALE, neg, ALU.mult, ALU.add, "sb_scored")
                    tt(y, y, x, ALU.add, "sb_scored")
                    dve.wait_ge(S("sb_scored"), 3 * k + 2)
                    tt(y, y, past, ALU.mult, "sb_scored")

            def z_aside(c, j):
                if j % 2 == 0:
                    sb_stage(4 * c + j // 2)

            def z_gate(c):
                for t in range(TT):
                    dve.wait_ge(S("projected"), 2 * (PROJ0["ev_z"] + c) + t + 1)
                    x = u[:, t, 1024 + CH * c:1024 + CH * c + CH]
                    tt(x, x, pj_at("ev_z")[:, t], ALU.mult, "mixed")

            linear("ev_z", z_gate, lambda: None, z_aside)

            def gained(name, c):
                n = POST[name]
                if n < 4 and c == 0:
                    dve.wait_ge(S("grow_in"), 16 * (n + 1))
                    if n:
                        dve.wait_ge(S("h_done"), 8 * n)
                pair = (CHUNK0[name] + c) % 2
                cl = slice(c * CH, c * CH + CH)
                if name[:2] == "dn":
                    l = int(name[2])
                    chunk_done(name, c)
                    dve.wait_ge(S("half_done"), 8 * (l + 1))
                    for t in range(TT):
                        tt(u[:, t, cl], acc[2 * pair + t][:], u[:, t, cl], ALU.add, "u_done")
                for t in range(TT):
                    dve.wait_ge(S("sq_done"), 8 * n + 2 * c + t + 1)
                    src = u[:, t, cl] if name[:2] == "dn" else acc[2 * pair + t][:]
                    tt(u[:, t, cl], src, grow[:, cl], ALU.mult, "ug_done")

            def into_stream(name, user):
                n = POST[name]
                dve.wait_ge(S("sq_done"), 8 * n + 8)
                if n:
                    dve.wait_ge(S("rmsu_done"), n)
                dve.tensor_reduce(ssum, ss.rearrange("p (t c) -> p t c", t=TT), AX_X, ALU.add)\
                    .then_inc(S("ssum_done"), 1)
                dve.wait_ge(S("rmsu_done"), n + 1)
                dve.reciprocal(rstd_u, rms_u).then_inc(S("rstdu_done"), 1)
                dve.wait_ge(S("rstdu_done"), n + 1)
                dve.wait_ge(S("ug_done"), 8 * n + 8)
                if n == 0:
                    dve.wait_ge(S("x_back"), 16)
                for c in range(4):
                    for t in range(TT):
                        cl = slice(c * CH, c * CH + CH)
                        stt(h[:, t, cl], u[:, t, cl], rstd_u[:, t:t + 1], h[:, t, cl], ALU.mult, ALU.add, "h_done")
                    if c:
                        features_lo(user, range(2 * c - 2, 2 * c))
                features_lo(user, range(6, 8))

            linear("ev_out", lambda c: gained("ev_out", c), lambda: (sb_stage(9), z_gate(1), features_lo("ev_out")),
                   lambda c, j: sb_stage(HEADS) if (c, j) == (0, 0) else None)

            def hidden_product(n):
                dve.wait_ge(S("sg_done"), 2 * n + 2)
                for t in range(TT):
                    dve.scalar_tensor_tensor(hm[:, t], acc[2 + t][:], rstd[:, t:t + 1], sg[:, t],
                                             ALU.mult, ALU.mult).then_inc(S("hm_done"), 1)

            def hidden_lo(n, k):
                for b in range(2):
                    dve.wait_ge(S("hTh_done"), 2 * n + b + 1)
                    kk = slice(4 * k + 2 * b, 4 * k + 2 * b + 2) if isinstance(k, int) else bass.ds(4 * k + 2 * b, 2)
                    dve.tensor_tensor(hTl[:, kk], side[b][:].rearrange("p (a b) -> p a b", a=2),
                                      hTh[:, kk].bitcast(F32), ALU.subtract).then_inc(S("hTl_done"), 1)

            def hidden(name, lead):
                n0, blocks, g0 = FFB[name], CHUNKS[name] // 2, GRAN0[name]

                def block_of(i, first):
                    for m in range(2):
                        for j in range(8):
                            split(i * 16 + (g0 + 8 * m + j), j)
                            if m == 0 and j == 2:
                                if first:
                                    lead()
                                else:
                                    dve.wait_ge(S("used"), i * 16 + g0)
                                    hidden_product(i + (n0 - 1))
                            if first and m == 0 and j == STATS + 1 and name[3] == "a":
                                reciprocal_rms(NORM[name])
                            if not first and m == 0 and j == 6:
                                hidden_lo(i + (n0 - 1), i - 1)

                block_of(0, True)
                with dve.Fori(1, blocks) as i:
                    block_of(i, False)

            def down(name, up, evac):
                n, blocks = FFB[up] + CHUNKS[up] // 2 - 1, CHUNKS[up] // 2

                def lead():
                    dve.wait_ge(S("used"), GRAN0[name])
                    hidden_product(n)

                linear(name, evac, lead, lambda c, j: hidden_lo(n, blocks - 1) if c == 0 and j == 6 else None)

            def feed_forward(l, before):
                def lead():
                    gained(before, 3)
                    into_stream(before, f"up{l}a")

                hidden(f"up{l}a", lead)
                down(f"dn{l}a", f"up{l}a", lambda c: None)
                hidden(f"up{l}b", lambda: None)
                down(f"dn{l}b", f"up{l}b", lambda c: gained(f"dn{l}b", c))

            feed_forward(0, "ev_out")

            def lead():
                gained("dn0b", 3)
                into_stream("dn0b", "od_in")

            linear("od_in", lambda c: None, lead,
                   lambda c, j: reciprocal_rms(NORM["od_in"]) if (c, j) == (0, STATS + 1) else None)

            def attention():
                def scored(n):
                    dve.wait_ge(S("at_s"), n + 1)
                    if n == 0:
                        dve.wait_ge(S("masks_in"), 32)
                        dve.wait_ge(S("turned"), 36)
                    if n >= 2:
                        dve.wait_ge(S("at_turned"), n - 1)
                    m = pc[:, 0:384] if n < HEADS else pc[:, 384:768]
                    p = atw(n, 0)
                    stt(p, side[n % 2][:, 0:384], SCALE, m, ALU.mult, ALU.add, "at_scored")
                    dve.wait_ge(S("at_scored"), 3 * n + 1)
                    for t, cl in enumerate((slice(0, P), slice(P, 384))):
                        o = st[:, 24 + 2 * (n % 2) + t:25 + 2 * (n % 2) + t]
                        dve.tensor_reduce(o, p[:, cl], AX_X, ALU.max, negate=True).then_inc(S("at_scored"), 1)

                def recip(n):
                    dve.wait_ge(S("at_exp"), 2 * n + 2)
                    if n >= 2:
                        dve.wait_ge(S("at_out"), 2 * n - 2)
                    k = 2 * (n % 2)
                    dve.reciprocal(st[:, 40 + k:42 + k], st[:, 32 + k:34 + k]).then_inc(S("at_recip"), 1)

                for n in range(2 * HEADS + 1):
                    if n < 2 * HEADS:
                        scored(n)
                    if n >= 1:
                        recip(n - 1)

            linear("od_out", lambda c: gained("od_out", c), lambda: (attention(), features_lo("od_out")))
            feed_forward(1, "od_out")

            def lead():
                gained("dn1b", 3)
                into_stream("dn1b", "s_in")

            mult, add, sub = ALU.mult, ALU.add, ALU.subtract
            count = [0]

            def done(ins, name="par"):
                ins.then_inc(S(name), 1)
                count[0] += 1

            def own():
                dve.wait_ge(S("par"), count[0])

            def angles():
                dve.wait_ge(S("dt_done"), 1)
                done(dve.tensor_scalar(par(LAM), scol(0), -1e-4, None, ALU.min))
                done(dve.tensor_tensor(par(ANG), scol(1), par(DTP), mult))
                own()
                done(dve.tensor_tensor(par(LR), par(LAM), par(DTP), mult))

                def reduce_angle(s, c, x, k):
                    ops = [
                        lambda: dve.tensor_scalar(k, x, 1 / TWO_PI, MAGIC, mult, add),
                        lambda: dve.tensor_scalar(k, k, -MAGIC, None, add),
                        lambda: dve.scalar_tensor_tensor(s, k, -CW1, x, mult, add),
                        lambda: dve.scalar_tensor_tensor(s, k, -CW2, s, mult, add),
                        lambda: dve.tensor_scalar(k, s, math.pi / 2, -TWO_PI, ALU.is_gt, mult),
                        lambda: dve.scalar_tensor_tensor(c, s, math.pi / 2, k, add, add),
                        lambda: dve.tensor_scalar(c, c, PI_IN, -PI_IN, ALU.min, ALU.max),
                        lambda: dve.tensor_scalar(s, s, PI_IN, -PI_IN, ALU.min, ALU.max),
                    ]
                    for op in ops:
                        own()
                        done(op())

                reduce_angle(par(AS), par(AC), par(ANG), par(K_))
                own()
                done(dve.tensor_scalar(par(TA), par(AS), float(P), None, mult))
                reduce_angle(par(AS2), par(AC2), par(TA), par(K_))
                assert count[0] == ANGLES, count[0]
                own()
                done(dve.tensor_scalar(par(TURNS), par(AS), 1 / TWO_PI, None, mult))

            def factors():
                dve.wait_ge(S("mag_done"), 1)
                dve.wait_ge(S("sines"), 4)
                T, B = par(TA), par(TB)
                for op in (
                    lambda: dve.tensor_tensor(par(NRE), par(MAG), par(CS), mult),
                    lambda: dve.tensor_scalar(par(NRE), par(NRE), -1.0, None, add),
                    lambda: dve.tensor_tensor(par(NIM), par(MAG), par(SN), mult),
                    lambda: dve.tensor_tensor(T, par(LAM), par(LAM), mult),
                    lambda: dve.tensor_tensor(B, scol(1), scol(1), mult),
                    lambda: dve.tensor_tensor(T, T, B, add),
                    lambda: dve.reciprocal(par(DEN), T),
                    lambda: dve.tensor_tensor(T, par(NRE), par(LAM), mult),
                    lambda: dve.tensor_tensor(B, par(NIM), scol(1), mult),
                    lambda: dve.tensor_tensor(T, T, B, add),
                    lambda: dve.tensor_tensor(par(QRE), T, par(DEN), mult),
                    lambda: dve.tensor_tensor(T, par(NIM), par(LAM), mult),
                    lambda: dve.tensor_tensor(B, par(NRE), scol(1), mult),
                    lambda: dve.tensor_tensor(T, T, B, sub),
                    lambda: dve.tensor_tensor(par(QIM), T, par(DEN), mult),
                ):
                    own()
                    done(op())

            def widen_c():
                craw = at(PT + 1024, 2, 8, 64)
                dve.wait_ge(S("c_in"), 32)
                dve.wait_ge(S("masks_in"), 48)
                for n in range(2):
                    w = at(SGS, 2, 1024)[:, n].rearrange("p (a g n) -> p a g n", a=8, g=2)
                    for g in range(2):
                        c0 = 4 * TOK + P + g
                        ts(w[:, :, g], craw[:, n], pc[:, c0:c0 + 1], None, mult, ALU.bypass, "c_wide")

            def widen_b(n):
                braw, wide = at(PT, 2, PAIRS, 16), at(SGP, 2, 1024)
                t1, t2 = (spare[:, CH * k:CH * k + CH].rearrange("p (a c) -> p a c", a=PAIRS) for k in range(2))
                q = lambda k: par(k).unsqueeze(2).to_broadcast([P, PAIRS, 16])
                dve.wait_ge(S("b_in"), 32)
                own()
                if n == 0:
                    done(dve.memset(wide, 0.0))
                else:
                    dve.wait_ge(S("b_wide"), 2)
                done(dve.tensor_tensor(t1, braw[:, n], q(QRE), mult))
                done(dve.tensor_tensor(t2, braw[:, 1 - n], q(QIM), mult))
                own()
                w = wide[:, n].rearrange("p (a g c) -> p a g c", a=PAIRS, g=2)
                for g in range(2):
                    r = slice(64 * g, 64 * g + 64)
                    tt(w[r, :, g], t1[r], t2[r], add if n else sub, "b_wide")

            def magnitude(n):
                return par(MAG)[:, n:n + 1].to_broadcast([P, P])

            def rotate(n):
                ct, r = n // 4, n % 4
                t1, t2 = (spare[:, CH * k:CH * k + CH].rearrange("p (a b) -> p a b", a=4) for k in range(2))
                b = side[n % 3][:].rearrange("p (a b) -> p a b", a=4)
                c = tab(ct)[:, 0, r:r + 1].to_broadcast([P, 4, P])
                s2 = tab(ct)[:, 1, r:r + 1].to_broadcast([P, 2, P])
                if r == 0:
                    dve.wait_ge(S("tab_done"), 2 * ct + 2)
                dve.wait_ge(S("bu_ready"), n + 1)
                if n:
                    dve.wait_ge(S("rotated"), 5 * n)
                else:
                    dve.wait_ge(S("b_wide"), 4)
                    dve.wait_ge(S("h_done"), 8 * 4)
                tt(t1, b, c, mult, "rotated")
                tt(t2[:, 0:2], b[:, 2:4], s2, mult, "rotated")
                tt(t2[:, 2:4], b[:, 0:2], s2, mult, "rotated")
                dve.wait_ge(S("rotated"), 5 * n + 3)
                if ct and r == 0:
                    dve.wait_ge(S("unrotated"), 8 * ct)
                o = states[:, r].rearrange("p (a b) -> p a b", a=4)
                tt(o[:, 0:2], t1[:, 0:2], t2[:, 0:2], add, "rotated")
                tt(o[:, 2:4], t1[:, 2:4], t2[:, 2:4], sub, "rotated")

            def scan_tiles(ct):
                dve.wait_ge(S("rotated"), 5 * 4 * (ct + 1))

                def scan(t, start):
                    for r in range(4):
                        for m in range(2):
                            x = states[:, r, 256 * m + P * t:256 * m + P * t + P]
                            dve.tensor_tensor_scan(x, magnitude(4 * ct + r), x, start(r, m), mult, add)\
                                .then_inc(S("scanned"), 1)

                scan(0, lambda r, m: 0.0)
                dve.wait_ge(S("scanned"), 16 * ct + 8)
                er, ei = states[:, :, P - 1], states[:, :, 256 + P - 1]
                c4, s4 = par(C128)[:, 4 * ct:4 * ct + 4], par(S128)[:, 4 * ct:4 * ct + 4]
                w = lambda k: st[:, 56 + 4 * k:60 + 4 * k]
                tt(w(0), er, c4, mult, "turned_on")
                tt(w(1), ei, s4, mult, "turned_on")
                tt(w(2), ei, c4, mult, "turned_on")
                tt(w(3), er, s4, mult, "turned_on")
                dve.wait_ge(S("turned_on"), 6 * ct + 4)
                tt(w(4), w(0), w(1), sub, "turned_on")
                tt(w(5), w(2), w(3), add, "turned_on")
                dve.wait_ge(S("turned_on"), 6 * ct + 6)
                scan(1, lambda r, m: st[:, 72 + 4 * m + r:73 + 4 * m + r])

            def unrotate(n):
                ct, r = n // 4, n % 4
                if r == 0:
                    dve.wait_ge(S("scanned"), 16 * ct + 16)
                if n >= 2:
                    dve.wait_ge(S("y_part"), n - 1)
                x = states[:, r].rearrange("p (a b) -> p a b", a=4)
                for m in range(2):
                    f = tab(ct)[:, m, r:r + 1].to_broadcast([P, 4, P])
                    tt(products(n)[:, m].rearrange("p (a b) -> p a b", a=4), x, f, mult, "unrotated")

            def skip(ct):
                uT = at(UT, 8, TOK)[:, ct]
                dve.wait_ge(S("y_part"), 4 * ct + 4)
                stt(uT, uT, dskip_col(ct), side[3][:, 0:TOK], mult, add, "y_done")

            def s_aside(c, j):
                at_ = 8 * c + j
                if at_ == STATS + 1:
                    reciprocal_rms(NORM["s_in"])
                if at_ == 7:
                    srow = at(SROW, 4, P)
                    dve.wait_ge(S("srow_in"), 48)
                    dve.tensor_copy(srow[0:PAIRS, 2].rearrange("p (a b) -> p a b", a=2),
                                    srow[0:PAIRS, 3, 0:2].unsqueeze(2).to_broadcast([PAIRS, 2, 64]))\
                        .then_inc(S("srow_ready"), 1)
                if at_ == 10:
                    widen_c()
                if at_ == 12:
                    angles()
                if at_ == 16:
                    factors()
                if at_ == 18:
                    widen_b(0)
                if at_ == 20:
                    widen_b(1)
                for ct in range(8):
                    if at_ == SSM_AT[ct] + 2:
                        for r in range(3):
                            rotate(4 * ct + r)
                    if at_ == SSM_AT[ct] + 3:
                        rotate(4 * ct + 3)
                        scan_tiles(ct)
                        if ct:
                            skip(ct - 1)
                    if at_ == SSM_AT[ct] + 4:
                        unrotate(4 * ct)
                        unrotate(4 * ct + 1)
                    if at_ == SSM_AT[ct] + 6:
                        unrotate(4 * ct + 2)
                        unrotate(4 * ct + 3)

            linear("s_in", lambda c: None, lead, s_aside)

            pool_steps = [0]

            def pool_group(g):
                def step(o, a, b, op):
                    dve.tensor_tensor(o, a, b, op).then_inc(S("pool_step"), 1)
                    pool_steps[0] += 1
                    dve.wait_ge(S("pool_step"), pool_steps[0])

                if g == 0:
                    dve.wait_ge(S("turn_done"), 2 * TURN["s_in", 3] + 2 - 12)
                    dve.wait_ge(S("y_part"), 32)
                v = at(PT, 8, TOK)[:, 2 * g:2 * g + 2]
                src = v
                if g:
                    dve.wait_ge(S("pooled"), g)
                for k in range(g + 1):
                    o = at(POOLT + CH * (k % 2), 2, TOK)
                    step(o[:, :, 1 << k:], src[:, :, 1 << k:], src[:, :, 0:TOK - (1 << k)], ALU.add)
                    step(o[:, :, 0:1 << k], src[:, :, 0:1 << k], src[:, :, 0:1 << k], ALU.max)
                    src = o
                inv = pc[:, g * TOK:(g + 1) * TOK].unsqueeze(1).to_broadcast([P, 2, TOK])
                step(src, src, inv, ALU.mult)
                tt(at(POOLED, 8, TOK)[:, 2 * g:2 * g + 2], src, v, ALU.subtract, "pooled")

            def pool_gate(g):
                dve.wait_ge(S("pool_mixed"), g + 1)
                dve.wait_ge(S("projected"), 2 * (PROJ0["s_in"] + 6))
                cl = slice(g * 256, g * 256 + 256)
                tt(u[:, :, cl], side[g][:].rearrange("p (t n) -> p t n", t=TT),
                   at(SGP, TT, 1024)[:, :, cl], ALU.mult, "pool_out")

            def low(ct):
                dve.wait_ge(S("gh_done"), ct + 1)
                tt(xl[:, ct], at(UT, 8, TOK)[:, ct], xh[:, ct].bitcast(F32), ALU.subtract, "gl_done")

            def glu_out(c):
                if c % 2:
                    m = c // 2
                    for t in range(TT):
                        dve.wait_ge(S("glu_sig"), 2 * m + t + 1)
                        x = at(UT, TT, CH)[:, t]
                        if m:
                            dve.wait_ge(S("mixed"), 4 + 2 * m)
                        else:
                            dve.wait_ge(S("gl_done"), 8)
                        tt(x, acc[t][:], spare[:, CH * t:CH * t + CH], ALU.mult, "glu_out")
                        dve.wait_ge(S("glu_out"), 2 * m + t + 1)
                        tt(u[:, t, 1024 + CH * m:1024 + CH * m + CH], x,
                           at(SGS, TT, 1024)[:, t, CH * m:CH * m + CH], ALU.mult, "mixed")

            def lead():
                for ct in range(8):
                    if ct == 2:
                        skip(7)
                    low(ct)

            def glu_aside(c, j):
                for k, where in enumerate(POOL_AT):
                    if 4 * c + j == where - 3:
                        pool_group(k)
                    if 4 * c + j == where + 2 and k < 3:
                        pool_gate(k)

            linear("glu", glu_out, lead, glu_aside)

            def s_out(c):
                chunk_done("s_out", c)
                pair = (CHUNK0["s_out"] + c) % 2
                for t in range(TT):
                    x = h[:, t, CH * c:CH * c + CH]
                    tt(x, acc[2 * pair + t][:], x, ALU.add, "h_done")

            def s_out_aside(c, j):
                if (c, j) == (2, 4):
                    dve.wait_ge(S("ph_done"), 4)
                    for t in range(TT):
                        tt(hTl[:, 0:2, t * P:t * P + P],
                           side[t][:, 0:256].rearrange("p (k n) -> p k n", k=2),
                           hTh[:, 0:2, t * P:t * P + P].bitcast(F32), ALU.subtract, "pl_done")

            linear("s_out", s_out, lambda: (pool_gate(3), glu_out(3), features_lo("s_out")), s_out_aside)

            for c in range(4):
                split(gran("ple", c))
                if c == 2:
                    s_out(3)
                    features_lo("pg")

            def gate_out(c):
                for t in range(TT):
                    n = 2 * c + t
                    dve.wait_ge(S("pg_sig"), n + 1)
                    cl = slice(CH * c, CH * c + CH)
                    x = at(13312, TT, CH)[:, t]
                    dve.wait_ge(S("ple_out"), 8)
                    tt(x, sg[:, t], u[:, t, cl], ALU.mult, "gated")
                    dve.wait_ge(S("gated"), 3 * n + 1)
                    tt(h[:, t, cl], h[:, t, cl], x, ALU.add, "gated")
                    dve.wait_ge(S("gated"), 3 * n + 2)
                    dve.wait_ge(S("grow_in"), 80)
                    tt(u[:, t, cl], h[:, t, cl], grow[:, cl], ALU.mult, "gated")

            linear("pg", gate_out, lambda: None)
            gate_out(3)
            dve.wait_ge(S("final_sq"), 8)
            dve.wait_ge(S("rmsu_done"), 4)
            dve.tensor_reduce(ssum, ss.rearrange("p (t c) -> p t c", t=TT), AX_X, ALU.add).then_inc(S("ssum_done"), 1)
            dve.wait_ge(S("rmsu_done"), 5)
            dve.reciprocal(rstd_u, rms_u).then_inc(S("rstdu_done"), 1)
            dve.wait_ge(S("rstdu_done"), 5)
            dve.wait_ge(S("gated"), 24)
            for c in range(4):
                cl = slice(CH * c, CH * c + CH)
                ts(u[:, 0, cl], u[:, 0, cl], rstd_u[:, 0:1], None, ALU.mult, ALU.bypass, "final0")


_INS = ["x", "mix_norm_pre", "mix_norm_post", "ffn_norm_pre", "ffn_norm_post", "ev_w_in", "ev_conv_w", "ev_a_log",
        "ev_dt_bias", "ev_onorm", "ev_w_out", "od_w_in", "od_w_out", "ffn_w_gate", "ffn_w_up", "ffn_w_down", "p_2",
        "norm_gain_2", "w_in_2", "w_pool_2", "pool_scale_2", "a_re_2", "a_im_2", "log_dt_2", "b_re_2", "b_im_2",
        "c_re_2", "c_im_2", "d_skip_2", "w_glu_2", "w_out_2", "w_ple_2", "w_ple_gate_2", "final_gain_2"]


def kernel(**inputs):
    import concourse.bacc as _bacc
    from concourse.bass_utils import run_bass_kernel_spmd as _run

    nc = _bacc.Bacc("TRN2", target_bir_lowering=False, num_devices=1)
    arrays = {n: np.ascontiguousarray(inputs[n]) for n in _INS}
    arrays.update(shape_constants())
    A = {n: nc.dram_tensor(f"in_{n}", a.shape, F32, kind="ExternalInput").ap() for n, a in arrays.items()}
    out = nc.dram_tensor("out", (1, TOK, DM), F32, kind="ExternalOutput").ap()
    build(nc, A, out)
    r = _run(nc, [{f"in_{n}": a for n, a in arrays.items()}], core_ids=[0])
    return r.results[0]["out"]
```
